# Optimizing a Trainium2 kernel written in Bass

```python
import jax, jax.numpy as jnp
from jax import lax
import numpy as np

D_MODEL = 1024
BATCH = 1
SEQ = 1024
DEPTH = 1

MLA_HEADS = 8
MLA_NOPE = 64
MLA_ROPE = 32
MLA_V = 64
MLA_QK = MLA_NOPE + MLA_ROPE
MLA_Q_RANK = 256
MLA_KV_RANK = 128
RET_HEADS = 4
RET_DK = 64
RET_DV = 128
CHUNK = 128
Q_BLOCK = 128
D_FF = 4 * D_MODEL
ROPE_BASE = 10000.0
EPS = 1e-5
MLA_WIDTH = MLA_HEADS * MLA_V
RET_WIDTH = RET_HEADS * RET_DV
MIX_WIDTH = MLA_WIDTH + RET_WIDTH
ALPHA = (2.0 * DEPTH) ** 0.25
BETA = (8.0 * DEPTH) ** -0.25
IN_SPLITS = (MLA_Q_RANK, MLA_KV_RANK, MLA_ROPE,
             RET_HEADS * RET_DK, RET_HEADS * RET_DK, RET_WIDTH, RET_WIDTH)
IN_WIDTH = sum(IN_SPLITS)
IN_OFFSETS = tuple(int(v) for v in np.cumsum(IN_SPLITS)[:-1])


def layer_norm(x, g, b):
    xf = x.astype(jnp.float32)
    mu = jnp.mean(xf, -1, keepdims=True)
    var = jnp.mean(jnp.square(xf - mu), -1, keepdims=True)
    return ((xf - mu) * lax.rsqrt(var + EPS) * g.astype(jnp.float32) + b.astype(jnp.float32)).astype(x.dtype)

def rms_norm(x, g):
    xf = x.astype(jnp.float32)
    ms = jnp.mean(jnp.square(xf), -1, keepdims=True)
    return (xf * lax.rsqrt(ms + EPS) * g.astype(jnp.float32)).astype(x.dtype)

def rotary(x, pos):
    half = x.shape[-1] // 2
    inv = ROPE_BASE ** (-jnp.arange(half, dtype=jnp.float32) / half)
    ang = pos.astype(jnp.float32)[..., None] * inv
    cos = jnp.cos(ang)[:, :, None, :]
    sin = jnp.sin(ang)[:, :, None, :]
    x1 = x[..., :half].astype(jnp.float32)
    x2 = x[..., half:].astype(jnp.float32)
    return jnp.concatenate([x1 * cos - x2 * sin, x2 * cos + x1 * sin], -1).astype(x.dtype)

def causal_block_attention(q, k, v):
    b, s, h, dq = q.shape
    dv = v.shape[-1]
    nb = s // Q_BLOCK
    scale = dq ** -0.5
    qb = q.reshape(b, nb, Q_BLOCK, h, dq).transpose(1, 0, 3, 2, 4)
    kt = k.transpose(0, 2, 1, 3)
    vt = v.transpose(0, 2, 1, 3)
    k_idx = jnp.arange(s)

    def one_block(args):
        q_blk, i = args
        sc = jnp.einsum('bhqd,bhkd->bhqk', q_blk, kt,
                        preferred_element_type=jnp.float32) * scale
        q_idx = i * Q_BLOCK + jnp.arange(Q_BLOCK)
        mask = k_idx[None, :] <= q_idx[:, None]
        p = jax.nn.softmax(jnp.where(mask, sc, -jnp.inf), axis=-1)
        return jnp.einsum('bhqk,bhkd->bhqd', p.astype(vt.dtype), vt)

    out = lax.map(one_block, (qb, jnp.arange(nb)))
    return out.transpose(1, 0, 3, 2, 4).reshape(b, s, h * dv)

def mla_mixer(q_c, kv_c, k_r, pos, g_q, w_uq, g_kv, w_ukv):
    b, s, _ = q_c.shape
    q = (rms_norm(q_c, g_q) @ w_uq).reshape(b, s, MLA_HEADS, MLA_QK)
    q = jnp.concatenate([q[..., :MLA_NOPE], rotary(q[..., MLA_NOPE:], pos)], -1)
    kv = (rms_norm(kv_c, g_kv) @ w_ukv).reshape(b, s, MLA_HEADS, MLA_NOPE + MLA_V)
    k_nope, v = kv[..., :MLA_NOPE], kv[..., MLA_NOPE:]
    k_rope = rotary(k_r[:, :, None, :], pos)
    k = jnp.concatenate([k_nope, jnp.broadcast_to(k_rope, (b, s, MLA_HEADS, MLA_ROPE))], -1)
    return causal_block_attention(q, k, v)

def retention_mixer(q, k, v, g, pos, gn_g, gn_b):
    b, s, _ = q.shape
    n = s // CHUNK
    q = rotary(q.reshape(b, s, RET_HEADS, RET_DK), pos)
    k = rotary(k.reshape(b, s, RET_HEADS, RET_DK), pos) * (RET_DK ** -0.5)
    v = v.reshape(b, s, RET_HEADS, RET_DV)
    qc = q.reshape(b, n, CHUNK, RET_HEADS, RET_DK).transpose(0, 3, 1, 2, 4)
    kc = k.reshape(b, n, CHUNK, RET_HEADS, RET_DK).transpose(0, 3, 1, 2, 4)
    vc = v.reshape(b, n, CHUNK, RET_HEADS, RET_DV).transpose(0, 3, 1, 2, 4)

    log_g = jnp.log(1.0 - 2.0 ** (-5.0 - jnp.arange(RET_HEADS, dtype=jnp.float32)))
    idx = jnp.arange(CHUNK, dtype=jnp.float32)
    diff = idx[:, None] - idx[None, :]
    decay = jnp.where(diff >= 0, jnp.exp(log_g[:, None, None] * jnp.maximum(diff, 0.0)), 0.0)
    zeta = jnp.exp(log_g[:, None] * (CHUNK - 1 - idx))
    xi = jnp.exp(log_g[:, None] * (idx + 1.0))

    scores = jnp.einsum('bhnid,bhnjd->bhnij', qc, kc) * decay[None, :, None]
    inner = jnp.einsum('bhnij,bhnjv->bhniv', scores, vc)
    chunk_kv = jnp.einsum('bhnjd,hj,bhnjv->bhndv', kc, zeta, vc)
    g_chunk = jnp.exp(log_g * CHUNK).astype(chunk_kv.dtype)[None, :, None, None]

    def step(state, kv_n):
        return state * g_chunk + kv_n, state

    init = jnp.zeros((b, RET_HEADS, RET_DK, RET_DV), chunk_kv.dtype)
    _, prev = lax.scan(step, init, chunk_kv.transpose(2, 0, 1, 3, 4))
    prev = prev.transpose(1, 2, 0, 3, 4)
    cross = jnp.einsum('bhnid,bhndv->bhniv', qc, prev) * xi[None, :, None, :, None]

    o = (inner + cross).transpose(0, 2, 3, 1, 4).reshape(b, s, RET_HEADS, RET_DV)
    of = o.astype(jnp.float32)
    mu = jnp.mean(of, -1, keepdims=True)
    var = jnp.mean(jnp.square(of - mu), -1, keepdims=True)
    on = ((of - mu) * lax.rsqrt(var + EPS)).reshape(b, s, RET_WIDTH)
    on = on * gn_g.astype(jnp.float32) + gn_b.astype(jnp.float32)
    return (on * jax.nn.silu(g.astype(jnp.float32))).astype(g.dtype)

def first_inputs(seed: int = 0) -> dict:
    key = jax.random.key(seed)
    ks = jax.random.split(key, 24)
    f32 = jnp.float32
    nrm = lambda k, shape, fan: jax.random.normal(k, shape, f32) * (fan ** -0.5)
    gain = lambda k, shape: 1.0 + 0.05 * jax.random.normal(k, shape, f32)
    bias = lambda k, shape: 0.02 * jax.random.normal(k, shape, f32)

    x = jax.random.normal(ks[0], (BATCH, SEQ, D_MODEL), f32)
    c = jax.random.normal(ks[1], (BATCH, D_MODEL), f32)
    offset = jax.random.randint(ks[2], (BATCH, 1), 0, 1024, dtype=jnp.int32)
    positions = (offset + jnp.arange(SEQ, dtype=jnp.int32)[None, :]).astype(jnp.int32)

    in_col_scale = jnp.concatenate([
        jnp.ones((IN_WIDTH - 2 * RET_WIDTH,), f32),
        jnp.full((RET_WIDTH,), BETA, f32),
        jnp.ones((RET_WIDTH,), f32)])
    ukv_col_scale = jnp.tile(jnp.concatenate([jnp.ones((MLA_NOPE,), f32),
                                              jnp.full((MLA_V,), BETA, f32)]), MLA_HEADS)
    return {
        "x": x,
        "c": c,
        "positions": positions,
        "ln_in_g": gain(ks[3], (D_MODEL,)),
        "ln_in_b": bias(ks[4], (D_MODEL,)),
        "w_ada": nrm(ks[5], (DEPTH, D_MODEL, 6 * D_MODEL), D_MODEL) * 0.5,
        "b_ada": bias(ks[6], (DEPTH, 6 * D_MODEL)),
        "w_in": nrm(ks[7], (DEPTH, D_MODEL, IN_WIDTH), D_MODEL) * in_col_scale,
        "mla_q_norm": gain(ks[8], (DEPTH, MLA_Q_RANK)),
        "w_uq": nrm(ks[9], (DEPTH, MLA_Q_RANK, MLA_HEADS * MLA_QK), MLA_Q_RANK),
        "mla_kv_norm": gain(ks[10], (DEPTH, MLA_KV_RANK)),
        "w_ukv": nrm(ks[11], (DEPTH, MLA_KV_RANK, MLA_HEADS * (MLA_NOPE + MLA_V)), MLA_KV_RANK) * ukv_col_scale,
        "ret_gn_g": gain(ks[12], (DEPTH, RET_WIDTH)),
        "ret_gn_b": bias(ks[13], (DEPTH, RET_WIDTH)),
        "w_out": nrm(ks[14], (DEPTH, MIX_WIDTH, D_MODEL), MIX_WIDTH) * BETA,
        "ln1_g": gain(ks[15], (DEPTH, D_MODEL)),
        "ln1_b": bias(ks[16], (DEPTH, D_MODEL)),
        "w_ff1": nrm(ks[17], (DEPTH, D_MODEL, D_FF), D_MODEL) * BETA,
        "w_ff2": nrm(ks[18], (DEPTH, D_FF, D_MODEL), D_FF) * BETA,
        "ln2_g": gain(ks[19], (DEPTH, D_MODEL)),
        "ln2_b": bias(ks[20], (DEPTH, D_MODEL)),
    }

def first_block(x, c, positions, ln_in_g, ln_in_b, w_ada, b_ada, w_in, mla_q_norm, w_uq,
              mla_kv_norm, w_ukv, ret_gn_g, ret_gn_b, w_out, ln1_g, ln1_b,
              w_ff1, w_ff2, ln2_g, ln2_b):
    x = layer_norm(x, ln_in_g, ln_in_b)
    c_act = jax.nn.silu(c)
    for l in range(DEPTH):
        mod = c_act @ w_ada[l] + b_ada[l]
        sh1, sc1, gt1, sh2, sc2, gt2 = [m[:, None, :] for m in jnp.split(mod, 6, axis=-1)]

        h = x * (1.0 + sc1) + sh1
        proj = h @ w_in[l]
        q_c, kv_c, k_r, r_q, r_k, r_v, r_g = jnp.split(proj, IN_OFFSETS, axis=-1)
        a = mla_mixer(q_c, kv_c, k_r, positions, mla_q_norm[l], w_uq[l], mla_kv_norm[l], w_ukv[l])
        r = retention_mixer(r_q, r_k, r_v, r_g, positions, ret_gn_g[l], ret_gn_b[l])
        y = jnp.concatenate([a, r], axis=-1) @ w_out[l]
        x = layer_norm(ALPHA * x + gt1 * y, ln1_g[l], ln1_b[l])

        h = x * (1.0 + sc2) + sh2
        f = jnp.square(jax.nn.relu(h @ w_ff1[l])) @ w_ff2[l]
        x = layer_norm(ALPHA * x + gt2 * f, ln2_g[l], ln2_b[l])
    return x


DEPTH_2 = 2

GRID_W = 64
CTX_LEN = 256
EPS_2 = 1e-6
A_WIDTH = D_MODEL // 2
A_CONV_W = 31
B_GROUPS = 4
B_WIDTH = D_MODEL // 2
B_GROUP_DIM = B_WIDTH // B_GROUPS
C_WIDTH = D_MODEL // 2
C_CONV_W = 3
HEAD_DIM = 64
N_Q_HEADS = (D_MODEL // 2) // HEAD_DIM
N_KV_HEADS = max(N_Q_HEADS // 4, 1)
Q_GROUP = N_Q_HEADS // N_KV_HEADS
ATT_WIDTH = N_Q_HEADS * HEAD_DIM
KV_WIDTH = N_KV_HEADS * HEAD_DIM
WINDOW = 128
BLOCK = 128
NEG_INF = -1e30
EVEN_IN = 3 * A_WIDTH + 2 * B_WIDTH
EVEN_MIX = A_WIDTH + B_WIDTH
ODD_IN = 4 * C_WIDTH + 2 * ATT_WIDTH + 2 * KV_WIDTH
ODD_MIX = C_WIDTH + ATT_WIDTH


def _rmsnorm(x, g):
    xf = x.astype(jnp.float32)
    y = xf * lax.rsqrt(jnp.mean(xf * xf, axis=-1, keepdims=True) + EPS_2)
    return (y * g.astype(jnp.float32)).astype(x.dtype)

def _layernorm(x, g, b):
    xf = x.astype(jnp.float32)
    mu = jnp.mean(xf, axis=-1, keepdims=True)
    var = jnp.mean(jnp.square(xf - mu), axis=-1, keepdims=True)
    y = (xf - mu) * lax.rsqrt(var + EPS_2)
    return (y * g.astype(jnp.float32) + b.astype(jnp.float32)).astype(x.dtype)

def _split(t, widths):
    cuts, acc = [], 0
    for w in widths[:-1]:
        acc += w
        cuts.append(acc)
    return jnp.split(t, cuts, axis=-1)

def _modulation(cvec, w_mod, b_mod):
    h = jax.nn.silu(cvec) @ w_mod + b_mod
    shift, scale, gate = jnp.split(h[:, None, :], 3, axis=-1)
    return shift, scale, gate

def _pre(x, g, shift, scale):
    return _rmsnorm(x, g) * (1 + scale) + shift

def _dwconv(u, w):
    pad = (w.shape[0] - 1) // 2
    return lax.conv_general_dilated(
        u, w[:, None, :].astype(u.dtype), window_strides=(1,), padding=[(pad, pad)],
        dimension_numbers=('NWC', 'WIO', 'NWC'), feature_group_count=u.shape[-1])

def _fourier_mix(v, fw):
    b, l, _ = v.shape
    vg = v.reshape(b, l, B_GROUPS, B_GROUP_DIM).astype(jnp.float32)
    f = jnp.fft.fftn(vg, axes=(1, 3), norm='ortho').real.astype(v.dtype)
    return jnp.einsum('blgd,gde->blge', f, fw).reshape(b, l, B_WIDTH)

def _even_mix(h, w_in, a_conv_w, a_conv_b, a_ln_g, a_ln_b, a_pw_w, a_pw_b, b_fw, w_out):
    a_val, a_glu, a_gate, b_val, b_gate = _split(h @ w_in, [A_WIDTH, A_WIDTH, A_WIDTH, B_WIDTH, B_WIDTH])
    u = a_val * jax.nn.sigmoid(a_glu)
    u = jax.nn.silu(_layernorm(_dwconv(u, a_conv_w) + a_conv_b, a_ln_g, a_ln_b))
    y_a = (u @ a_pw_w + a_pw_b) * jax.nn.silu(a_gate)
    y_b = _fourier_mix(b_val, b_fw) * jax.nn.silu(b_gate)
    return jnp.concatenate([y_a, y_b], axis=-1) @ w_out

def _rope_tables(row, col):
    nf = HEAD_DIM // 4
    inv = jnp.power(ROPE_BASE, -jnp.arange(nf, dtype=jnp.float32) / nf)
    ang = jnp.stack([row.astype(jnp.float32)[:, None] * inv,
                     col.astype(jnp.float32)[:, None] * inv], axis=1)
    return jnp.cos(ang), jnp.sin(ang)

def _apply_rope(t, cos, sin):
    b, l, h, d = t.shape
    tr = t.astype(jnp.float32).reshape(b, l, h, 2, 2, d // 4)
    t1, t2 = tr[..., 0, :], tr[..., 1, :]
    cs, sn = cos[None, :, None], sin[None, :, None]
    out = jnp.stack([t1 * cs - t2 * sn, t2 * cs + t1 * sn], axis=-2)
    return out.reshape(b, l, h, d).astype(t.dtype)

def _sink_softmax(logits, sink):
    m = sink
    for s in logits:
        m = jnp.maximum(m, jnp.max(s, axis=-1, keepdims=True))
    ps = [jnp.exp(s - m) for s in logits]
    denom = jnp.exp(sink - m)
    for p in ps:
        denom = denom + jnp.sum(p, axis=-1, keepdims=True)
    return [p / denom for p in ps]

def _window_attention(q, k, v, kc, vc, sink):
    b, l, hq, hd = q.shape
    nb = l // BLOCK
    scale = HEAD_DIM ** -0.5
    qb = q.reshape(b, nb, BLOCK, N_KV_HEADS, Q_GROUP, hd)

    def band(t):
        tp = jnp.pad(t, ((0, 0), (BLOCK, BLOCK), (0, 0), (0, 0))).reshape(b, nb + 2, BLOCK, N_KV_HEADS, hd)
        return jnp.concatenate([tp[:, :-2], tp[:, 1:-1], tp[:, 2:]], axis=2)

    kw, vw = band(k), band(v)
    qpos = jnp.arange(l).reshape(nb, BLOCK)
    kpos = jnp.arange(-BLOCK, l + BLOCK).reshape(nb + 2, BLOCK)
    kwpos = jnp.concatenate([kpos[:-2], kpos[1:-1], kpos[2:]], axis=1)
    valid = ((jnp.abs(qpos[:, :, None] - kwpos[:, None, :]) <= WINDOW)
             & (kwpos >= 0)[:, None, :] & (kwpos < l)[:, None, :])
    s_win = jnp.einsum('bnqhgd,bnkhd->bnhgqk', qb, kw).astype(jnp.float32) * scale
    s_win = jnp.where(valid[None, :, None, None], s_win, NEG_INF)
    s_ctx = jnp.einsum('bnqhgd,bchd->bnhgqc', qb, kc).astype(jnp.float32) * scale
    sink_b = sink.astype(jnp.float32).reshape(N_KV_HEADS, Q_GROUP)[None, None, :, :, None, None]
    p_win, p_ctx = _sink_softmax([s_win, s_ctx], sink_b)
    o = (jnp.einsum('bnhgqk,bnkhd->bnqhgd', p_win.astype(v.dtype), vw)
         + jnp.einsum('bnhgqc,bchd->bnqhgd', p_ctx.astype(v.dtype), vc))
    return o.reshape(b, l, hq * hd)

def _context_attention(q, k, v, sink):
    b, lc, hq, hd = q.shape
    qg = q.reshape(b, lc, N_KV_HEADS, Q_GROUP, hd)
    s = jnp.einsum('bqhgd,bkhd->bhgqk', qg, k).astype(jnp.float32) * (HEAD_DIM ** -0.5)
    sink_b = sink.astype(jnp.float32).reshape(N_KV_HEADS, Q_GROUP)[None, :, :, None, None]
    (p,) = _sink_softmax([s], sink_b)
    o = jnp.einsum('bhgqk,bkhd->bqhgd', p.astype(v.dtype), v)
    return o.reshape(b, lc, hq * hd)

def _odd_proj(h, w_in):
    cb, cc, cx, cg, q, k, v, ag = _split(
        h @ w_in, [C_WIDTH, C_WIDTH, C_WIDTH, C_WIDTH, ATT_WIDTH, KV_WIDTH, KV_WIDTH, ATT_WIDTH])
    b, l, _ = h.shape
    return (cb, cc, cx, cg,
            q.reshape(b, l, N_Q_HEADS, HEAD_DIM),
            k.reshape(b, l, N_KV_HEADS, HEAD_DIM),
            v.reshape(b, l, N_KV_HEADS, HEAD_DIM), ag)

def _odd_out(cb, cc, cx, cg, att, ag, c_conv_w, w_out):
    y_c = cb * _dwconv(cc * cx, c_conv_w) * jax.nn.silu(cg)
    y_d = att * jax.nn.silu(ag)
    return jnp.concatenate([y_c, y_d], axis=-1) @ w_out

def second_inputs(seed: int = 0) -> dict:
    key = jax.random.key(seed)
    ks = jax.random.split(key, 24)
    ne, no = (DEPTH_2 + 1) // 2, DEPTH_2 // 2

    def nrm(k, shape):
        return jax.random.normal(k, shape, jnp.float32)

    return {
        'x': nrm(ks[0], (BATCH, SEQ, D_MODEL)),
        'c': nrm(ks[1], (BATCH, D_MODEL)),
        'ctx': nrm(ks[2], (BATCH, CTX_LEN, D_MODEL)),
        'c_ctx': nrm(ks[3], (D_MODEL,)),
        'e_norm': 1.0 + 0.02 * nrm(ks[4], (ne, D_MODEL)),
        'e_w_mod': nrm(ks[5], (ne, D_MODEL, 3 * D_MODEL)) * (0.5 * D_MODEL ** -0.5),
        'e_b_mod': 0.02 * nrm(ks[6], (ne, 3 * D_MODEL)),
        'e_w_in': nrm(ks[7], (ne, D_MODEL, EVEN_IN)) * D_MODEL ** -0.5,
        'e_a_conv_w': nrm(ks[8], (ne, A_CONV_W, A_WIDTH)) * A_CONV_W ** -0.5,
        'e_a_conv_b': 0.02 * nrm(ks[9], (ne, A_WIDTH)),
        'e_a_ln_g': 1.0 + 0.02 * nrm(ks[10], (ne, A_WIDTH)),
        'e_a_ln_b': 0.02 * nrm(ks[11], (ne, A_WIDTH)),
        'e_a_pw_w': nrm(ks[12], (ne, A_WIDTH, A_WIDTH)) * A_WIDTH ** -0.5,
        'e_a_pw_b': 0.02 * nrm(ks[13], (ne, A_WIDTH)),
        'e_b_fw': nrm(ks[14], (ne, B_GROUPS, B_GROUP_DIM, B_GROUP_DIM)) * B_GROUP_DIM ** -0.5,
        'e_w_out': nrm(ks[15], (ne, EVEN_MIX, D_MODEL)) * EVEN_MIX ** -0.5,
        'o_norm': 1.0 + 0.02 * nrm(ks[16], (no, D_MODEL)),
        'o_w_mod': nrm(ks[17], (no, D_MODEL, 3 * D_MODEL)) * (0.5 * D_MODEL ** -0.5),
        'o_b_mod': 0.02 * nrm(ks[18], (no, 3 * D_MODEL)),
        'o_w_in': nrm(ks[19], (no, D_MODEL, ODD_IN)) * D_MODEL ** -0.5,
        'o_c_conv_w': nrm(ks[20], (no, C_CONV_W, C_WIDTH)) * C_CONV_W ** -0.5,
        'o_sink': 0.5 * nrm(ks[21], (no, N_Q_HEADS)),
        'o_w_out': nrm(ks[22], (no, ODD_MIX, D_MODEL)) * ODD_MIX ** -0.5,
        'final_norm': 1.0 + 0.02 * nrm(ks[23], (D_MODEL,)),
    }

def second_block(x, c, ctx, c_ctx, e_norm, e_w_mod, e_b_mod, e_w_in, e_a_conv_w, e_a_conv_b,
              e_a_ln_g, e_a_ln_b, e_a_pw_w, e_a_pw_b, e_b_fw, e_w_out,
              o_norm, o_w_mod, o_b_mod, o_w_in, o_c_conv_w, o_sink, o_w_out, final_norm):
    l = x.shape[1]
    rows = l // GRID_W
    row = jnp.broadcast_to(jnp.arange(rows)[:, None], (rows, GRID_W)).reshape(l)
    col = jnp.broadcast_to(jnp.arange(GRID_W)[None, :], (rows, GRID_W)).reshape(l)
    cos, sin = _rope_tables(row, col)
    c_ctx2 = c_ctx[None, :]
    xc = ctx
    for layer in range(DEPTH_2):
        i = layer // 2
        ctx_needed = layer < DEPTH_2 - 1
        if layer % 2 == 0:
            args = (e_w_in[i], e_a_conv_w[i], e_a_conv_b[i], e_a_ln_g[i], e_a_ln_b[i],
                    e_a_pw_w[i], e_a_pw_b[i], e_b_fw[i], e_w_out[i])
            sh, sc, gt = _modulation(c, e_w_mod[i], e_b_mod[i])
            x_new = x + gt * _even_mix(_pre(x, e_norm[i], sh, sc), *args)
            if ctx_needed:
                sh_c, sc_c, gt_c = _modulation(c_ctx2, e_w_mod[i], e_b_mod[i])
                xc = xc + gt_c * _even_mix(_pre(xc, e_norm[i], sh_c, sc_c), *args)
            x = x_new
        else:
            sh, sc, gt = _modulation(c, o_w_mod[i], o_b_mod[i])
            sh_c, sc_c, gt_c = _modulation(c_ctx2, o_w_mod[i], o_b_mod[i])
            cb_c, cc_c, cx_c, cg_c, q_c, k_c, v_c, ag_c = _odd_proj(_pre(xc, o_norm[i], sh_c, sc_c), o_w_in[i])
            cb, cc, cx, cg, q, k, v, ag = _odd_proj(_pre(x, o_norm[i], sh, sc), o_w_in[i])
            att = _window_attention(_apply_rope(q, cos, sin), _apply_rope(k, cos, sin), v, k_c, v_c, o_sink[i])
            x_new = x + gt * _odd_out(cb, cc, cx, cg, att, ag, o_c_conv_w[i], o_w_out[i])
            if ctx_needed:
                att_c = _context_attention(q_c, k_c, v_c, o_sink[i])
                xc = xc + gt_c * _odd_out(cb_c, cc_c, cx_c, cg_c, att_c, ag_c, o_c_conv_w[i], o_w_out[i])
            x = x_new
    return _rmsnorm(x, final_norm)


def setup_inputs(seed=0):
    out = dict(first_inputs(seed))
    for name, value in second_inputs(seed + 1).items():
        if name != "x":
            out[name + "_2"] = value
    return out


def reference(
    x, c, positions, ln_in_g, ln_in_b, w_ada, b_ada, w_in, mla_q_norm, w_uq, mla_kv_norm, w_ukv,
    ret_gn_g, ret_gn_b, w_out, ln1_g, ln1_b, w_ff1, w_ff2, ln2_g, ln2_b, c_2, ctx_2, c_ctx_2,
    e_norm_2, e_w_mod_2, e_b_mod_2, e_w_in_2, e_a_conv_w_2, e_a_conv_b_2, e_a_ln_g_2,
    e_a_ln_b_2, e_a_pw_w_2, e_a_pw_b_2, e_b_fw_2, e_w_out_2, o_norm_2, o_w_mod_2, o_b_mod_2,
    o_w_in_2, o_c_conv_w_2, o_sink_2, o_w_out_2, final_norm_2,
):
    x = first_block(
        x, c, positions, ln_in_g, ln_in_b, w_ada, b_ada, w_in, mla_q_norm, w_uq, mla_kv_norm,
        w_ukv, ret_gn_g, ret_gn_b, w_out, ln1_g, ln1_b, w_ff1, w_ff2, ln2_g, ln2_b,
    )
    return second_block(
        x, c_2, ctx_2, c_ctx_2, e_norm_2, e_w_mod_2, e_b_mod_2, e_w_in_2, e_a_conv_w_2,
        e_a_conv_b_2, e_a_ln_g_2, e_a_ln_b_2, e_a_pw_w_2, e_a_pw_b_2, e_b_fw_2, e_w_out_2,
        o_norm_2, o_w_mod_2, o_b_mod_2, o_w_in_2, o_c_conv_w_2, o_sink_2, o_w_out_2,
        final_norm_2,
    )


_drawn_inputs = setup_inputs


def setup_inputs(seed=0):
    import zlib

    import numpy as np

    out = dict(_drawn_inputs(seed))
    spreads = {}
    factors = {'ln_in_b': 2.671,
     'b_ada': 5.873,
     'mla_q_norm': 8.0,
     'w_uq': 7.744,
     'mla_kv_norm': 8.0,
     'ret_gn_g': 8.0,
     'ret_gn_b': 8.0,
     'ln1_b': 2.723,
     'ln2_b': 2.805,
     'ctx_2': 44.679,
     'c_ctx_2': 3.06,
     'e_norm_2': 8.0,
     'e_b_mod_2': 5.225,
     'e_a_conv_b_2': 8.0,
     'e_a_ln_g_2': 8.0,
     'e_a_ln_b_2': 8.0,
     'e_a_pw_b_2': 8.0,
     'o_norm_2': 7.707,
     'o_b_mod_2': 3.638,
     'o_sink_2': 8.0,
     'final_norm_2': 24.638}
    for name, (base, spread) in spreads.items():
        noise = np.random.default_rng([zlib.crc32(name.encode()), seed]).standard_normal(out[name].shape)
        drawn = base * np.exp(spread * noise) if base else spread * noise
        out[name] = __import__('jax').numpy.asarray(drawn.astype(out[name].dtype))
    for name, factor in factors.items():
        out[name] = (out[name] * factor).astype(out[name].dtype)
    return out
```

```python
from contextlib import ExitStack

import concourse.bass as bass
import numpy as np
from concourse import mybir

F32 = mybir.dt.float32
F32R = mybir.dt.float32r
BF16 = mybir.dt.bfloat16
I32 = mybir.dt.int32
ALU = mybir.AluOpType
ACT = mybir.ActivationFunctionType
AX = mybir.AxisListType

P = 128
D = 1024
KT = D // P
SEQ = 1024
CTX = 256
D_FF = 4096
N_CHUNK = D_FF // D
MLA_HEADS, NOPE, ROPE, MLA_V = 8, 64, 32, 64
MLA_QK = NOPE + ROPE
RET_HEADS, RET_DK, RET_DV = 4, 64, 128
N_Q, HEAD = 8, 64
GRID_W = 64
CONV_W = 31
PAD = CONV_W // 2
EPS_1, EPS_2 = 1e-5, 1e-6
ALPHA = 2.0 ** 0.25
IN_KR = 320
MAGIC = 1.5 * 2.0 ** 23
TWO_PI_PARTS = (6.28125, 0.0019350051879882812, 3.0199157663446e-07)
PI_SAFE = 3.1415925
NEG = -1e30

VEC_PARTS = [
    ("c", 8), ("c2", 16), ("ln_in_g", 8), ("ln_in_b", 8), ("ln1_g", 8), ("ln1_b", 8), ("ln2_g", 8), ("ln2_b", 8),
    ("e_norm", 8), ("o_norm", 8), ("final", 8), ("b_ada", 48), ("e_b", 24), ("o_b", 24), ("q_norm", 2),
    ("kv_norm", 1), ("gn_g", 4), ("gn_b", 4), ("conv_w", 4 * CONV_W), ("conv_b", 4), ("a_ln_g", 4), ("a_ln_b", 4),
    ("pw_b", 4), ("c_conv", 12), ("sink", 8), ("zeta", 4), ("inv_ret", 1), ("inv_mla", 1), ("g_chunk", 2),
    ("eps1", 1), ("eps2", 1),
]
VEC, _at = {}, 0
for _name, _n in VEC_PARTS:
    VEC[_name] = _at
    _at += _n
N_VEC = _at


def shape_constants():
    f = np.float64
    out = {}
    out["ident"] = np.eye(P, dtype=np.float32)

    def pairs(period, half, lo, hi):
        m = np.zeros((P, P), np.float32)
        for d in range(lo, hi):
            if (d - lo) % period < half:
                m[d + half, d] = -1.0
            else:
                m[d - half, d] = 1.0
        return m

    out["swap_ret"] = pairs(64, 32, 0, P)
    out["swap_mla"] = pairs(32, 16, NOPE, MLA_QK)
    out["swap_win"] = pairs(32, 16, 0, P)
    log_g = np.log(1.0 - 2.0 ** (-5.0 - np.arange(RET_HEADS, dtype=f)))
    idx = np.arange(P, dtype=f)
    k_scale = RET_DK ** -0.5
    dec = np.zeros((P, RET_HEADS, P), f)
    for h in range(RET_HEADS):
        diff = idx[None, :] - idx[:, None]
        dec[:, 2 * (h % 2) + h // 2] = np.where(diff >= 0, np.exp(log_g[h] * np.maximum(diff, 0)), 0.0) * k_scale
    out["decay"] = dec.reshape(P, -1).astype(np.float32)
    xi = np.zeros((P, 2, P), f)
    for p in range(2):
        for hh in range(2):
            xi[64 * hh:64 * hh + 64, p] = np.exp(log_g[2 * p + hh] * (idx + 1.0))[None]
    out["xi"] = xi.reshape(P, -1).astype(np.float32)
    cols = np.zeros((P, 11), f)
    for h in range(RET_HEADS):
        cols[:, h] = np.exp(log_g[h] * (P - 1 - idx)) * k_scale
    inv32 = (np.float32(10000.0) ** (-np.arange(32, dtype=np.float32) / np.float32(32))).astype(np.float32)
    inv16 = (np.float32(10000.0) ** (-np.arange(16, dtype=np.float32) / np.float32(16))).astype(np.float32)
    cols[:, 4] = inv32[np.arange(P) % 32]
    cols[:, 5] = inv16[np.arange(P) % 16]
    for p in range(2):
        for hh in range(2):
            cols[64 * hh:64 * hh + 64, 6 + p] = np.exp(log_g[2 * p + hh] * P)
    cols[:, 8], cols[:, 9] = EPS_1, EPS_2
    out["cols"] = cols[:, :10].astype(np.float32)
    tok = np.arange(SEQ)
    where = np.stack([tok // GRID_W, tok % GRID_W]).astype(np.float32)
    d = np.arange(P) % HEAD
    ang = (where[d // 32] * inv16[d % 16][:, None]).astype(np.float32).astype(f)
    out["cos_win"], out["sin_win"] = np.cos(ang).astype(np.float32), np.sin(ang).astype(np.float32)
    n = np.arange(P, dtype=f)
    th = 2 * np.pi * (np.outer(n, n) % P) / P
    out["dft_d"] = np.concatenate([np.cos(th), -np.sin(th)], 1).astype(f) / np.sqrt(P)
    out["dft_d"] = out["dft_d"].astype(np.float32)
    for length in (SEQ, CTX):
        tiles = []
        for parity in range(2):
            for m in range(length // 2 // P):
                l = 2 * (m * P + np.arange(P)) + parity
                a = 2 * np.pi * (np.outer(l, np.arange(length // 2)) % length) / length
                tiles.append(np.concatenate([np.cos(a), np.sin(a)], 1))
        out[f"dft_{length}"] = np.concatenate(tiles).astype(np.float32)
    return out


def mask_constants():
    q, k = np.arange(P)[:, None], np.arange(P)[None, :]
    return np.concatenate([np.eye(P), np.where(k > q, NEG, 0.0), np.where(k < q, NEG, 0.0)], 1).astype(np.float32)


def build_program(nc, A, out):
    ctx = ExitStack()
    with ctx:
        BANK = 40
        banks_of_signals = [[ctx.enter_context(nc.semaphore(f"stage_signal_{b}_{i}")) for i in range(BANK)]
                            for b in range(2)]
        named = {}
        current = [0]

        def S(name):
            mine = named.setdefault(current[0], {})
            if name not in mine:
                mine[name] = banks_of_signals[current[0] % 2][len(mine)]
            return mine[name]

        def whole(name):
            return ctx.enter_context(nc.semaphore(name))

        base = 16640
        kb = 1024

        def at(name, shape, dt, offset):
            return nc.alloc_sbuf_tensor_at(name, shape, dt, offset=base + offset)

        X = at("X", [P, KT, SEQ], F32, 0)
        RAW = [at(f"RAW{s}", [P, KT, P], F32, 32 * kb + 4 * kb * s) for s in range(2)]
        WH = [at(f"WH{s}", [P, KT, P], F32R, 40 * kb + 4 * kb * s) for s in range(2)]
        WL = [at(f"WL{s}", [P, KT, P], F32R, 48 * kb + 4 * kb * s) for s in range(2)]
        small = [56 * kb]

        def keep(name, shape, dt):
            n = int(np.prod(shape[1:])) * (2 if dt == BF16 else 4)
            t = at(name, shape, dt, small[0])
            small[0] += (n + 31) // 32 * 32
            return t

        IDENT = keep("IDENT", [P, P], F32)
        ONES = keep("ONES", [P, P], F32)
        MASKS = keep("MASKS", [P, 3 * P], BF16)
        V = keep("V", [P, N_VEC], F32)
        MODA = keep("MODA", [P, 48], F32)
        MODE = keep("MODE", [P, 24, 2], F32)
        MODO = keep("MODO", [P, 24, 2], F32)
        CACT = keep("CACT", [P, 8], F32)
        C2ACT = keep("C2ACT", [P, 8, 2], F32)
        GS = keep("GS", [P, 2, 8, 2], F32)
        KC = keep("KC", [P, CTX], F32)
        VC = keep("VC", [P, 2, P], F32)
        BNS = keep("BNS", [P, 8, 4, 6], F32)
        MV = keep("MV", [P, 32, 2], F32)
        SD = keep("SD", [P, 32], F32)
        RS = keep("RS", [P, 32], F32)
        ROW = {n: keep(n, [P, 8], F32) for n in ("NMX", "NB", "SUM", "RDEN", "ESINK")}
        assert small[0] <= 64 * kb, small[0]
        z0 = small[0]
        assert base + z0 + 144 * kb <= 229368, base + z0 + 144 * kb

        def Z(name, shape, dt, offset_kb):
            return at(name, shape, dt, z0 + int(offset_kb * kb))

        HH = Z("HH", [P, KT, SEQ], F32R, 80)
        HL = Z("HL", [P, KT, SEQ], F32R, 112)
        T32 = [Z(f"T32_{s}", [P, SEQ], F32, 72 + 4 * s) for s in range(2)]

        G = [ctx.enter_context(nc.psum_tensor(f"G{s}", [P, 1024], F32)) for s in range(2)]
        M = [ctx.enter_context(nc.psum_tensor(f"M{s}", [P, 1024], F32)) for s in range(2)]

        raw_loaded = [whole(f"raw_loaded{s}") for s in range(2)]
        raw_used = [whole(f"raw_used{s}") for s in range(2)]
        w_split = [whole(f"w_split{s}") for s in range(2)]
        unit_done = [whole(f"unit_done{s}") for s in range(2)]
        unit_freed = [whole(f"unit_freed{s}") for s in range(2)]
        left = {k: whole(f"stages_left_by_{k}") for k in ("act", "pe", "dve")}
        w_high = whole("w_high")
        split_begun = whole("split_begun")
        q_half = whole("q_half")
        moved = whole("moved")

        def vec(name, i=0, n=1):
            return V[:, VEC[name] + i:VEC[name] + i + n]

        stages = []
        count = {"raw": 0, "unit": 0, "dma": 0}

        def stage(name, progs, raw=None, units=0, dmas=()):
            n_raw = sum(2 * n for n, _ in raw or [])
            stages.append(dict(name=name, progs=progs, raw=raw or [], r0=count["raw"], u0=count["unit"],
                               units=units, dmas=list(dmas), dma_end=count["dma"] + 16 * len(dmas)))
            count["raw"] += n_raw
            count["unit"] += units
            count["dma"] += 16 * len(dmas)

        def info(name):
            return next(s for s in stages if s["name"] == name)

        def cols(w, c0):
            return lambda s, i: w[:, bass.ds(c0 + i * 256 + s * P, P)].rearrange("(k p) n -> p k n", p=P)

        def load_unit(sp, r2, s, src, view):
            need(sp, raw_used[s], r2)
            sp.dma_start(view, src).then_inc(raw_loaded[s], 16)

        def split_pairs(pool, r0, u0, n_pairs):
            def pair(i):
                for s in range(2):
                    pool.wait_ge(raw_loaded[s], (i + r0 // 2) * 16 + 16)
                    need(pool, unit_done[s], i + u0 // 2)
                    pool.sem_inc(split_begun, 1)
                    pool.tensor_scalar(WH[s][:], RAW[s][:], 1.0, 0.0, ALU.mult, ALU.add).then_inc(w_high, 1)
                    pool.wait_ge(w_high, (i + u0 // 2) * 2 + s + 1)
                    need(pool, w_split[s], i + u0 // 2)
                    pool.tensor_tensor(WL[s][:], RAW[s][:], WH[s][:].bitcast(F32), ALU.subtract).then_inc(w_split[s], 1)
                    pool.wait_ge(w_split[s], i + u0 // 2 + 1)
                    pool.sem_inc(raw_used[s], 1)
            turns(pool, n_pairs, pair)

        def gemm_pairs(pe, u0, n_pairs, T, acts, waits=None):
            hi, lo = acts
            nt = max(1, T // 512)
            w = T // nt

            def pair(i, wait=None):
                for s in range(2):
                    pe.wait_ge(w_split[s], i + u0 // 2 + 1)
                    need(pe, unit_freed[s], i + u0 // 2)
                    for k in range(KT):
                        if wait and s == 0:
                            pe.wait_ge(wait[0], wait[1] + k)
                        for part, moving in ((WH, hi), (WH, lo), (WL, hi)):
                            for n in range(nt):
                                m = pe.matmul(G[s][:, n * w:(n + 1) * w], part[s][:, k, :],
                                              moving[:, k, n * w:(n + 1) * w],
                                              start=(k == 0 and part is WH and moving is hi),
                                              stop=(k == KT - 1 and part is WL))
                    m.then_inc(unit_done[s], 1)
            turns(pe, n_pairs, lambda i: pair(i, waits if isinstance(i, int) else None))

        def turns(eng, n, body):
            body(0)
            if n > 1:
                with eng.Fori(1, n) as i:
                    body(i)

        def need(eng, signal, value):
            if not isinstance(value, int) or value > 0:
                eng.wait_ge(signal, value)

        def unit_ready(eng, U):
            eng.wait_ge(unit_done[U % 2], U // 2 + 1)

        def mods_act(act):
            act.wait_ge(moved, info("mods")["dma_end"])
            act.activation(CACT[:], vec("c", 0, 8), ACT.Silu).then_inc(S("c_act"), 1)
            act.activation(C2ACT[:].rearrange("p k c -> p (k c)"), vec("c2", 0, 16), ACT.Silu).then_inc(S("c_act"), 1)

        MOD_SETS = [("b_ada", 24, 1), ("e_b", 12, 2), ("o_b", 12, 2)]

        def mods_pe(pe):
            pe.wait_ge(S("c_act"), 2)
            r2 = 0
            for name, n_pairs, width in MOD_SETS:
                def pair(i):
                    for s in range(2):
                        pe.wait_ge(raw_loaded[s], (i + r2) * 16 + 16)
                        need(pe, S(f"mod_read{s}"), i + r2)
                        for k in range(KT):
                            x = CACT[:, k:k + 1] if width == 1 else C2ACT[:, k, :]
                            m = pe.matmul(M[s][:, 0:width], RAW[s][:, k, :], x, start=(k == 0), stop=(k == KT - 1))
                        m.then_inc(raw_used[s], 1)
                turns(pe, n_pairs, pair)
                r2 += n_pairs

        MASK32 = Z("MASK32", [P, 3 * P], F32, 40)

        def mods_dve(dve):
            dve.memset(ONES[:], 1.0).then_inc(S("ones"), 1)
            dve.wait_ge(moved, info("mods")["dma_end"])
            dve.tensor_copy(MASKS[:], MASK32[:]).then_inc(S("masks"), 1)
            r2 = 0
            for (name, n_pairs, width), dst in zip(MOD_SETS, (MODA, MODE, MODO)):
                def pair(i):
                    for s in range(2):
                        dve.wait_ge(raw_used[s], i + r2 + 1)
                        o = dst[:, bass.ds(i * 2 + s, 1)] if width == 1 else dst[:, bass.ds(i * 2 + s, 1), :]
                        if width == 1:
                            dve.tensor_tensor(o, M[s][:, 0:1], V[:, bass.ds(i * 2 + (VEC[name] + s), 1)],
                                              ALU.add).then_inc(S(f"mod_read{s}"), 1)
                        else:
                            dve.tensor_scalar(o.rearrange("p a b -> p (a b)"), M[s][:, 0:2],
                                              V[:, bass.ds(i * 2 + (VEC[name] + s), 1)], None,
                                              ALU.add).then_inc(S(f"mod_read{s}"), 1)
                turns(dve, n_pairs, pair)
                r2 += n_pairs
            for s in range(2):
                dve.wait_ge(S(f"mod_read{s}"), r2)
            one = S("one_plus")
            dve.tensor_scalar(MODA[:, 8:16], MODA[:, 8:16], 1.0, None, ALU.add).then_inc(one, 1)
            dve.tensor_scalar(MODA[:, 32:40], MODA[:, 32:40], 1.0, None, ALU.add).then_inc(one, 1)
            for l, (mod, gain) in enumerate(((MODE, "e_norm"), (MODO, "o_norm"))):
                for c in range(2):
                    dve.scalar_tensor_tensor(out=GS[:, l, :, c], in0=mod[:, 8:16, c], scalar=1.0,
                                             in1=vec(gain, 0, 8), op0=ALU.add, op1=ALU.mult).then_inc(one, 1)

        stage("mods", dict(act=mods_act, pe=mods_pe, dve=mods_dve),
              raw=[(24, cols(A["w_ada"], 0)), (12, cols(A["e_w_mod"], 0)), (12, cols(A["o_w_mod"], 0))],
              dmas=[(V[:], A["vecs"]), (IDENT[:], A["ident"]), (MASK32[:], A["masks"])])

        def h_act(act, tag, ready, T, src, scale, shift, hh=None):
            for f in range(KT):
                act.wait_ge(ready, f + 1)
                if f >= 2:
                    act.wait_ge(S(tag + "_lo"), f - 1)
                act.activation(T32[f % 2][:, :T], src(f), ACT.Identity, bias=shift(f),
                               scale=scale(f)).then_inc(S(tag + "_t32"), 1)
                act.wait_ge(S(tag + "_t32"), f + 1)
                act.activation(HH[:, f, :T], T32[f % 2][:, :T], ACT.Copy).then_inc(S(tag + "_hi"), 1)

        def h_low(dve, tag, f, T):
            dve.wait_ge(S(tag + "_hi"), f + 1)
            dve.tensor_tensor(HL[:, f, :T], T32[f % 2][:, :T], HH[:, f, :T].bitcast(F32),
                              ALU.subtract).then_inc(S(tag + "_lo"), 1)

        def prescale(dve, tag, f):
            dve.tensor_scalar(X[:, f, :], X[:, f, :], ALPHA, None, ALU.mult).then_inc(S(tag + "_alpha"), 1)

        XT = Z("XT", [P, KT, D], F32, 0)
        NT = SEQ // P

        def lnin_dve(dve):
            dve.wait_ge(moved, info("lnin")["dma_end"])
            for t in range(NT):
                for j in range(2):
                    dve.bn_stats(BNS[:, t, j, :], XT[:, t, 512 * j:512 * j + 512]).then_inc(S("li_st"), 1)
                dve.wait_ge(S("li_st"), 2 * t + 2)
                dve.bn_aggr(MV[:, t, :], BNS[:, t, 0:2, :].rearrange("p a b -> p (a b)")).then_inc(S("li_mv"), 1)
            dve.wait_ge(S("li_sd"), 1)
            dve.reciprocal(RS[:, 0:NT], SD[:, 0:NT]).then_inc(S("li_rs"), 1)
            dve.wait_ge(S("li_rs"), 1)
            for t in range(NT):
                dve.tensor_scalar(XT[:, t, :], XT[:, t, :], MV[:, t, 0:1], RS[:, t:t + 1], ALU.subtract,
                                  ALU.mult).then_inc(S("li_xn"), 1)
            for f in range(KT):
                dve.wait_ge(S("li_tr"), f + 1)
                dve.tensor_scalar(X[:, f, :], M[f % 2][:], vec("ln_in_g", f), vec("ln_in_b", f), ALU.mult,
                                  ALU.add).then_inc(S("li_x"), 1)
                if f:
                    h_low(dve, "li", f - 1, SEQ)
                    prescale(dve, "li", f - 1)
            h_low(dve, "li", KT - 1, SEQ)
            prescale(dve, "li", KT - 1)

        def lnin_act(act):
            act.wait_ge(S("li_mv"), NT)
            act.activation(SD[:, 0:NT], MV[:, 0:NT, 1], ACT.Sqrt, bias=vec("eps1"), scale=1.0).then_inc(S("li_sd"), 1)
            h_act(act, "li", S("li_x"), SEQ, lambda f: X[:, f, :], lambda f: MODA[:, 8 + f:9 + f],
                  lambda f: MODA[:, f:f + 1])

        def lnin_pe(pe):
            pe.wait_ge(S("li_xn"), NT)
            for f in range(KT):
                if f >= 2:
                    pe.wait_ge(S("li_x"), f - 1)
                for t in range(NT):
                    m = pe.transpose(M[f % 2][:, t * P:(t + 1) * P], XT[:, t, f * P:(f + 1) * P], IDENT[:])
                m.then_inc(S("li_tr"), 1)

        stage("lnin", dict(act=lnin_act, pe=lnin_pe, dve=lnin_dve),
              dmas=[(XT[:, t, :], A["x"][t * P:(t + 1) * P, :]) for t in range(NT)])

        QC = Z("QC", [P, 2, SEQ], F32, 0)
        KVC = Z("KVC", [P, SEQ], F32, 8)
        KR = Z("KR", [P, SEQ], F32, 12)
        RQ = Z("RQ", [P, 2, SEQ], F32, 16)
        RK = Z("RK", [P, 2, SEQ], F32, 24)
        RV = Z("RV", [P, 4, SEQ], F32, 32)
        RG = Z("RG", [P, 4, SEQ], F32, 48)
        WIN_COLS = [0, 128, 256, IN_KR, 416, 544, 672, 800] + [928 + 128 * i for i in range(4)] + \
            [1440 + 128 * i for i in range(4)]
        win_dst = [QC[:, 0, :], QC[:, 1, :], KVC[:], KR[:], RQ[:, 0, :], RQ[:, 1, :], RK[:, 0, :], RK[:, 1, :]] + \
            [RV[:, i, :] for i in range(4)]

        def win_dve(dve):
            u0 = info("win")["u0"]
            for j, dst in enumerate(win_dst):
                unit_ready(dve, u0 + j)
                dve.tensor_copy(dst, G[j % 2][:]).then_inc(unit_freed[j % 2], 1)

        def win_act(act):
            u0 = info("win")["u0"]
            for j in range(12, 16):
                unit_ready(act, u0 + j)
                act.activation(RG[:, j - 12, :], G[j % 2][:], ACT.Silu).then_inc(unit_freed[j % 2], 1)

        def win_unit(j):
            return A["w_in"][:, WIN_COLS[j]:WIN_COLS[j] + P].rearrange("(k p) n -> p k n", p=P)

        stage("win", dict(act=win_act, pe=lambda pe: gemm_pairs(pe, info("win")["u0"], 8, SEQ, (HH, HL)), dve=win_dve),
              raw=[(1, lambda s, i, j=j: win_unit(2 * j + s)) for j in range(8)], units=16)

        COSR, SINR = Z("COSR", [P, SEQ], F32, 112), Z("SINR", [P, SEQ], F32, 116)
        COSM, SINM = Z("COSM", [P, SEQ], F32, 120), Z("SINM", [P, SEQ], F32, 124)
        POSI = Z("POSI", [P, SEQ], I32, 80)
        POSF = Z("POSF", [P, SEQ], F32, 84)
        ANG, TRN = Z("ANG", [P, SEQ], F32, 88), Z("TRN", [P, SEQ], F32, 92)

        def trig_pe(pe):
            pe.wait_ge(S("tr_pos"), 1)
            for n in range(2):
                m = pe.matmul(M[0][:, 512 * n:512 * n + 512], ONES[0:1, :], POSF[0:1, 512 * n:512 * n + 512],
                              start=True, stop=True)
            m.then_inc(S("tr_bc"), 1)

        def trig_dve(dve):
            dve.wait_ge(moved, info("trig")["dma_end"])
            dve.tensor_copy(POSF[0:1, :], POSI[0:1, :]).then_inc(S("tr_pos"), 1)
            dve.wait_ge(S("tr_bc"), 1)
            chain = S("tr_chain")
            n = [0]

            def step(ins):
                ins.then_inc(chain, 1)
                n[0] += 1
                dve.wait_ge(chain, n[0])
            for q, (inv, sin, cos) in enumerate((("inv_ret", SINR, COSR), ("inv_mla", SINM, COSM))):
                step(dve.tensor_scalar(ANG[:], M[0][:], vec(inv), None, ALU.mult))
                step(dve.tensor_scalar(TRN[:], ANG[:], 1.0 / (2.0 * np.pi), MAGIC, ALU.mult, ALU.add))
                step(dve.tensor_scalar(TRN[:], TRN[:], -MAGIC, None, ALU.add))
                for part in TWO_PI_PARTS:
                    step(dve.scalar_tensor_tensor(out=ANG[:], in0=TRN[:], scalar=-part, in1=ANG[:], op0=ALU.mult,
                                                  op1=ALU.add))
                dve.tensor_scalar(ANG[:], ANG[:], PI_SAFE, -PI_SAFE, ALU.min, ALU.max).then_inc(S("tr_ang"), 1)
                dve.wait_ge(S("tr_sin"), 3 * q + 3)
                dve.tensor_scalar(cos[:], cos[:], -2.0, 1.0, ALU.mult, ALU.add).then_inc(S("tr_cos"), 1)

        def trig_act(act):
            for q, (sin, cos) in enumerate(((SINR, COSR), (SINM, COSM))):
                act.wait_ge(S("tr_ang"), q + 1)
                act.activation(sin[:], ANG[:], ACT.Sin).then_inc(S("tr_sin"), 1)
                act.activation(cos[:], ANG[:], ACT.Sin, scale=0.5).then_inc(S("tr_sin"), 1)
                act.wait_ge(S("tr_sin"), 3 * q + 2)
                act.activation(cos[:], cos[:], ACT.Square).then_inc(S("tr_sin"), 1)

        stage("trig", dict(act=trig_act, pe=trig_pe, dve=trig_dve), dmas=[(POSI[0:1, :], A["positions"])])

        def swap_pe(pe, tag, i, tile, swap):
            if i >= 2:
                pe.wait_ge(S(tag + "_mul"), i - 1)
            for n in range(2):
                m = pe.matmul(M[i % 2][:, 512 * n:512 * n + 512], swap, tile[:, 512 * n:512 * n + 512],
                              start=True, stop=True)
            m.then_inc(S(tag + "_sw"), 1)

        def rope_dve(dve, tag, i, tile, cos, sin, tmp):
            dve.wait_ge(S(tag + "_sw"), i + 1)
            if i:
                dve.wait_ge(S(tag + "_rot"), 2 * i)
            dve.tensor_tensor(tmp, M[i % 2][:], sin, ALU.mult).then_inc(S(tag + "_mul"), 1)
            dve.tensor_tensor(tile, tile, cos, ALU.mult).then_inc(S(tag + "_rot"), 1)
            dve.wait_ge(S(tag + "_mul"), i + 1)
            dve.wait_ge(S(tag + "_rot"), 2 * i + 1)
            dve.tensor_tensor(tile, tile, tmp, ALU.add).then_inc(S(tag + "_rot"), 1)

        VT = Z("VT", [P, NT, 512], F32, 64)
        KZ = Z("KZ", [P, NT, 256], F32, 80)
        SWAPR = Z("SWAPR", [P, P], F32, 88)
        DECAY = Z("DECAY", [P, 512], F32, 89)
        XI = Z("XI", [P, 2, P], F32, 91)
        QX = [Z(f"QX{s}", [P, 2, P], F32, 92 + s) for s in range(2)]
        RTMP = Z("RTMP", [P, SEQ], F32, 120)
        STATE = [Z(f"STATE{s}", [P, 2, 256], F32, 112 + 2 * s) for s in range(2)]
        SCT = [Z(f"SCT{s}", [P, 512], F32, 116 + 2 * s) for s in range(2)]
        RTMP = Z("RTMP_", [P, SEQ], F32, 100)

        def rpre_pe(pe):
            pe.wait_ge(moved, info("rpre")["dma_end"])
            for i in range(4):
                swap_pe(pe, "rr", i, (RQ if i < 2 else RK)[:, i % 2, :], SWAPR[:])
            for j in range(4):
                pe.wait_ge(S("rr_mul"), min(3 + j, 4))
                if j >= 2:
                    pe.wait_ge(S("rv_out"), j - 1)
                for t in range(NT):
                    m = pe.transpose(M[j % 2][:, t * P:(t + 1) * P], RV[:, j, t * P:(t + 1) * P], IDENT[:])
                m.then_inc(S("rv_tr"), 1)
            pe.wait_ge(S("rr_rot"), 8)
            for j in range(2):
                pe.wait_ge(S("rv_out"), 3 + j)
                for t in range(NT):
                    m = pe.transpose(M[j][:, t * P:(t + 1) * P], RK[:, j, t * P:(t + 1) * P], IDENT[:])
                m.then_inc(S("rk_tr"), 1)

        def rpre_dve(dve):
            for i in range(4):
                rope_dve(dve, "rr", i, (RQ if i < 2 else RK)[:, i % 2, :], COSR[:], SINR[:], RTMP[:])
            for j in range(4):
                dve.wait_ge(S("rv_tr"), j + 1)
                dve.tensor_copy(VT[:, :, j * P:(j + 1) * P], M[j % 2][:].rearrange("p (t n) -> p t n", n=P))\
                   .then_inc(S("rv_out"), 1)

        def rpre_act(act):
            for j in range(2):
                act.wait_ge(S("rk_tr"), j + 1)
                for hh in range(2):
                    act.activation(KZ[:, :, j * P + 64 * hh:j * P + 64 * hh + 64],
                                   M[j][:].rearrange("p (t n) -> p t n", n=P)[:, :, 64 * hh:64 * hh + 64],
                                   ACT.Copy, scale=vec("zeta", 2 * j + hh)).then_inc(S("kz"), 1)

        stage("rpre", dict(act=rpre_act, pe=rpre_pe, dve=rpre_dve),
              dmas=[(SWAPR[:], A["swap_ret"]), (DECAY[:], A["decay"]), (XI[:].rearrange("p a b -> p (a b)"), A["xi"])])

        def in_bank(ps, h):
            return ps[:, 512 * (h % 2) + P * (h // 2):512 * (h % 2) + P * (h // 2) + P]

        def ret_pe(pe):
            def scores(c):
                if c >= 2:
                    pe.wait_ge(S("ret_dec"), c - 1)
                    pe.wait_ge(S("ret_state"), 2 * c - 2)
                for p in range(2):
                    pe.matmul(G[c % 2][:, 512 * p + 256:512 * p + 512], KZ[:, c, p * P:(p + 1) * P],
                              VT[:, c, p * 256:(p + 1) * 256], start=True, stop=True)
                t = slice(c * P, (c + 1) * P)
                for h in range(RET_HEADS):
                    r = slice(64 * (h % 2), 64 * (h % 2) + 64)
                    m = pe.matmul(in_bank(G[c % 2], h), RK[r, h // 2, t], RQ[r, h // 2, t], start=True, stop=True)
                m.then_inc(S("ret_sc"), 1)
            scores(0)
            for c in range(NT):
                if c + 1 < NT:
                    scores(c + 1)
                pe.wait_ge(S("ret_dec"), c + 1)
                if c >= 2:
                    pe.wait_ge(S("ret_out"), c - 1)
                if c:
                    pe.wait_ge(S("ret_qx"), 2 * c)
                    pe.wait_ge(S("ret_state"), 2 * c)
                for h in range(RET_HEADS):
                    r = slice(64 * (h % 2), 64 * (h % 2) + 64)
                    q = 2 * (h % 2) + h // 2
                    m = pe.matmul(in_bank(M[c % 2], h), SCT[c % 2][:, q * P:(q + 1) * P], VT[:, c, h * P:(h + 1) * P],
                                  start=True, stop=(c == 0))
                    if c:
                        m = pe.matmul(in_bank(M[c % 2], h), QX[c % 2][r, h // 2, :],
                                      STATE[(c - 1) % 2][r, h // 2, P * (h % 2):P * (h % 2) + P], start=False,
                                      stop=True)
                m.then_inc(S("ret_o"), 1)

        def ret_dve(dve):
            for c in range(NT):
                dve.wait_ge(S("ret_sc"), c + 1)
                if c >= 2:
                    dve.wait_ge(S("ret_o"), c - 1)
                dve.tensor_tensor(SCT[c % 2][:].rearrange("p (o n) -> p o n", o=2),
                                  G[c % 2][:].rearrange("p (o n) -> p o n", o=2)[:, :, 0:256],
                                  DECAY[:].rearrange("p (o n) -> p o n", o=2), ALU.mult).then_inc(S("ret_dec"), 1)
                if c:
                    for p in range(2):
                        dve.tensor_tensor(QX[c % 2][:, p, :], RQ[:, p, c * P:(c + 1) * P], XI[:, p, :],
                                          ALU.mult).then_inc(S("ret_qx"), 1)
                if c + 1 < NT:
                    for p in range(2):
                        kv = G[c % 2][:, 512 * p + 256:512 * p + 512]
                        if c == 0:
                            dve.tensor_copy(STATE[0][:, p, :], kv).then_inc(S("ret_state"), 1)
                        else:
                            dve.wait_ge(S("ret_state"), 2 * c)
                            dve.wait_ge(S("ret_o"), c)
                            dve.scalar_tensor_tensor(out=STATE[c % 2][:, p, :], in0=STATE[(c - 1) % 2][:, p, :],
                                                     scalar=vec("g_chunk", p), in1=kv, op0=ALU.mult,
                                                     op1=ALU.add).then_inc(S("ret_state"), 1)
            for c in range(NT):
                dve.wait_ge(S("ret_out"), c + 1)
                for h in range(RET_HEADS):
                    dve.bn_stats(BNS[:, c, h, :], VT[:, c, h * P:(h + 1) * P]).then_inc(S("ret_st"), 1)
            dve.wait_ge(S("ret_st"), 32)
            for c in range(NT):
                for h in range(RET_HEADS):
                    dve.bn_aggr(MV[:, 4 * c + h, :], BNS[:, c, h, :]).then_inc(S("ret_mv"), 1)
            dve.wait_ge(S("ret_sd"), 1)
            dve.reciprocal(RS[:], SD[:]).then_inc(S("ret_rs"), 1)
            dve.wait_ge(S("ret_rs"), 1)
            for h in range(RET_HEADS):
                for c in range(NT):
                    o = VT[:, c, h * P:(h + 1) * P]
                    q = 4 * c + h
                    dve.tensor_scalar(o, o, MV[:, q, 0:1], RS[:, q:q + 1], ALU.subtract, ALU.mult)\
                       .then_inc(S("ret_n"), 1)
            for h in range(RET_HEADS):
                dve.wait_ge(S("ret_t32"), h + 1)
                dve.tensor_tensor(RG[:, h, :], T32R[h % 2][:], RG[:, h, :], ALU.mult).then_inc(S("ret_gate"), 1)
                dve.wait_ge(S("ret_hi"), h + 1)
                dve.tensor_tensor(HL[:, 4 + h, :], RG[:, h, :], HH[:, 4 + h, :].bitcast(F32),
                                  ALU.subtract).then_inc(S("ret_lo"), 1)

        T32R = [Z(f"T32R{s}", [P, SEQ], F32, 80 + 4 * s) for s in range(2)]

        def ret_act(act):
            for c in range(NT):
                act.wait_ge(S("ret_o"), c + 1)
                act.activation(VT[:, c, :].rearrange("q (p o n) -> q o p n", p=2, o=2),
                               M[c % 2][:].rearrange("q (o p n) -> q o p n", o=2, n=P)[:, :, 0:2, :], ACT.Copy)\
                   .then_inc(S("ret_out"), 1)
            act.wait_ge(S("ret_mv"), 32)
            act.activation(SD[:], MV[:, :, 1], ACT.Sqrt, bias=vec("eps1"), scale=1.0).then_inc(S("ret_sd"), 1)
            for h in range(RET_HEADS):
                act.wait_ge(S("ret_nt"), h + 1)
                if h >= 2:
                    act.wait_ge(S("ret_gate"), h - 1)
                act.activation(T32R[h % 2][:], M[h % 2][:], ACT.Identity, bias=vec("gn_b", h),
                               scale=vec("gn_g", h)).then_inc(S("ret_t32"), 1)
                act.wait_ge(S("ret_gate"), h + 1)
                act.activation(HH[:, 4 + h, :], RG[:, h, :], ACT.Copy).then_inc(S("ret_hi"), 1)

        def ret_pe2(pe):
            ret_pe(pe)
            for h in range(RET_HEADS):
                pe.wait_ge(S("ret_n"), 8 * h + 8)
                if h >= 2:
                    pe.wait_ge(S("ret_t32"), h - 1)
                for c in range(NT):
                    m = pe.transpose(M[h % 2][:, c * P:(c + 1) * P], VT[:, c, h * P:(h + 1) * P], IDENT[:])
                m.then_inc(S("ret_nt"), 1)

        stage("ret", dict(act=ret_act, pe=ret_pe2, dve=ret_dve))

        ATT = Z("ATT", [P, NT, 512], F32, 16)
        QH = [Z(f"QH{s}", [P, SEQ], F32, 32 + 4 * s) for s in range(2)]
        KH = [Z(f"KH{s}", [P, SEQ], F32, 40 + 4 * s) for s in range(2)]
        VH = [Z(f"VH{s}", [P, NT, MLA_V], F32, 48 + 2 * s) for s in range(2)]
        PR = [Z(f"PR{s}", [P, SEQ], F32, 52 + 4 * s) for s in range(2)]
        PT = [Z(f"PT{s}", [P, SEQ], F32, 60 + 4 * s) for s in range(2)]
        LTMP = Z("LTMP", [P, SEQ], F32, 68)
        LSQ = [Z(f"LSQ{s}", [P, SEQ], F32, 80 + 4 * s) for s in range(3)]
        SWAPM = Z("SWAPM", [P, P], F32, 92)
        MWQ = [Z(f"MWQ{s}", [P, 2, MLA_QK], F32, 92.5 + s) for s in range(2)]
        MWK = [Z(f"MWK{s}", [P, P], F32, 94.5 + 0.5 * s) for s in range(2)]
        LR = [Z(f"LR{s}", [P, SEQ], F32, 112 + 4 * s) for s in range(2)]

        def lat_act(act):
            for i, t in enumerate((QC[:, 0, :], QC[:, 1, :], KVC[:])):
                act.activation(LSQ[i][:], t, ACT.Square).then_inc(S("lat_sq"), 1)
            for i, n in enumerate((256, 128)):
                act.wait_ge(S("lat_ms"), i + 1)
                act.activation(LR[i][:], M[i][:], ACT.Sqrt, bias=vec("eps1"), scale=1.0 / n).then_inc(S("lat_sd"), 1)

        def lat_pe(pe):
            pe.wait_ge(S("lat_sq"), 3)
            for i, tiles in enumerate(((0, 1), (2,))):
                for n in range(2):
                    for k in tiles:
                        m = pe.matmul(M[i][:, 512 * n:512 * n + 512], ONES[:], LSQ[k][:, 512 * n:512 * n + 512],
                                      start=(k == tiles[0]), stop=(k == tiles[-1]))
                m.then_inc(S("lat_ms"), 1)
            pe.wait_ge(moved, info("lat")["dma_end"])
            for n in range(2):
                m = pe.matmul(G[0][:, 512 * n:512 * n + 512], SWAPM[:], KR[:, 512 * n:512 * n + 512], start=True,
                              stop=True)
            m.then_inc(S("lat_sw"), 1)

        def lat_dve(dve):
            for i in range(2):
                dve.wait_ge(S("lat_sd"), i + 1)
                dve.reciprocal(LR[i][:], LR[i][:]).then_inc(S("lat_r"), 1)
                dve.wait_ge(S("lat_r"), i + 1)
                for k, t in (((0, QC[:, 0, :]), (1, QC[:, 1, :])) if i == 0 else ((0, KVC[:]),)):
                    dve.scalar_tensor_tensor(out=t, in0=t, scalar=vec("q_norm" if i == 0 else "kv_norm", k),
                                             in1=LR[i][:], op0=ALU.mult, op1=ALU.mult).then_inc(S("lat_n"), 1)
            dve.wait_ge(S("lat_sw"), 1)
            r = slice(NOPE, MLA_QK)
            dve.tensor_tensor(LTMP[r, :], G[0][r, :], SINM[r, :], ALU.mult).then_inc(S("lat_k"), 1)
            dve.tensor_tensor(KR[r, :], KR[r, :], COSM[r, :], ALU.mult).then_inc(S("lat_k"), 1)
            dve.wait_ge(S("lat_k"), 2)
            for s in range(2):
                dve.tensor_tensor(KH[s][r, :], KR[r, :], LTMP[r, :], ALU.add).then_inc(S("lat_k"), 1)

        stage("lat", dict(act=lat_act, pe=lat_pe, dve=lat_dve), dmas=[(SWAPM[:], A["swap_mla"])])

        SCALE_M = MLA_QK ** -0.5
        causal, before = MASKS[:, P:2 * P], MASKS[:, 2 * P:3 * P]
        identb = MASKS[:, 0:P]

        def mla_head_pe(pe, i, s):
            h8 = (i * 2 + s) * 8
            need(pe, S(f"mla_w{s}"), i * 32 + 32)
            need(pe, S("mla_smax"), h8)
            need(pe, S("mla_exp"), h8)
            need(pe, S("mla_att"), h8)
            for n in range(2):
                for k in range(2):
                    m = pe.matmul(G[0][0:MLA_QK, 512 * n:512 * n + 512], MWQ[s][:, k, :],
                                  QC[:, k, 512 * n:512 * n + 512], start=(k == 0), stop=(k == 1))
            m.then_inc(S("mla_q"), 1)
            for n in range(2):
                m = pe.matmul(G[1][0:NOPE, 512 * n:512 * n + 512], MWK[s][:, 0:NOPE], KVC[:, 512 * n:512 * n + 512],
                              start=True, stop=True)
            m.then_inc(S("mla_k"), 1)
            for t in range(NT):
                m = pe.matmul(M[1][:, t * MLA_V:(t + 1) * MLA_V], KVC[:, t * P:(t + 1) * P], MWK[s][:, NOPE:P],
                              start=True, stop=True)
            m.then_inc(S("mla_v"), 1)
            need(pe, S("mla_qc"), (i * 2 + s) + 1)
            for n in range(2):
                m = pe.matmul(G[0][0:MLA_QK, 512 * n:512 * n + 512], SWAPM[0:MLA_QK, 0:MLA_QK],
                              QH[s][0:MLA_QK, 512 * n:512 * n + 512], start=True, stop=True)
            m.then_inc(S("mla_sw"), 1)
            need(pe, S("mla_kc"), (i * 2 + s) * 2 + 2)
            need(pe, S("mla_rot"), (i * 2 + s) * 3 + 3)

            def scores(t):
                if t >= 2:
                    need(pe, S("mla_exp"), h8 + (t - 1))
                for n in range(0, t * P + P, 512):
                    e = min(n + 512, t * P + P)
                    last = e == t * P + P
                    m = pe.matmul(G[t % 2][:, n:e], QH[s][0:MLA_QK, t * P:(t + 1) * P], KH[s][0:MLA_QK, n:e],
                                  start=True, stop=not last)
                m = pe.matmul(G[t % 2][:, t * P:(t + 1) * P], identb, causal, start=False, stop=True)
                m.then_inc(S("mla_sc"), 1)

            def turn(t):
                need(pe, S("mla_exp"), h8 + (t + 1))
                need(pe, S("mla_pt"), h8 + t)
                for b in range(t + 1):
                    m = pe.transpose(M[0][:, b * P:(b + 1) * P], PR[t % 2][:, b * P:(b + 1) * P], IDENT[:])
                m.then_inc(S("mla_tr"), 1)

            def values(t):
                need(pe, S("mla_pt"), h8 + (t + 1))
                if t >= 2:
                    need(pe, S("mla_att"), h8 + (t - 1))
                for b in range(t + 1):
                    m = pe.matmul(M[1][:, 512 * (t % 2):512 * (t % 2) + MLA_V], PT[t % 2][:, b * P:(b + 1) * P],
                                  VH[s][:, b, :], start=(b == 0), stop=(b == t))
                m.then_inc(S("mla_pv"), 1)
            scores(0)
            for t in range(NT):
                if t + 1 < NT:
                    scores(t + 1)
                if t:
                    values(t - 1)
                turn(t)
            values(NT - 1)

        def mla_pe(pe):
            turns(pe, MLA_HEADS // 2, lambda i: [mla_head_pe(pe, i, s) for s in range(2)])

        def mla_dve(dve):
            def pair(i):
                for s in range(2):
                    h = i * 2 + s
                    h8 = h * 8
                    r = slice(NOPE, MLA_QK)
                    need(dve, S("mla_sw"), h + 1)
                    need(dve, S("mla_rot"), h * 3)
                    dve.tensor_tensor(LTMP[r, :], G[0][r, :], SINM[r, :], ALU.mult).then_inc(S("mla_rot"), 1)
                    dve.tensor_tensor(QH[s][r, :], QH[s][r, :], COSM[r, :], ALU.mult).then_inc(S("mla_rot"), 1)
                    need(dve, S("mla_rot"), h * 3 + 2)
                    dve.tensor_tensor(QH[s][r, :], QH[s][r, :], LTMP[r, :], ALU.add).then_inc(S("mla_rot"), 1)

                    def smax(t):
                        need(dve, S("mla_sc"), h8 + (t + 1))
                        need(dve, S("mla_smax"), h8 + t)
                        dve.tensor_reduce(ROW["NMX"][:, t:t + 1], G[t % 2][:, 0:(t + 1) * P], AX.X, ALU.max)\
                           .then_inc(S("mla_mx"), 1)
                        need(dve, S("mla_mx"), h8 + (t + 1))
                        need(dve, S("mla_exp"), h8)
                        dve.tensor_scalar(ROW["NB"][:, t:t + 1], ROW["NMX"][:, t:t + 1], -SCALE_M, None, ALU.mult)\
                           .then_inc(S("mla_smax"), 1)

                    def tail(t):
                        need(dve, S("mla_tr"), h8 + (t + 1))
                        need(dve, S("mla_pv"), h8 + (t - 1) if t else h8)
                        dve.tensor_copy(PT[t % 2][:, 0:(t + 1) * P], M[0][:, 0:(t + 1) * P]).then_inc(S("mla_pt"), 1)
                        need(dve, S("mla_rd"), h8 + t)
                        dve.reciprocal(ROW["RDEN"][:, t:t + 1], ROW["SUM"][:, t:t + 1]).then_inc(S("mla_rd"), 1)

                    def put(t):
                        need(dve, S("mla_pv"), h8 + (t + 1))
                        need(dve, S("mla_rd"), h8 + (t + 1))
                        dve.tensor_scalar(ATT[:, t, bass.ds(h * MLA_V, MLA_V)],
                                          M[1][:, 512 * (t % 2):512 * (t % 2) + MLA_V], ROW["RDEN"][:, t:t + 1],
                                          None, ALU.mult).then_inc(S("mla_att"), 1)
                    smax(0)
                    for t in range(NT):
                        if t + 1 < NT:
                            smax(t + 1)
                        if t:
                            put(t - 1)
                        tail(t)
                    put(NT - 1)
            turns(dve, MLA_HEADS // 2, pair)

        def mla_act(act):
            def pair(i):
                for s in range(2):
                    h = i * 2 + s
                    h8 = h * 8
                    need(act, S("mla_q"), h + 1)
                    act.activation(QH[s][0:MLA_QK, :], G[0][0:MLA_QK, :], ACT.Copy).then_inc(S("mla_qc"), 1)
                    need(act, S("mla_k"), h + 1)
                    act.activation(KH[s][0:NOPE, :], G[1][0:NOPE, :], ACT.Copy).then_inc(S("mla_kc"), 1)
                    need(act, S("mla_v"), h + 1)
                    act.activation(VH[s][:].rearrange("p t n -> p (t n)"), M[1][:, 0:512], ACT.Copy)\
                       .then_inc(S("mla_kc"), 1)
                    for t in range(NT):
                        need(act, S("mla_smax"), h8 + (t + 1))
                        need(act, S("mla_tr"), h8 + (t - 1) if t else h8)
                        need(act, S("mla_rd"), h8)
                        act.activation(PR[t % 2][:, 0:(t + 1) * P], G[t % 2][:, 0:(t + 1) * P], ACT.Exp,
                                       bias=ROW["NB"][:, t:t + 1], scale=SCALE_M,
                                       accum_out=ROW["SUM"][:, t:t + 1]).then_inc(S("mla_exp"), 1)
            turns(act, MLA_HEADS // 2, pair)

        def mla_sp(sp):
            def pair(i):
                for s in range(2):
                    need(sp, S("mla_v"), i * 2)
                    h = i * 2 + s
                    sp.dma_start(MWQ[s][:], A["w_uq"][:, bass.ds(h * MLA_QK, MLA_QK)]
                                 .rearrange("(k p) n -> p k n", p=P)).then_inc(S(f"mla_w{s}"), 16)
                    sp.dma_start(MWK[s][:], A["w_ukv"][:, bass.ds(h * P, P)]).then_inc(S(f"mla_w{s}"), 16)
            turns(sp, MLA_HEADS // 2, pair)

        stage("mla", dict(act=mla_act, pe=mla_pe, dve=mla_dve, sp_gated=mla_sp))

        def turn_stage(tag, att, tile0, gate=None, tmp=None):
            tmp = tmp or T32

            def pe_(pe):
                for j in range(4):
                    if j >= 2:
                        pe.wait_ge(S(tag + "_out"), j - 1)
                    for t in range(NT):
                        m = pe.transpose(M[j % 2][:, t * P:(t + 1) * P], att[:, t, j * P:(j + 1) * P], IDENT[:])
                    m.then_inc(S(tag + "_tr"), 1)

            def dve_(dve):
                for j in range(4):
                    dve.wait_ge(S(tag + "_tr"), j + 1)
                    if j >= 2:
                        dve.wait_ge(S(tag + "_hi"), j - 1)
                        dve.wait_ge(S(tag + "_lo"), j - 1)
                    if gate is None:
                        dve.tensor_copy(tmp[j % 2][:], M[j % 2][:]).then_inc(S(tag + "_out"), 1)
                    else:
                        dve.tensor_tensor(tmp[j % 2][:], M[j % 2][:], gate[:, j, :], ALU.mult)\
                           .then_inc(S(tag + "_out"), 1)
                    dve.wait_ge(S(tag + "_hi"), j + 1)
                    dve.tensor_tensor(HL[:, tile0 + j, :], tmp[j % 2][:], HH[:, tile0 + j, :].bitcast(F32),
                                      ALU.subtract).then_inc(S(tag + "_lo"), 1)

            def act_(act):
                for j in range(4):
                    act.wait_ge(S(tag + "_out"), j + 1)
                    act.activation(HH[:, tile0 + j, :], tmp[j % 2][:], ACT.Copy).then_inc(S(tag + "_hi"), 1)
            stage(tag, dict(act=act_, pe=pe_, dve=dve_))

        turn_stage("mturn", ATT, 0)

        def add_gated(dve, U, f, T, X_, gate):
            unit_ready(dve, U)
            dve.scalar_tensor_tensor(out=X_[:, f, :T], in0=G[U % 2][:, :T], scalar=gate, in1=X_[:, f, :T],
                                     op0=ALU.mult, op1=ALU.add).then_inc(unit_freed[U % 2], 1)

        def out_stage(name, w, T, X_, gate):
            def dve_(dve):
                u0 = info(name)["u0"]
                for f in range(KT):
                    add_gated(dve, u0 + f, f, T, X_, gate(f))
            stage(name, dict(pe=lambda pe: gemm_pairs(pe, info(name)["u0"], 4, T, (HH, HL)), dve=dve_),
                  raw=[(4, cols(w, 0))], units=8)

        out_stage("wout", A["w_out"], SEQ, X, lambda f: MODA[:, 16 + f:17 + f])

        NSQ = [Z(f"NSQ{s}", [P, SEQ], F32, 4 * s) for s in range(2)]
        NR = Z("NR", [P, SEQ], F32, 8)

        def ones_sum(pe, dst, T, tiles, ready=None, used=None):
            nt = max(1, T // 512)
            w = T // nt
            for k in range(len(tiles)):
                if ready:
                    pe.wait_ge(ready, k + 1)
                for n in range(nt):
                    m = pe.matmul(dst[:, n * w:(n + 1) * w], ONES[:], tiles[k][:, n * w:(n + 1) * w],
                                  start=(k == 0), stop=(k == len(tiles) - 1))
                if used and k < len(tiles) - 1:
                    m.then_inc(used, 1)
            return m

        def norm_stage(tag, X_, T, mean, eps, finish_dve, finish_act, n_tiles=KT, sq=NSQ, r=NR):
            tiles = [X_[:, f, :T] for f in range(n_tiles)]
            width = n_tiles * P

            def pe_(pe):
                if mean:
                    ones_sum(pe, M[0], T, tiles).then_inc(S(tag + "_mean"), 1)
                ones_sum(pe, M[1], T, [sq[k % 2] for k in range(n_tiles)], ready=S(tag + "_sq"),
                         used=S(tag + "_squ")).then_inc(S(tag + "_var"), 1)

            def dve_(dve):
                if mean:
                    dve.wait_ge(S(tag + "_mean"), 1)
                    dve.tensor_scalar(r[:, :T], M[0][:, :T], -1.0 / width, None, ALU.mult).then_inc(S(tag + "_nm"), 1)
                    dve.wait_ge(S(tag + "_nm"), 1)
                    for f in range(n_tiles):
                        dve.tensor_tensor(tiles[f], tiles[f], r[:, :T], ALU.add).then_inc(S(tag + "_c"), 1)
                dve.wait_ge(S(tag + "_sd"), 1)
                dve.reciprocal(r[:, :T], r[:, :T]).then_inc(S(tag + "_r"), 1)
                dve.wait_ge(S(tag + "_r"), 1)
                finish_dve(dve, tag, r)

            def act_(act):
                for f in range(n_tiles):
                    if mean:
                        act.wait_ge(S(tag + "_c"), f + 1)
                    if f >= 2:
                        act.wait_ge(S(tag + "_squ"), f - 1)
                    act.activation(sq[f % 2][:, :T], tiles[f], ACT.Square).then_inc(S(tag + "_sq"), 1)
                act.wait_ge(S(tag + "_var"), 1)
                act.activation(r[:, :T], M[1][:, :T], ACT.Sqrt, bias=vec(eps), scale=1.0 / width)\
                   .then_inc(S(tag + "_sd"), 1)
                finish_act(act, tag)
            stage(tag, dict(act=act_, pe=pe_, dve=dve_))

        def ln_finish(g, b, scale=None, shift=None):
            def dve_(dve, tag, r):
                for f in range(KT + 1):
                    if f < KT:
                        dve.scalar_tensor_tensor(out=X[:, f, :], in0=X[:, f, :], scalar=vec(g, f), in1=r[:],
                                                 op0=ALU.mult, op1=ALU.mult).then_inc(S(tag + "_g"), 1)
                        dve.wait_ge(S(tag + "_g"), f + 1)
                        dve.tensor_scalar(X[:, f, :], X[:, f, :], vec(b, f), None, ALU.add).then_inc(S(tag + "_x"), 1)
                    if f and scale is not None:
                        h_low(dve, tag, f - 1, SEQ)
                        prescale(dve, tag, f - 1)

            def act_(act, tag):
                if scale is not None:
                    h_act(act, tag, S(tag + "_x"), SEQ, lambda f: X[:, f, :], scale, shift)
            return dve_, act_

        norm_stage("ln1", X, SEQ, True, "eps1", *ln_finish("ln1_g", "ln1_b", lambda f: MODA[:, 32 + f:33 + f],
                                                           lambda f: MODA[:, 24 + f:25 + f]))

        FH = Z("FH", [P, KT, SEQ], F32R, 0)
        FL = Z("FL", [P, KT, SEQ], F32R, 32)
        T2 = [Z(f"T2_{s}", [P, SEQ], F32, 64 + 4 * s) for s in range(2)]

        def ff_pe(pe):
            u0 = info("ff")["u0"]
            with pe.Fori(0, N_CHUNK) as c:
                for hid in (False, True):
                    for j in range(KT):
                        s = j % 2
                        pe.wait_ge(w_split[s], c * 8 + (u0 // 2 + (4 if hid else 0) + j // 2 + 1))
                        pe.wait_ge(unit_freed[s], c * 8 + (u0 // 2 + (4 if hid else 0) + j // 2))
                        hi, lo = (FH, FL) if hid else (HH, HL)
                        for k in range(KT):
                            if hid and j == 0:
                                pe.wait_ge(S("ff_lo"), c * 8 + (k + 2))
                            for part, moving in ((WH, hi), (WH, lo), (WL, hi)):
                                for n in range(2):
                                    m = pe.matmul(G[s][:, n * 512:(n + 1) * 512], part[s][:, k, :],
                                                  moving[:, k, n * 512:(n + 1) * 512],
                                                  start=(k == 0 and part is WH and moving is hi),
                                                  stop=(k == KT - 1 and part is WL))
                        m.then_inc(unit_done[s], 1)

        def ff_act(act):
            u0 = info("ff")["u0"]
            act.sem_inc(S("ff_sq"), 1)
            with act.Fori(0, N_CHUNK) as c:
                for j in range(KT):
                    s = j % 2
                    act.wait_ge(unit_done[s], c * 8 + (u0 // 2 + j // 2 + 1))
                    act.wait_ge(S("ff_sq"), c * 8 + (max(j - 1, 0) + 1))
                    act.activation(T2[s][:], G[s][:], ACT.Relu).then_inc(unit_freed[s], 1)
                    act.wait_ge(unit_freed[s], c * 8 + (u0 // 2 + j // 2 + 1))
                    act.wait_ge(S("ff_lo"), c * 8 + (max(j - 1, 0) + 1))
                    act.activation(T32[s][:], T2[s][:], ACT.Square).then_inc(S("ff_sq"), 1)
                    act.wait_ge(S("ff_sq"), c * 8 + (j + 2))
                    act.activation(FH[:, j, :], T32[s][:], ACT.Copy).then_inc(S("ff_hi"), 1)

        def ff_dve(dve):
            u0 = info("ff")["u0"]
            dve.sem_inc(S("ff_lo"), 1)
            with dve.Fori(0, N_CHUNK) as c:
                for j in range(KT):
                    dve.wait_ge(S("ff_hi"), c * 8 + (j + 1))
                    dve.tensor_tensor(FL[:, j, :], T32[j % 2][:], FH[:, j, :].bitcast(F32),
                                      ALU.subtract).then_inc(S("ff_lo"), 1)
                for f in range(KT):
                    s = f % 2
                    dve.wait_ge(unit_done[s], c * 8 + (u0 // 2 + 4 + f // 2 + 1))
                    dve.wait_ge(unit_freed[s], c * 8 + (u0 // 2 + 4 + f // 2))
                    dve.scalar_tensor_tensor(out=X[:, f, :], in0=G[s][:], scalar=MODA[:, 40 + f:41 + f],
                                             in1=X[:, f, :], op0=ALU.mult, op1=ALU.add).then_inc(unit_freed[s], 1)

        def ff_sp(sp, r0):
            with sp.Fori(0, N_CHUNK) as c:
                for j in range(KT):
                    load_unit(sp, c * 8 + (r0 // 2 + j // 2), j % 2,
                              A["w_ff1"][:, bass.ds(c * D + j * P, P)].rearrange("(k p) n -> p k n", p=P),
                              RAW[j % 2][:])
                for f in range(KT):
                    load_unit(sp, c * 8 + (r0 // 2 + 4 + f // 2), f % 2,
                              A["w_ff2"][bass.ds(c * D, D), f * P:(f + 1) * P].rearrange("(k p) n -> p k n", p=P),
                              RAW[f % 2][:])

        stage("ff", dict(act=ff_act, pe=ff_pe, dve=ff_dve, sp_free=ff_sp), raw=[(8 * N_CHUNK, None)],
              units=16 * N_CHUNK)
        norm_stage("ln2", X, SEQ, True, "eps1", *ln_finish("ln2_g", "ln2_b"))

        def rms_h(tag, X_, T, layer, c):
            mod = (MODE, MODO)[layer]
            XN = [Z(f"XN{tag}{s}", [P, T], F32, 12 + 4 * s) for s in range(2)]

            def dve_(dve, tag, r):
                for f in range(KT + 1):
                    if f < KT:
                        if f >= 2:
                            dve.wait_ge(S(tag + "_t32"), f - 1)
                        dve.tensor_tensor(XN[f % 2][:], X_[:, f, :T], r[:, :T], ALU.mult).then_inc(S(tag + "_xn"), 1)
                    if f:
                        h_low(dve, tag, f - 1, T)

            def act_(act, tag):
                h_act(act, tag, S(tag + "_xn"), T, lambda f: XN[f % 2][:], lambda f: GS[:, layer, f, c:c + 1],
                      lambda f: mod[:, f, c:c + 1])
            norm_stage(tag, X_, T, False, "eps2", dve_, act_)

        def even_layer(tag, X_, T, c):
            rms_h(tag + "n", X_, T, 0, c)
            w = T + 2 * PAD
            U = Z(tag + "U", [P, 4, w], F32, 0)
            GA = Z(tag + "GA", [P, 4, T], F32, 17)
            VB = Z(tag + "VB", [P, 4, T], F32, 33)
            GB = Z(tag + "GB", [P, 4, T], F32, 49)
            ACC = Z(tag + "ACC", [P, T], F32, 65)
            SG = [Z(f"{tag}SG{s}", [P, T], F32, 69 + 3.5 * 0 + 4 * s) for s in range(1)]
            name = tag + "in"
            unit_cols = [x for j in range(4) for x in (512 + P * j, P * j)] + \
                [1536 + P * j for j in range(4)] + [2048 + P * j for j in range(4)] + [1024 + P * j for j in range(4)]

            def conv(dve, a, b):
                for q in range(a, b):
                    j, k = divmod(q, CONV_W)
                    src, wk = U[:, j, k:k + T], V[:, VEC["conv_w"] + j * CONV_W + k:VEC["conv_w"] + j * CONV_W + k + 1]
                    if q:
                        dve.wait_ge(S(name + "_tap"), q)
                    if k == 0:
                        dve.wait_ge(S(name + "_u"), 1 + j + 1)
                        if j:
                            dve.wait_ge(S(name + "_cv"), j)
                        dve.tensor_scalar(ACC[:], src, wk, vec("conv_b", j), ALU.mult, ALU.add)\
                           .then_inc(S(name + "_tap"), 1)
                    else:
                        dve.scalar_tensor_tensor(out=ACC[:], in0=src, scalar=wk, in1=ACC[:], op0=ALU.mult,
                                                 op1=ALU.add).then_inc(S(name + "_tap"), 1)
                    if k == CONV_W - 1:
                        dve.wait_ge(S(name + "_tap"), q + 1)
                        dve.tensor_copy(U[:, j, 0:T], ACC[:]).then_inc(S(name + "_cv"), 1)

            def in_dve(dve):
                u0 = info(name)["u0"]
                dve.memset(U[:, :, 0:PAD], 0.0).then_inc(S(name + "_pad"), 1)
                dve.memset(U[:, :, PAD + T:w], 0.0).then_inc(S(name + "_u"), 1)
                step = 0
                for j in range(4):
                    unit_ready(dve, u0 + 2 * j + 1)
                    dve.wait_ge(unit_freed[0], u0 // 2 + j + 1)
                    dve.tensor_tensor(U[:, j, PAD:PAD + T], G[1][:, :T], SG[0][:], ALU.mult)\
                       .then_inc(S(name + "_u"), 1)
                    dve.wait_ge(S(name + "_u"), j + 2)
                    dve.sem_inc(unit_freed[1], 1)
                    if j < 3:
                        conv(dve, step, step + 12)
                        step += 12
                conv(dve, step, 4 * CONV_W)

            def in_act(act):
                u0 = info(name)["u0"]
                for j in range(4):
                    unit_ready(act, u0 + 2 * j)
                    if j:
                        act.wait_ge(S(name + "_u"), j + 1)
                    act.activation(SG[0][:], G[0][:, :T], ACT.Sigmoid).then_inc(unit_freed[0], 1)
                for j in range(12):
                    U_ = u0 + 8 + j
                    unit_ready(act, U_)
                    dst = (VB, GB, GA)[j // 4][:, j % 4, :]
                    act.activation(dst, G[U_ % 2][:, :T], ACT.Copy if j < 4 else ACT.Silu)\
                       .then_inc(unit_freed[U_ % 2], 1)

            def unit_src(j):
                return A["e_w_in"][:, unit_cols[j]:unit_cols[j] + P].rearrange("(k p) n -> p k n", p=P)
            stage(name, dict(act=in_act, pe=lambda pe: gemm_pairs(pe, info(name)["u0"], 10, T, (HH, HL)), dve=in_dve),
                  raw=[(1, lambda s, i, j=j: unit_src(2 * j + s)) for j in range(10)], units=20)

            n_tok = T // P
            half = T // 2
            VP = Z(tag + "VP", [P, n_tok, 512], F32, 80)
            VQ = Z(tag + "VQ", [P, n_tok, 512], F32, 112)
            FW = Z(tag + "FW", [P, 4, P], F32, 96)
            DFTD = Z(tag + "DFTD", [P, 256], F32, 98)
            PQ = Z(tag + "PQ", [P, 4, 2, P], F32, 99)
            EV = [Z(f"{tag}EV{s}", [P, half], F32, 69 + 2 * s) for s in range(2)]
            YB = Z(tag + "YB", [P, T], F32, 73)
            fn = tag + "fo"
            banks = [[G[j // 2][:, 512 * (j % 2):512 * (j % 2) + half] for j in range(4)],
                     [M[j // 2][:, 512 * (j % 2):512 * (j % 2) + half] for j in range(4)]]

            def fo_pe(pe):
                pe.wait_ge(moved, info(fn)["dma_end"])
                for q in range(2):
                    for g in range(4):
                        m = pe.matmul(M[q][:, g * P:(g + 1) * P], DFTD[:, q * P:(q + 1) * P], FW[:, g, :], start=True,
                                      stop=True)
                m.then_inc(S(fn + "_pq"), 1)
                pe.wait_ge(S(fn + "_pqs"), 2)
                for t in range(n_tok):
                    par, i = divmod(t, n_tok // 2)
                    if t >= 2:
                        pe.wait_ge(S(fn + "_v"), 2 * (t - 1))
                    first = 2 * P * i + par
                    for g in range(4):
                        m = pe.matmul(G[t % 2][:, g * 256:(g + 1) * 256], VB[:, g, first:first + 2 * P - 1:2],
                                      PQ[:, g, :, :].rearrange("p a b -> p (a b)"), start=True, stop=True)
                    m.then_inc(S(fn + "_vp"), 1)
                pe.wait_ge(S(fn + "_v"), 2 * n_tok)
                r0 = info(fn)["r0"]
                for t in range(n_tok):
                    par, i = divmod(t, n_tok // 2)
                    pe.wait_ge(raw_loaded[t % 2], 16 * ((r0 + t) // 2 + 1))
                    tab = RAW[t % 2][:].rearrange("p k n -> p (k n)")
                    for g in range(4):
                        for q, vv in enumerate((VP, VQ)):
                            m = pe.matmul(banks[par][g], vv[:, t, g * P:(g + 1) * P],
                                          tab[:, q * half:(q + 1) * half], start=(i == 0 and q == 0),
                                          stop=(i == n_tok // 2 - 1 and q == 1))
                    m.then_inc(raw_used[t % 2], 1)

            def fo_act(act):
                act.wait_ge(S(fn + "_pq"), 1)
                for q in range(2):
                    act.activation(PQ[:, :, q, :], M[q][:, 0:512].rearrange("p (g n) -> p g n", n=P), ACT.Copy,
                                   scale=float(T) ** -0.5).then_inc(S(fn + "_pqs"), 1)
                r0 = info(fn)["r0"]
                for s in range(2):
                    act.wait_ge(raw_used[s], (r0 + n_tok) // 2)
                for g in range(4):
                    if g >= 2:
                        act.wait_ge(S(fn + "_y"), 2 * (g - 1))
                    act.activation(EV[g % 2][:], banks[0][g], ACT.Copy).then_inc(S(fn + "_ev"), 1)
                    act.wait_ge(S(fn + "_gate"), g + 1)
                    act.activation(HH[:, 4 + g, :T], YB[:], ACT.Copy).then_inc(S(fn + "_hi"), 1)

            def fo_dve(dve):
                for t in range(n_tok):
                    dve.wait_ge(S(fn + "_vp"), t + 1)
                    both = G[t % 2][:].rearrange("p (g q n) -> p g q n", g=4, q=2)
                    for q, vv in enumerate((VP, VQ)):
                        dve.tensor_copy(vv[:, t, :].rearrange("p (g n) -> p g n", n=P), both[:, :, q, :])\
                           .then_inc(S(fn + "_v"), 1)
                r0 = info(fn)["r0"]
                for s in range(2):
                    dve.wait_ge(raw_used[s], (r0 + n_tok) // 2)
                for g in range(4):
                    dve.wait_ge(S(fn + "_ev"), g + 1)
                    if g:
                        dve.wait_ge(S(fn + "_lo"), g)
                    dve.tensor_tensor(YB[:, 0:half], banks[1][g], EV[g % 2][:], ALU.add).then_inc(S(fn + "_y"), 1)
                    dve.scalar_tensor_tensor(out=YB[:, half:T], in0=banks[1][g], scalar=-1.0, in1=EV[g % 2][:],
                                             op0=ALU.mult, op1=ALU.add).then_inc(S(fn + "_y"), 1)
                    dve.wait_ge(S(fn + "_y"), 2 * g + 2)
                    dve.tensor_tensor(YB[:], YB[:], GB[:, g, :], ALU.mult).then_inc(S(fn + "_gate"), 1)
                    dve.wait_ge(S(fn + "_hi"), g + 1)
                    dve.tensor_tensor(HL[:, 4 + g, :T], YB[:], HH[:, 4 + g, :T].bitcast(F32),
                                      ALU.subtract).then_inc(S(fn + "_lo"), 1)

            def dft_unit(t):
                return A[f"dft_{T}"][t * P:(t + 1) * P, :]

            def fo_sp(sp, r0):
                for t in range(n_tok):
                    load_unit(sp, (r0 + t) // 2, t % 2, dft_unit(t),
                              RAW[t % 2][:].rearrange("p k n -> p (k n)")[:, 0:T])
            stage(fn, dict(act=fo_act, pe=fo_pe, dve=fo_dve, sp_free=fo_sp), raw=[(n_tok // 2, None)],
                  dmas=[(FW[:], A["e_b_fw"].rearrange("g d e -> d g e")), (DFTD[:], A["dft_d"])])

            def ln_dve(dve, t_, r):
                for j in range(4):
                    dve.tensor_tensor(U[:, j, 0:T], U[:, j, 0:T], r[:, :T], ALU.mult).then_inc(S(t_ + "_xn"), 1)

            def ln_act(act, t_):
                for j in range(4):
                    act.wait_ge(S(t_ + "_xn"), j + 1)
                    act.activation(U[:, j, 0:T], U[:, j, 0:T], ACT.Silu, bias=vec("a_ln_b", j),
                                   scale=vec("a_ln_g", j)).then_inc(S(t_ + "_s"), 1)
            norm_stage(tag + "an", U, T, True, "eps2", ln_dve, ln_act, n_tiles=4,
                       sq=[Z(f"{tag}ASQ{s}", [P, T], F32, 33 + 4 * s) for s in range(2)],
                       r=Z(tag + "AR", [P, T], F32, 41))
            pn = tag + "pw"
            nt = max(1, T // 512)
            cw = T // nt

            def pw_pe(pe):
                r0 = info(pn)["r0"]
                for j in range(4):
                    pe.wait_ge(raw_loaded[j % 2], 16 * ((r0 + j) // 2 + 1))
                    if j >= 2:
                        pe.wait_ge(S(pn + "_g"), j - 1)
                    for k in range(4):
                        for n in range(nt):
                            m = pe.matmul(G[j % 2][:, n * cw:(n + 1) * cw], RAW[j % 2][:, k, :],
                                          U[:, k, n * cw:(n + 1) * cw], start=(k == 0), stop=(k == 3))
                    m.then_inc(raw_used[j % 2], 1)

            def pw_dve(dve):
                r0 = info(pn)["r0"]
                for j in range(4):
                    dve.wait_ge(raw_used[j % 2], (r0 + j) // 2 + 1)
                    dve.scalar_tensor_tensor(out=GA[:, j, :], in0=G[j % 2][:, :T], scalar=vec("pw_b", j),
                                             in1=GA[:, j, :], op0=ALU.add, op1=ALU.mult).then_inc(S(pn + "_g"), 1)
                    dve.wait_ge(S(pn + "_hi"), j + 1)
                    dve.tensor_tensor(HL[:, j, :T], GA[:, j, :], HH[:, j, :T].bitcast(F32),
                                      ALU.subtract).then_inc(S(pn + "_lo"), 1)

            def pw_act(act):
                for j in range(4):
                    act.wait_ge(S(pn + "_g"), j + 1)
                    act.activation(HH[:, j, :T], GA[:, j, :], ACT.Copy).then_inc(S(pn + "_hi"), 1)

            def pw_sp(sp, r0):
                for j in range(4):
                    load_unit(sp, (r0 + j) // 2, j % 2,
                              A["e_a_pw_w"][:, j * P:(j + 1) * P].rearrange("(k p) n -> p k n", p=P),
                              RAW[j % 2][:, 0:4, :])
            stage(pn, dict(act=pw_act, pe=pw_pe, dve=pw_dve, sp_free=pw_sp), raw=[(2, None)])
            out_stage(tag + "out", A["e_w_out"], T, X_, lambda f: MODE[:, 16 + f, c:c + 1])

        XC = Z("XC", [P, KT, CTX], F32, 22)
        CT = Z("CT", [P, 2, D], F32, 0)

        def cin_pe(pe):
            pe.wait_ge(moved, info("cin")["dma_end"])
            for q in range(4):
                if q >= 2:
                    pe.wait_ge(S("cin_x"), q - 1)
                for f in range(2 * q, 2 * q + 2):
                    for t in range(2):
                        m = pe.transpose(M[q % 2][:, 256 * (f % 2) + t * P:256 * (f % 2) + (t + 1) * P],
                                         CT[:, t, f * P:(f + 1) * P], IDENT[:])
                m.then_inc(S("cin_tr"), 1)

        def cin_dve(dve):
            for q in range(4):
                dve.wait_ge(S("cin_tr"), q + 1)
                dve.tensor_copy(XC[:, 2 * q:2 * q + 2, :].rearrange("p a b -> p (a b)"), M[q % 2][:, 0:512])\
                   .then_inc(S("cin_x"), 1)

        stage("cin", dict(pe=cin_pe, dve=cin_dve), dmas=[(CT[:, t, :], A["ctx"][t * P:(t + 1) * P, :]) for t in range(2)])

        O_Q, O_K, O_V, O_AG = 2048, 2560, 2688, 2816
        even_layer("c", XC, CTX, 1)
        rms_h("ckn", XC, CTX, 1, 1)
        CV = Z("CV", [P, CTX], F32, 0)

        def ckv_act(act):
            u0 = info("ckv")["u0"]
            for j, dst in enumerate((KC, CV)):
                unit_ready(act, u0 + j)
                act.activation(dst[:], G[j][:, 0:CTX], ACT.Copy).then_inc(unit_freed[j], 1)
            act.wait_ge(S("ckv_tr"), 1)
            act.activation(VC[:].rearrange("p a b -> p (a b)"), M[0][:, 0:CTX], ACT.Copy).then_inc(S("ckv_v"), 1)

        def ckv_pe(pe):
            u0 = info("ckv")["u0"]
            gemm_pairs(pe, u0, 1, CTX, (HH, HL))
            pe.wait_ge(unit_freed[1], u0 // 2 + 1)
            for t in range(2):
                m = pe.transpose(M[0][:, t * P:(t + 1) * P], CV[:, t * P:(t + 1) * P], IDENT[:])
            m.then_inc(S("ckv_tr"), 1)

        stage("ckv", dict(act=ckv_act, pe=ckv_pe), raw=[(1, cols(A["o_w_in"], O_K))], units=2)

        even_layer("e", X, SEQ, 0)

        rms_h("on", X, SEQ, 1, 0)
        SX = Z("SX", [P, 4, SEQ + 2], F32, 0)
        CB = Z("CB", [P, 4, SEQ], F32, 16.25)
        OQ = Z("OQ", [P, 4, SEQ], F32, 32.25)
        OK = Z("OK", [P, SEQ], F32, 48.25)
        OV = Z("OV", [P, SEQ], F32, 52.25)
        AG = Z("AG", [P, 4, SEQ], F32, 56.25)
        TG = Z("TG", [P, SEQ], F32, 72.25)
        odd_units = [("s", c0 + P * j) for j in range(4) for c0 in (512, 1024)] + \
            [("b", c0 + P * j) for j in range(4) for c0 in (1536, 0)] + \
            [("q", O_Q + HEAD * j) for j in range(4)] + [("k", O_K), ("v", O_V)] + \
            [("g", O_AG + P * j) for j in range(4)]

        def odd_unit(j):
            kind, c0 = odd_units[j]
            w = A["o_w_in"]
            return w[:, c0:c0 + P].rearrange("(k p) n -> p k n", p=P)

        def odd_act(act):
            u0 = info("odd")["u0"]
            for j in range(26):
                kind = odd_units[j][0]
                if j < 16 and j % 2:
                    continue
                unit_ready(act, u0 + j)
                if j < 16:
                    if j:
                        act.wait_ge(S("odd_p"), j // 2)
                    act.activation(TG[:], G[0][:], ACT.Copy if kind == "s" else ACT.Silu).then_inc(unit_freed[0], 1)
                elif j < 22:
                    dst = OQ[:, j - 16, :] if j < 20 else (OK, OV)[j - 20][:]
                    act.activation(dst, G[j % 2][:], ACT.Copy).then_inc(unit_freed[j % 2], 1)
                else:
                    act.activation(AG[:, j - 22, :], G[j % 2][:], ACT.Silu).then_inc(unit_freed[j % 2], 1)

        def odd_dve(dve):
            u0 = info("odd")["u0"]
            dve.memset(SX[:, :, 0:1], 0.0).then_inc(S("odd_z"), 1)
            dve.memset(SX[:, :, SEQ + 1:SEQ + 2], 0.0).then_inc(S("odd_z"), 1)
            for j in range(8):
                unit_ready(dve, u0 + 2 * j + 1)
                dve.wait_ge(unit_freed[0], u0 // 2 + j + 1)
                dst = SX[:, j, 1:SEQ + 1] if j < 4 else CB[:, j - 4, :]
                dve.tensor_tensor(dst, G[1][:], TG[:], ALU.mult).then_inc(S("odd_p"), 1)
                dve.wait_ge(S("odd_p"), j + 1)
                dve.sem_inc(unit_freed[1], 1)

        def odd_sp(sp, r0):
            for j in range(26):
                view = RAW[j % 2][:]
                kind, c0 = odd_units[j]
                if kind == "q":
                    sp.wait_ge(raw_used[j % 2], (r0 + j) // 2)
                    sp.dma_start(view[:, :, 0:HEAD], A["o_w_in"][:, c0:c0 + HEAD].rearrange("(k p) n -> p k n", p=P))\
                      .then_inc(q_half, 16)
                    sp.wait_ge(q_half, 16 * (j - 15))
                    c0 += 4 * HEAD
                    sp.dma_start(view[:, :, HEAD:P], A["o_w_in"][:, c0:c0 + HEAD].rearrange("(k p) n -> p k n", p=P))\
                      .then_inc(raw_loaded[j % 2], 16)
                else:
                    load_unit(sp, (r0 + j) // 2, j % 2, odd_unit(j), view)

        stage("odd", dict(act=odd_act, pe=lambda pe: gemm_pairs(pe, info("odd")["u0"], 13, SEQ, (HH, HL)),
                          dve=odd_dve, sp_free=odd_sp), raw=[(13, None)], units=26)

        WC, WS = Z("WC", [P, SEQ], F32, 96), Z("WS", [P, SEQ], F32, 100)
        OTMP = Z("OTMP", [P, SEQ], F32, 104)
        SWAPW = Z("SWAPW", [P, P], F32, 108)
        WVT = Z("WVT", [P, NT, P], F32, 128)
        YC = [Z(f"YC{s}", [P, SEQ], F32, 132 + 4 * s) for s in range(2)]

        def opre_pe(pe):
            pe.wait_ge(moved, info("opre")["dma_end"])
            for i in range(5):
                swap_pe(pe, "or", i, OQ[:, i, :] if i < 4 else OK[:], SWAPW[:])
            pe.wait_ge(S("or_mul"), 4)
            for t in range(NT):
                m = pe.transpose(M[1][:, t * P:(t + 1) * P], OV[:, t * P:(t + 1) * P], IDENT[:])
            m.then_inc(S("ov_tr"), 1)

        def opre_dve(dve):
            for i in range(5):
                rope_dve(dve, "or", i, OQ[:, i, :] if i < 4 else OK[:], WC[:], WS[:], OTMP[:])
            for j in range(4):
                y = YC[j % 2][:]
                wk = [V[:, VEC["c_conv"] + 3 * j + k:VEC["c_conv"] + 3 * j + k + 1] for k in range(3)]
                if j >= 2:
                    dve.wait_ge(S("oc_lo"), j - 1)
                dve.tensor_scalar(y, SX[:, j, 0:SEQ], wk[0], None, ALU.mult).then_inc(S("oc_t"), 1)
                for k in (1, 2):
                    dve.wait_ge(S("oc_t"), 3 * j + k)
                    dve.scalar_tensor_tensor(out=y, in0=SX[:, j, k:k + SEQ], scalar=wk[k], in1=y, op0=ALU.mult,
                                             op1=ALU.add).then_inc(S("oc_t"), 1)
                dve.wait_ge(S("oc_t"), 3 * j + 3)
                dve.tensor_tensor(y, y, CB[:, j, :], ALU.mult).then_inc(S("oc_y"), 1)
                dve.wait_ge(S("oc_hi"), j + 1)
                dve.tensor_tensor(HL[:, j, :], y, HH[:, j, :].bitcast(F32), ALU.subtract).then_inc(S("oc_lo"), 1)

        def opre_act(act):
            act.wait_ge(S("ov_tr"), 1)
            act.activation(WVT[:].rearrange("p t n -> p (t n)"), M[1][:], ACT.Copy).then_inc(S("ov_out"), 1)
            for j in range(4):
                act.wait_ge(S("oc_y"), j + 1)
                act.activation(HH[:, j, :], YC[j % 2][:], ACT.Copy).then_inc(S("oc_hi"), 1)

        stage("opre", dict(act=opre_act, pe=opre_pe, dve=opre_dve),
              dmas=[(WC[:], A["cos_win"]), (WS[:], A["sin_win"]), (SWAPW[:], A["swap_win"])])

        WATT = Z("WATT", [P, NT, 512], F32, 0)
        WP = [Z(f"WP{s}", [P, 640], F32, 16.25 + 2.5 * s) for s in range(2)]
        WPT = [Z(f"WPT{s}", [P, 640], F32, 21.25 + 2.5 * s) for s in range(2)]
        SCALE_W = HEAD ** -0.5
        steps = [(n, h) for n in range(NT) for h in range(N_Q)]

        def span(n):
            return list(range(max(n - 1, 0), min(n + 2, NT)))

        def wa_pe(pe):
            def scores(i):
                n, h = steps[i]
                g, j = divmod(h, 4)
                r = slice(64 * g, 64 * g + 64)
                q = OQ[r, j, n * P:(n + 1) * P]
                blocks = span(n)
                a = 512 - P * len(blocks)
                ps = G[i % 2]
                if i >= 2:
                    pe.wait_ge(S("wa_exp"), i - 1)
                pe.matmul(ps[:, a:512], q, OK[r, blocks[0] * P:(blocks[-1] + 1) * P], start=True, stop=False)
                if n > 0:
                    pe.matmul(ps[:, a:a + P], identb, before, start=False, stop=(n == NT - 1))
                if n < NT - 1:
                    pe.matmul(ps[:, 512 - P:512], identb, causal, start=False, stop=True)
                pe.matmul(ps[:, 512:768], q, KC[r, :], start=True, stop=True).then_inc(S("wa_sc"), 1)

            def turn(i):
                n, h = steps[i]
                nb = len(span(n)) + 2
                pe.wait_ge(S("wa_exp"), i + 1)
                if i:
                    pe.wait_ge(S("wa_pt"), i)
                for b in range(nb):
                    m = pe.transpose(M[0][:, b * P:(b + 1) * P], WP[i % 2][:, b * P:(b + 1) * P], IDENT[:])
                m.then_inc(S("wa_tr"), 1)

            def values(i):
                n, h = steps[i]
                g = h // 4
                blocks = span(n)
                pe.wait_ge(S("wa_pt"), i + 1)
                if i >= 2:
                    pe.wait_ge(S("wa_att"), i - 1)
                for b in range(len(blocks) + 2):
                    v = WVT[:, blocks[b], 64 * g:64 * g + 64] if b < len(blocks) else \
                        VC[:, b - len(blocks), 64 * g:64 * g + 64]
                    m = pe.matmul(M[1][:, 512 * (i % 2):512 * (i % 2) + 64], WPT[i % 2][:, b * P:(b + 1) * P], v,
                                  start=(b == 0), stop=(b == len(blocks) + 1))
                m.then_inc(S("wa_pv"), 1)
            scores(0)
            for i in range(len(steps)):
                if i + 1 < len(steps):
                    scores(i + 1)
                if i:
                    values(i - 1)
                turn(i)
            values(len(steps) - 1)

        NMX, NB, SUM, RDEN, ESINK = (ROW[n] for n in ("NMX", "NB", "SUM", "RDEN", "ESINK"))

        def wa_dve(dve):
            def smax(i):
                n, h = steps[i]
                a = 512 - P * len(span(n))
                c = i % 8
                dve.wait_ge(S("wa_sc"), i + 1)
                if i >= 8:
                    dve.wait_ge(S("wa_es"), i - 7)
                dve.tensor_reduce(NMX[:, c:c + 1], G[i % 2][:, a:768], AX.X, ALU.max).then_inc(S("wa_mx"), 1)
                dve.wait_ge(S("wa_mx"), 2 * i + 1)
                dve.tensor_scalar(NMX[:, c:c + 1], NMX[:, c:c + 1], SCALE_W, vec("sink", h), ALU.mult, ALU.max)\
                   .then_inc(S("wa_mx"), 1)
                dve.wait_ge(S("wa_mx"), 2 * i + 2)
                dve.tensor_scalar(NB[:, c:c + 1], NMX[:, c:c + 1], -1.0, None, ALU.mult).then_inc(S("wa_nb"), 1)

            def tail(i):
                n, h = steps[i]
                w = (len(span(n)) + 2) * P
                c = i % 8
                dve.wait_ge(S("wa_tr"), i + 1)
                if i >= 2:
                    dve.wait_ge(S("wa_pv"), i - 1)
                dve.tensor_copy(WPT[i % 2][:, 0:w], M[0][:, 0:w]).then_inc(S("wa_pt"), 1)
                dve.wait_ge(S("wa_es"), i + 1)
                dve.tensor_tensor(SUM[:, c:c + 1], SUM[:, c:c + 1], ESINK[:, c:c + 1], ALU.add).then_inc(S("wa_den"), 1)
                dve.wait_ge(S("wa_den"), 2 * i + 1)
                dve.reciprocal(RDEN[:, c:c + 1], SUM[:, c:c + 1]).then_inc(S("wa_den"), 1)

            def put(i):
                n, h = steps[i]
                c = i % 8
                dve.wait_ge(S("wa_pv"), i + 1)
                dve.wait_ge(S("wa_den"), 2 * i + 2)
                dve.tensor_scalar(WATT[:, n, h * HEAD:(h + 1) * HEAD], M[1][:, 512 * (i % 2):512 * (i % 2) + 64],
                                  RDEN[:, c:c + 1], None, ALU.mult).then_inc(S("wa_att"), 1)
            smax(0)
            for i in range(len(steps)):
                if i + 1 < len(steps):
                    smax(i + 1)
                if i:
                    put(i - 1)
                tail(i)
            put(len(steps) - 1)

        def wa_act(act):
            for i in range(len(steps)):
                n, h = steps[i]
                w = (len(span(n)) + 2) * P
                c = i % 8
                act.wait_ge(S("wa_nb"), i + 1)
                if i >= 2:
                    act.wait_ge(S("wa_tr"), i - 1)
                if i >= 8:
                    act.wait_ge(S("wa_den"), 2 * (i - 7))
                act.activation(WP[i % 2][:, 0:w], G[i % 2][:, 768 - w:768], ACT.Exp, bias=NB[:, c:c + 1],
                               scale=SCALE_W, accum_out=SUM[:, c:c + 1]).then_inc(S("wa_exp"), 1)
                act.activation(ESINK[:, c:c + 1], vec("sink", h), ACT.Exp, bias=NB[:, c:c + 1],
                               scale=1.0).then_inc(S("wa_es"), 1)

        stage("wa", dict(act=wa_act, pe=wa_pe, dve=wa_dve))
        turn_stage("oturn", WATT, 4, gate=AG, tmp=[Z(f"OT{s}", [P, SEQ], F32, 16.25 + 4 * s) for s in range(2)])
        out_stage("oout", A["o_w_out"], SEQ, X, lambda f: MODO[:, 16 + f, 0:1])

        OT = [Z(f"OUT{s}", [P, D], F32, 16 + 4 * s) for s in range(2)]

        def fin_dve(dve, tag, r):
            for f in range(KT):
                dve.scalar_tensor_tensor(out=X[:, f, :], in0=X[:, f, :], scalar=vec("final", f), in1=r[:],
                                         op0=ALU.mult, op1=ALU.mult).then_inc(S("fin_x"), 1)
        norm_stage("fin", X, SEQ, False, "eps2", fin_dve, lambda act, tag: None)

        def st_pe(pe):
            for t in range(NT):
                if t >= 2:
                    pe.wait_ge(S("st_o"), t - 1)
                for f in range(KT):
                    m = pe.transpose(M[t % 2][:, f * P:(f + 1) * P], X[:, f, t * P:(t + 1) * P], IDENT[:])
                m.then_inc(S("st_tr"), 1)

        def st_dve(dve):
            for t in range(NT):
                dve.wait_ge(S("st_tr"), t + 1)
                if t >= 2:
                    dve.wait_ge(S(f"stored{t % 2}"), 16 * (t // 2))
                dve.tensor_copy(OT[t % 2][:], M[t % 2][:]).then_inc(S("st_o"), 1)

        def st_act(act):
            for t in range(NT):
                act.wait_ge(S("st_o"), t + 1)
                act.dma_start(out[t * P:(t + 1) * P, :], OT[t % 2][:]).then_inc(S(f"stored{t % 2}"), 16)
            for s in range(2):
                act.wait_ge(S(f"stored{s}"), 16 * (NT // 2))

        stage("store", dict(act=st_act, pe=st_pe, dve=st_dve))

        block = ctx.enter_context(nc.Block())

        def gate(eng, n):
            for k in left:
                eng.wait_ge(left[k], n)

        def walk(eng, key):
            for n, st in enumerate(stages):
                current[0] = n
                if n:
                    gate(eng, n)
                    if key == "dve":
                        first = banks_of_signals[(n - 1) % 2][0].num
                        eng.sem_clear(range(first, first + BANK))
                if key in st["progs"]:
                    st["progs"][key](eng)
                eng.drain().then_inc(left[key], 1)

        @block.sync
        def _(sp):
            for n, st in enumerate(stages):
                current[0] = n
                if "sp_gated" in st["progs"]:
                    gate(sp, n)
                    st["progs"]["sp_gated"](sp)
                if "sp_free" in st["progs"]:
                    st["progs"]["sp_free"](sp, st["r0"])
                    continue
                r = st["r0"]
                for n_pairs, src in st["raw"]:
                    if n_pairs == 1:
                        for s in range(2):
                            load_unit(sp, r // 2, s, src(s, 0), RAW[s][:])
                    else:
                        def pair(i, r=r, src=src):
                            for s in range(2):
                                load_unit(sp, i + r // 2, s, src(s, i), RAW[s][:])
                        turns(sp, n_pairs, pair)
                    r += 2 * n_pairs

        @block.gpsimd
        def _(pool):
            for n, st in enumerate(stages):
                current[0] = n
                if st["dmas"]:
                    if n:
                        gate(pool, n)
                    for dst, src in st["dmas"]:
                        pool.dma_start(dst, src).then_inc(moved, 16)
                if st["units"]:
                    split_pairs(pool, st["r0"], st["u0"], st["units"] // 2)

        @block.scalar
        def _(act):
            walk(act, "act")

        @block.vector
        def _(dve):
            walk(dve, "dve")

        @block.tensor
        def _(pe):
            walk(pe, "pe")


def kernel(**inputs):
    import concourse.bacc as _bacc
    from concourse.bass_utils import run_bass_kernel_spmd as _run

    def tiles(a):
        a = np.asarray(a)
        return np.ascontiguousarray(a.reshape(-1, P).T)

    g = {k: np.asarray(v) for k, v in inputs.items()}
    const = shape_constants()
    two = np.stack([tiles(g["c_2"]), tiles(g["c_ctx_2"])], 2).reshape(P, 16)
    taps = lambda w: np.ascontiguousarray(w[0].reshape(w.shape[1], 4, P).transpose(2, 1, 0).reshape(P, -1))
    parts = {
        "c": tiles(g["c"]), "c2": two, "ln_in_g": tiles(g["ln_in_g"]), "ln_in_b": tiles(g["ln_in_b"]),
        "ln1_g": tiles(g["ln1_g"]), "ln1_b": tiles(g["ln1_b"]), "ln2_g": tiles(g["ln2_g"]),
        "ln2_b": tiles(g["ln2_b"]), "e_norm": tiles(g["e_norm_2"]), "o_norm": tiles(g["o_norm_2"]),
        "final": tiles(g["final_norm_2"]), "b_ada": tiles(g["b_ada"]), "e_b": tiles(g["e_b_mod_2"]),
        "o_b": tiles(g["o_b_mod_2"]), "q_norm": tiles(g["mla_q_norm"]), "kv_norm": tiles(g["mla_kv_norm"]),
        "gn_g": tiles(g["ret_gn_g"]), "gn_b": tiles(g["ret_gn_b"]), "conv_w": taps(g["e_a_conv_w_2"]),
        "conv_b": tiles(g["e_a_conv_b_2"]), "a_ln_g": tiles(g["e_a_ln_g_2"]), "a_ln_b": tiles(g["e_a_ln_b_2"]),
        "pw_b": tiles(g["e_a_pw_b_2"]), "c_conv": taps(g["o_c_conv_w_2"]),
        "sink": np.broadcast_to(g["o_sink_2"], (P, 8)), "zeta": const["cols"][:, 0:4],
        "inv_ret": const["cols"][:, 4:5], "inv_mla": const["cols"][:, 5:6], "g_chunk": const["cols"][:, 6:8],
        "eps1": const["cols"][:, 8:9], "eps2": const["cols"][:, 9:10],
    }
    arrays = {
        "vecs": np.concatenate([parts[n] for n, _ in VEC_PARTS], 1),
        "masks": mask_constants(),
        "x": g["x"][0], "ctx": g["ctx_2"][0], "positions": g["positions"],
        "w_ada": g["w_ada"][0], "w_in": g["w_in"][0], "w_uq": g["w_uq"][0], "w_ukv": g["w_ukv"][0],
        "w_out": g["w_out"][0], "w_ff1": g["w_ff1"][0], "w_ff2": g["w_ff2"][0],
        "e_w_mod": g["e_w_mod_2"][0], "e_w_in": g["e_w_in_2"][0], "e_a_pw_w": g["e_a_pw_w_2"][0],
        "e_b_fw": g["e_b_fw_2"][0], "e_w_out": g["e_w_out_2"][0], "o_w_mod": g["o_w_mod_2"][0],
        "o_w_in": g["o_w_in_2"][0], "o_w_out": g["o_w_out_2"][0],
    }
    arrays.update({k: v for k, v in const.items() if k != "cols"})
    nc = _bacc.Bacc("TRN2", target_bir_lowering=False, num_devices=1)
    named, args = {}, {}
    for name, a in arrays.items():
        a = np.ascontiguousarray(a)
        named[f"in_{name}"] = a
        args[name] = nc.dram_tensor(f"in_{name}", a.shape, mybir.dt.from_np(a.dtype), kind="ExternalInput").ap()
    out = nc.dram_tensor("out_0", (SEQ, D), F32, kind="ExternalOutput").ap()
    build_program(nc, args, out)
    r = _run(nc, [named], core_ids=[0])
    return r.results[0]["out_0"].reshape(1, SEQ, D)
```

```python
from contextlib import ExitStack

import concourse.bass as bass
import numpy as np
from concourse import mybir

F32 = mybir.dt.float32
F32R = mybir.dt.float32r
BF16 = mybir.dt.bfloat16
I32 = mybir.dt.int32
ALU = mybir.AluOpType
ACT = mybir.ActivationFunctionType
AX = mybir.AxisListType

P = 128
D = 1024
KT = D // P
SEQ = 1024
CTX = 256
D_FF = 4096
N_CHUNK = D_FF // D
MLA_HEADS, NOPE, ROPE, MLA_V = 8, 64, 32, 64
MLA_QK = NOPE + ROPE
RET_HEADS, RET_DK, RET_DV = 4, 64, 128
N_Q, HEAD = 8, 64
GRID_W = 64
CONV_W = 31
PAD = CONV_W // 2
EPS_1, EPS_2 = 1e-5, 1e-6
ALPHA = 2.0 ** 0.25
IN_KR = 320
MAGIC = 1.5 * 2.0 ** 23
TWO_PI_PARTS = (6.28125, 0.0019350051879882812, 3.0199157663446e-07)
PI_SAFE = 3.1415925
NEG = -1e30

VEC_PARTS = [
    ("c", 8), ("c2", 16), ("ln_in_g", 8), ("ln_in_b", 8), ("ln1_g", 8), ("ln1_b", 8), ("ln2_g", 8), ("ln2_b", 8),
    ("e_norm", 8), ("o_norm", 8), ("final", 8), ("b_ada", 48), ("e_b", 24), ("o_b", 24), ("q_norm", 2),
    ("kv_norm", 1), ("gn_g", 4), ("gn_b", 4), ("conv_w", 4 * CONV_W), ("conv_b", 4), ("a_ln_g", 4), ("a_ln_b", 4),
    ("pw_b", 4), ("c_conv", 12), ("sink", 8), ("zeta", 4), ("inv_ret", 1), ("inv_mla", 1), ("g_chunk", 2),
    ("eps1", 1), ("eps2", 1),
]
VEC, _at = {}, 0
for _name, _n in VEC_PARTS:
    VEC[_name] = _at
    _at += _n
N_VEC = _at


def shape_constants():
    f = np.float64
    out = {}
    out["ident"] = np.eye(P, dtype=np.float32)

    def pairs(period, half, lo, hi):
        m = np.zeros((P, P), np.float32)
        for d in range(lo, hi):
            if (d - lo) % period < half:
                m[d + half, d] = -1.0
            else:
                m[d - half, d] = 1.0
        return m

    out["swap_ret"] = pairs(64, 32, 0, P)
    out["swap_mla"] = pairs(32, 16, NOPE, MLA_QK)
    out["swap_win"] = pairs(32, 16, 0, P)
    log_g = np.log(1.0 - 2.0 ** (-5.0 - np.arange(RET_HEADS, dtype=f)))
    idx = np.arange(P, dtype=f)
    k_scale = RET_DK ** -0.5
    dec = np.zeros((P, RET_HEADS, P), f)
    for h in range(RET_HEADS):
        diff = idx[None, :] - idx[:, None]
        dec[:, 2 * (h % 2) + h // 2] = np.where(diff >= 0, np.exp(log_g[h] * np.maximum(diff, 0)), 0.0) * k_scale
    out["decay"] = dec.reshape(P, -1).astype(np.float32)
    xi = np.zeros((P, 2, P), f)
    for p in range(2):
        for hh in range(2):
            xi[64 * hh:64 * hh + 64, p] = np.exp(log_g[2 * p + hh] * (idx + 1.0))[None]
    out["xi"] = xi.reshape(P, -1).astype(np.float32)
    cols = np.zeros((P, 11), f)
    for h in range(RET_HEADS):
        cols[:, h] = np.exp(log_g[h] * (P - 1 - idx)) * k_scale
    inv32 = (np.float32(10000.0) ** (-np.arange(32, dtype=np.float32) / np.float32(32))).astype(np.float32)
    inv16 = (np.float32(10000.0) ** (-np.arange(16, dtype=np.float32) / np.float32(16))).astype(np.float32)
    cols[:, 4] = inv32[np.arange(P) % 32]
    cols[:, 5] = inv16[np.arange(P) % 16]
    for p in range(2):
        for hh in range(2):
            cols[64 * hh:64 * hh + 64, 6 + p] = np.exp(log_g[2 * p + hh] * P)
    cols[:, 8], cols[:, 9] = EPS_1, EPS_2
    out["cols"] = cols[:, :10].astype(np.float32)
    tok = np.arange(SEQ)
    where = np.stack([tok // GRID_W, tok % GRID_W]).astype(np.float32)
    d = np.arange(P) % HEAD
    ang = (where[d // 32] * inv16[d % 16][:, None]).astype(np.float32).astype(f)
    out["cos_win"], out["sin_win"] = np.cos(ang).astype(np.float32), np.sin(ang).astype(np.float32)
    n = np.arange(P, dtype=f)
    th = 2 * np.pi * (np.outer(n, n) % P) / P
    out["dft_d"] = np.concatenate([np.cos(th), -np.sin(th)], 1).astype(f) / np.sqrt(P)
    out["dft_d"] = out["dft_d"].astype(np.float32)
    for length in (SEQ, CTX):
        tiles = []
        for parity in range(2):
            for m in range(length // 2 // P):
                l = 2 * (m * P + np.arange(P)) + parity
                a = 2 * np.pi * (np.outer(l, np.arange(length // 2)) % length) / length
                tiles.append(np.concatenate([np.cos(a), np.sin(a)], 1))
        out[f"dft_{length}"] = np.concatenate(tiles).astype(np.float32)
    return out


def mask_constants():
    q, k = np.arange(P)[:, None], np.arange(P)[None, :]
    return np.concatenate([np.eye(P), np.where(k > q, NEG, 0.0), np.where(k < q, NEG, 0.0)], 1).astype(np.float32)


def build_program(nc, A, out):
    ctx = ExitStack()
    with ctx:
        BANK = 40
        banks_of_signals = [[ctx.enter_context(nc.semaphore(f"stage_signal_{b}_{i}")) for i in range(BANK)]
                            for b in range(2)]
        named = {}
        current = [0]

        def S(name):
            mine = named.setdefault(current[0], {})
            if name not in mine:
                mine[name] = banks_of_signals[current[0] % 2][len(mine)]
            return mine[name]

        def whole(name):
            return ctx.enter_context(nc.semaphore(name))

        base = 16640
        kb = 1024

        def at(name, shape, dt, offset):
            return nc.alloc_sbuf_tensor_at(name, shape, dt, offset=base + offset)

        X = at("X", [P, KT, SEQ], F32, 0)
        RAW = [at(f"RAW{s}", [P, KT, P], F32, 32 * kb + 4 * kb * s) for s in range(2)]
        WH = [at(f"WH{s}", [P, KT, P], F32R, 40 * kb + 4 * kb * s) for s in range(2)]
        WL = [at(f"WL{s}", [P, KT, P], F32R, 48 * kb + 4 * kb * s) for s in range(2)]
        small = [56 * kb]

        def keep(name, shape, dt):
            n = int(np.prod(shape[1:])) * (2 if dt == BF16 else 4)
            t = at(name, shape, dt, small[0])
            small[0] += (n + 31) // 32 * 32
            return t

        IDENT = keep("IDENT", [P, P], F32)
        ONES = keep("ONES", [P, P], F32)
        MASKS = keep("MASKS", [P, 3 * P], BF16)
        V = keep("V", [P, N_VEC], F32)
        MODA = keep("MODA", [P, 48], F32)
        MODE = keep("MODE", [P, 24, 2], F32)
        MODO = keep("MODO", [P, 24, 2], F32)
        CACT = keep("CACT", [P, 8], F32)
        C2ACT = keep("C2ACT", [P, 8, 2], F32)
        GS = keep("GS", [P, 2, 8, 2], F32)
        KC = keep("KC", [P, CTX], F32)
        VC = keep("VC", [P, 2, P], F32)
        BNS = keep("BNS", [P, 8, 4, 6], F32)
        MV = keep("MV", [P, 32, 2], F32)
        SD = keep("SD", [P, 32], F32)
        RS = keep("RS", [P, 32], F32)
        ROW = {n: keep(n, [P, 8], F32) for n in ("NMX", "NB", "SUM", "RDEN", "ESINK")}
        assert small[0] <= 64 * kb, small[0]
        z0 = small[0]
        assert base + z0 + 144 * kb <= 229368, base + z0 + 144 * kb

        def Z(name, shape, dt, offset_kb):
            return at(name, shape, dt, z0 + int(offset_kb * kb))

        HH = Z("HH", [P, KT, SEQ], F32R, 80)
        HL = Z("HL", [P, KT, SEQ], F32R, 112)
        T32 = [Z(f"T32_{s}", [P, SEQ], F32, 72 + 4 * s) for s in range(2)]

        G = [ctx.enter_context(nc.psum_tensor(f"G{s}", [P, 1024], F32)) for s in range(2)]
        M = [ctx.enter_context(nc.psum_tensor(f"M{s}", [P, 1024], F32)) for s in range(2)]

        raw_loaded = [whole(f"raw_loaded{s}") for s in range(2)]
        raw_used = [whole(f"raw_used{s}") for s in range(2)]
        w_split = [whole(f"w_split{s}") for s in range(2)]
        unit_done = [whole(f"unit_done{s}") for s in range(2)]
        unit_freed = [whole(f"unit_freed{s}") for s in range(2)]
        left = {k: whole(f"stages_left_by_{k}") for k in ("act", "pe", "dve")}
        w_high = whole("w_high")
        split_begun = whole("split_begun")
        q_half = whole("q_half")
        moved = whole("moved")

        def vec(name, i=0, n=1):
            return V[:, VEC[name] + i:VEC[name] + i + n]

        stages = []
        count = {"raw": 0, "unit": 0, "dma": 0}

        def stage(name, progs, raw=None, units=0, dmas=(), per_unit=1):
            n_raw = sum(2 * n for n, _ in raw or [])
            stages.append(dict(name=name, progs=progs, raw=raw or [], r0=count["raw"], u0=count["unit"],
                               units=units, per_unit=per_unit, dmas=list(dmas), dma_end=count["dma"] + 16 * len(dmas)))
            count["raw"] += n_raw
            count["unit"] += units
            count["dma"] += 16 * len(dmas)

        def info(name):
            return next(s for s in stages if s["name"] == name)

        def cols(w, c0):
            return lambda s, i: w[:, bass.ds(c0 + i * 256 + s * P, P)].rearrange("(k p) n -> p k n", p=P)

        def load_unit(sp, r2, s, src, view):
            need(sp, raw_used[s], r2)
            sp.dma_start(view, src).then_inc(raw_loaded[s], 16)

        def split_unit(pool, s, r2, u2):
            pool.wait_ge(raw_loaded[s], r2 * 16 + 16)
            need(pool, unit_done[s], u2)
            pool.sem_inc(split_begun, 1)
            pool.tensor_scalar(WH[s][:], RAW[s][:], 1.0, 0.0, ALU.mult, ALU.add).then_inc(w_high, 1)
            pool.wait_ge(w_high, u2 * 2 + s + 1)
            need(pool, w_split[s], u2)
            pool.tensor_tensor(WL[s][:], RAW[s][:], WH[s][:].bitcast(F32), ALU.subtract).then_inc(w_split[s], 1)
            pool.wait_ge(w_split[s], u2 + 1)
            pool.sem_inc(raw_used[s], 1)

        def split_pairs(pool, r0, u0, n_pairs, per_unit):
            turns(pool, n_pairs, lambda i: [split_unit(pool, s, i * per_unit + r0 // 2, i + u0 // 2)
                                            for s in range(2)])

        def gemm_unit(pe, s, u2, T, acts, order=range(KT), ready=None):
            hi, lo = acts
            nt = max(1, T // 512)
            w = T // nt
            pe.wait_ge(w_split[s], u2 + 1)
            need(pe, unit_freed[s], u2)
            for j, k in enumerate(order):
                if ready and k in ready:
                    pe.wait_ge(*ready[k])
                for part, moving in ((WH, hi), (WH, lo), (WL, hi)):
                    for n in range(nt):
                        m = pe.matmul(G[s][:, n * w:(n + 1) * w], part[s][:, k, :],
                                      moving[:, k, n * w:(n + 1) * w], start=(j == 0 and part is WH and moving is hi),
                                      stop=(j == KT - 1 and part is WL))
            m.then_inc(unit_done[s], 1)

        def lead_in(name, T, signal, tiles=range(KT), freed=None):
            def first_unit(pe):
                ready = {k: (S(signal), i + 1) for i, k in enumerate(tiles)}
                if freed:
                    pe.wait_ge(S(freed[0]), freed[1])
                gemm_unit(pe, 0, info(name)["u0"] // 2, T, (HH, HL),
                          [k for k in range(KT) if k not in ready] + list(tiles), ready)
            return first_unit

        def gemm_pairs(pe, u0, n_pairs, T, acts, after=None, led=False):
            def pair(i):
                for s in range(2):
                    if not (led and isinstance(i, int) and s == 0):
                        gemm_unit(pe, s, i + u0 // 2, T, acts)
                    if after:
                        after(pe, i, s)
            turns(pe, n_pairs, pair)

        def turns(eng, n, body):
            body(0)
            if n > 1:
                with eng.Fori(1, n) as i:
                    body(i)

        def need(eng, signal, value):
            if not isinstance(value, int) or value > 0:
                eng.wait_ge(signal, value)

        def unit_ready(eng, U):
            eng.wait_ge(unit_done[U % 2], U // 2 + 1)

        MP = Z("MP", [P, KT, P], F32, 72)
        MS = [Z(f"MS{s}", [P, 2, P], F32, 76 + s) for s in range(2)]

        def mod_begin(dve):
            dve.sem_inc(S("mod_rows"), 1)
            for s in range(2):
                dve.sem_inc(S(f"mod_read{s}"), 1)

        def mod_rows(dve, s, r2, n, xs):
            for c, x in enumerate(xs):
                dve.wait_ge(raw_loaded[s], r2 * 16 + 16)
                dve.wait_ge(S("mod_rows"), 2 * (n + c) + 1)
                dve.tensor_tensor(MP[:], RAW[s][:], x.unsqueeze(2).broadcast_to([P, KT, P]), ALU.mult)\
                   .then_inc(S("mod_rows"), 1)
                dve.wait_ge(S("mod_rows"), 2 * (n + c) + 2)
                dve.tensor_reduce(MS[s][:, c, :], MP[:].rearrange("p k n -> p n k"), AX.X, ALU.add)\
                   .then_inc(S("mod_rows"), 1)
            dve.sem_inc(raw_used[s], 1)
            dve.wait_ge(S("mod_rows"), 2 * (n + len(xs)) + 1)
            dve.sem_inc(S(f"mod_part{s}"), 1)

        def mod_sum(pe, s, n, width):
            pe.wait_ge(S(f"mod_part{s}"), n + 1)
            pe.wait_ge(S(f"mod_read{s}"), n + 1)
            for c in range(width):
                m = pe.matmul(M[s][:, c:c + 1], MS[s][:, c, :], ONES[:, 0:1], start=True, stop=True)
            m.then_inc(S(f"mod_sum{s}"), 1)

        def mod_add(dve, s, n, dst, bias):
            dve.wait_ge(S(f"mod_sum{s}"), n + 1)
            dve.tensor_scalar(dst, M[s][:, 0:dst.shape[-1]], bias, None, ALU.add).then_inc(S(f"mod_read{s}"), 1)

        def ada_rows(dve, name, j):
            mod_rows(dve, j % 2, info(name)["r0"] // 2 + 2 * (j // 2) + 1, j, [CACT[:]])

        def ada_add(dve, first, j):
            mod_add(dve, j % 2, j // 2, MODA[:, first + j:first + j + 1], vec("b_ada", first + j))

        def with_ada(sp, r0, n, unit, first):
            for j in range(n):
                r2 = r0 // 2 + 2 * (j // 2)
                load_unit(sp, r2, j % 2, unit(j), RAW[j % 2][:])
                c0 = (first + j) * P
                load_unit(sp, r2 + 1, j % 2, A["w_ada"][:, c0:c0 + P].rearrange("(k p) n -> p k n", p=P),
                          RAW[j % 2][:])

        def h_act(act, tag, ready, T, src, scale, shift, hh=None):
            for f in range(KT):
                act.wait_ge(ready, f + 1)
                if f >= 2:
                    act.wait_ge(S(tag + "_lo"), f - 1)
                act.activation(T32[f % 2][:, :T], src(f), ACT.Identity, bias=shift(f),
                               scale=scale(f)).then_inc(S(tag + "_t32"), 1)
                act.wait_ge(S(tag + "_t32"), f + 1)
                act.activation(HH[:, f, :T], T32[f % 2][:, :T], ACT.Copy).then_inc(S(tag + "_hi"), 1)

        def h_low(dve, tag, f, T):
            dve.wait_ge(S(tag + "_hi"), f + 1)
            dve.tensor_tensor(HL[:, f, :T], T32[f % 2][:, :T], HH[:, f, :T].bitcast(F32),
                              ALU.subtract).then_inc(S(tag + "_lo"), 1)

        XT = Z("XT", [P, KT, D], F32, 0)
        NT = SEQ // P
        MASK32 = Z("MASK32", [P, 3 * P], F32, 128)
        ADA = [Z(f"ADA{g}", [P, KT, 512], F32, 64 + 16 * g if g < 4 else 32 + 16 * (g - 4)) for g in range(6)]

        def start_sp(sp, r0):
            for t in range(NT):
                sp.dma_start(XT[:, t, :], A["x"][t * P:(t + 1) * P, :]).then_inc(S("x_in"), 16)
            for g in range(6):
                sp.dma_start(ADA[g][:], A["w_ada"][:, 512 * g:512 * g + 512].rearrange("(k p) n -> p k n", p=P))\
                  .then_inc(S(f"ada{g}"), 16)

        def start_dve(dve):
            dve.memset(ONES[:], 1.0).then_inc(S("ones"), 1)
            dve.wait_ge(moved, info("start")["dma_end"])
            dve.wait_ge(S("c_act"), 2)
            dve.tensor_copy(MASKS[:], MASK32[:]).then_inc(S("masks"), 1)
            g4 = V[:, VEC["ln_in_g"]:VEC["ln_in_g"] + 4 * KT]
            dve.tensor_scalar(g4, g4, ALPHA, None, ALU.mult).then_inc(S("masks"), 1)
            dve.wait_ge(S("x_in"), 16 * NT)
            for t in range(NT):
                for j in range(2):
                    dve.bn_stats(BNS[:, t, j, :], XT[:, t, 512 * j:512 * j + 512]).then_inc(S("li_st"), 1)
                dve.wait_ge(S("li_st"), 2 * t + 2)
                dve.bn_aggr(MV[:, t, :], BNS[:, t, 0:2, :].rearrange("p a b -> p (a b)")).then_inc(S("li_mv"), 1)
            dve.wait_ge(S("li_sd"), 1)
            dve.reciprocal(RS[:, 0:NT], SD[:, 0:NT]).then_inc(S("li_rs"), 1)
            dve.wait_ge(S("li_rs"), 1)
            for t in range(NT):
                dve.tensor_scalar(XT[:, t, :], XT[:, t, :], MV[:, t, 0:1], RS[:, t:t + 1], ALU.subtract,
                                  ALU.mult).then_inc(S("li_xn"), 1)
            prod = X[:, 0:4, :].rearrange("p a (b n) -> p (a b) n", n=512)
            for i, g in enumerate((0, 3)):
                dve.wait_ge(S(f"ada{g}"), 16)
                if i:
                    dve.wait_ge(S("ada_rows"), 2)
                dve.tensor_tensor(prod, ADA[g][:], CACT[:].unsqueeze(2).broadcast_to([P, KT, 512]), ALU.mult)\
                   .then_inc(S("ada_rows"), 1)
                dve.wait_ge(S("ada_rows"), 2 * i + 1)
                dve.tensor_reduce(X[:, 4 + i, 0:512], prod.rearrange("p k n -> p n k"), AX.X, ALU.add)\
                   .then_inc(S("ada_rows"), 1)
            dve.wait_ge(S("ada_sum"), 4)
            dve.tensor_tensor(MODA[:, 0:16], G[0][:, 0:16], vec("b_ada", 0, 16), ALU.add).then_inc(S("mod_in"), 1)
            dve.wait_ge(S("mod_in"), 1)
            dve.tensor_scalar(MODA[:, 8:16], MODA[:, 8:16], 1.0, 1.0 / ALPHA, ALU.add, ALU.mult).then_inc(S("mod_in"), 1)
            for f in range(KT):
                dve.wait_ge(S("li_tr"), f + 1)
                dve.tensor_scalar(X[:, f, :], M[f % 2][:], vec("ln_in_g", f), vec("ln_in_b", f), ALU.mult,
                                  ALU.add).then_inc(S("li_x"), 1)
                if f:
                    h_low(dve, "li", f - 1, SEQ)
            h_low(dve, "li", KT - 1, SEQ)
            dve.wait_ge(S("ada_sum"), 6)
            dve.tensor_tensor(MODA[:, 16:24], G[1][:, 0:8], vec("b_ada", 16, 8), ALU.add).then_inc(S("mod_in"), 1)

        def start_act(act):
            act.wait_ge(moved, info("start")["dma_end"])
            act.activation(CACT[:], vec("c", 0, 8), ACT.Silu).then_inc(S("c_act"), 1)
            act.activation(C2ACT[:].rearrange("p k c -> p (k c)"), vec("c2", 0, 16), ACT.Silu).then_inc(S("c_act"), 1)
            act.wait_ge(S("li_mv"), NT)
            act.activation(SD[:, 0:NT], MV[:, 0:NT, 1], ACT.Sqrt, bias=vec("eps1"), scale=1.0).then_inc(S("li_sd"), 1)
            act.wait_ge(S("mod_in"), 2)
            h_act(act, "li", S("li_x"), SEQ, lambda f: X[:, f, :], lambda f: MODA[:, 8 + f:9 + f],
                  lambda f: MODA[:, f:f + 1])

        def start_pe(pe):
            def ada(g):
                pe.wait_ge(S(f"ada{g}"), 16)
                for u in range(4):
                    col = 4 * (g % 4) + u
                    for k in range(KT):
                        m = pe.matmul(G[g // 4][:, col:col + 1], ADA[g][:, k, u * P:(u + 1) * P], CACT[:, k:k + 1],
                                      start=(k == 0), stop=(k == KT - 1))
                m.then_inc(S("ada_sum"), 1)
            pe.wait_ge(S("c_act"), 2)
            for g in (1, 2):
                ada(g)
            for i, g in enumerate((0, 3)):
                pe.wait_ge(S("ada_rows"), 2 * i + 2)
                for u in range(4):
                    m = pe.matmul(G[0][:, 4 * g + u:4 * g + u + 1], X[:, 4 + i, u * P:(u + 1) * P], ONES[:, 0:1],
                                  start=True, stop=True)
                m.then_inc(S("ada_sum"), 1)
            pe.wait_ge(S("li_xn"), NT)
            for f in range(KT):
                if f >= 2:
                    pe.wait_ge(S("li_x"), f - 1)
                for t in range(NT):
                    m = pe.transpose(M[f % 2][:, t * P:(t + 1) * P], XT[:, t, f * P:(f + 1) * P], IDENT[:])
                m.then_inc(S("li_tr"), 1)
            for g in (4, 5):
                ada(g)

        stage("start", dict(act=start_act, pe=start_pe, dve=start_dve, sp_free=start_sp), raw=[(0, None)],
              dmas=[(V[:], A["vecs"]), (IDENT[:], A["ident"]), (MASK32[:], A["masks"])])

        QC = Z("QC", [P, 2, SEQ], F32, 0)
        KVC = Z("KVC", [P, SEQ], F32, 8)
        KR = Z("KR", [P, SEQ], F32, 12)
        RQ = Z("RQ", [P, 2, SEQ], F32, 16)
        RK = Z("RK", [P, 2, SEQ], F32, 24)
        RV = Z("RV", [P, 4, SEQ], F32, 32)
        RG = Z("RG", [P, 4, SEQ], F32, 48)
        WIN_COLS = [0, 128, 256, IN_KR, 416, 544, 672, 800] + [928 + 128 * i for i in range(4)] + \
            [1440 + 128 * i for i in range(4)]
        win_dst = [QC[:, 0, :], QC[:, 1, :], KVC[:], KR[:], RQ[:, 0, :], RQ[:, 1, :], RK[:, 0, :], RK[:, 1, :]] + \
            [RV[:, i, :] for i in range(4)]

        def win_dve(dve):
            u0 = info("win")["u0"]
            mod_begin(dve)
            for j, dst in enumerate(win_dst):
                ada_rows(dve, "win", j)
                unit_ready(dve, u0 + j)
                dve.tensor_copy(dst, G[j % 2][:]).then_inc(unit_freed[j % 2], 1)
                ada_add(dve, 24, j)
            for j in range(12, 16):
                ada_rows(dve, "win", j)
                ada_add(dve, 24, j)
            for s in range(2):
                dve.wait_ge(S(f"mod_read{s}"), 8 + 1)
            dve.tensor_scalar(MODA[:, 32:40], MODA[:, 32:40], 1.0, 1.0 / ALPHA, ALU.add, ALU.mult).then_inc(S("one_plus"), 1)

        def win_act(act):
            u0 = info("win")["u0"]
            for j in range(12, 16):
                unit_ready(act, u0 + j)
                act.activation(RG[:, j - 12, :], G[j % 2][:], ACT.Silu).then_inc(unit_freed[j % 2], 1)

        def win_unit(j):
            return A["w_in"][:, WIN_COLS[j]:WIN_COLS[j] + P].rearrange("(k p) n -> p k n", p=P)

        def win_pe(pe):
            gemm_pairs(pe, info("win")["u0"], 8, SEQ, (HH, HL), led=True, after=lambda pe, i, s: mod_sum(pe, s, i, 1))

        stage("win", dict(lead=lead_in("win", SEQ, "li_lo"), act=win_act, pe=win_pe, dve=win_dve, sp_free=lambda sp, r0: with_ada(sp, r0, 16, win_unit, 24)),
              raw=[(16, None)], units=16, per_unit=2)

        COSR, SINR = Z("COSR", [P, SEQ], F32, 112), Z("SINR", [P, SEQ], F32, 116)
        COSM, SINM = Z("COSM", [P, SEQ], F32, 120), Z("SINM", [P, SEQ], F32, 124)
        POSI = Z("POSI", [P, SEQ], I32, 80)
        POSF = Z("POSF", [P, SEQ], F32, 84)
        ANG, TRN = Z("ANG", [P, SEQ], F32, 88), Z("TRN", [P, SEQ], F32, 92)

        def trig_pe(pe):
            pe.wait_ge(S("tr_pos"), 1)
            for n in range(2):
                m = pe.matmul(M[0][:, 512 * n:512 * n + 512], ONES[0:1, :], POSF[0:1, 512 * n:512 * n + 512],
                              start=True, stop=True)
            m.then_inc(S("tr_bc"), 1)

        def trig_dve(dve):
            dve.wait_ge(moved, info("trig")["dma_end"])
            dve.tensor_copy(POSF[0:1, :], POSI[0:1, :]).then_inc(S("tr_pos"), 1)
            dve.wait_ge(S("tr_bc"), 1)
            chain = S("tr_chain")
            n = [0]

            def step(ins):
                ins.then_inc(chain, 1)
                n[0] += 1
                dve.wait_ge(chain, n[0])
            for q, (inv, sin, cos) in enumerate((("inv_ret", SINR, COSR), ("inv_mla", SINM, COSM))):
                step(dve.tensor_scalar(ANG[:], M[0][:], vec(inv), None, ALU.mult))
                step(dve.tensor_scalar(TRN[:], ANG[:], 1.0 / (2.0 * np.pi), MAGIC, ALU.mult, ALU.add))
                step(dve.tensor_scalar(TRN[:], TRN[:], -MAGIC, None, ALU.add))
                for part in TWO_PI_PARTS:
                    step(dve.scalar_tensor_tensor(out=ANG[:], in0=TRN[:], scalar=-part, in1=ANG[:], op0=ALU.mult,
                                                  op1=ALU.add))
                dve.tensor_scalar(ANG[:], ANG[:], PI_SAFE, -PI_SAFE, ALU.min, ALU.max).then_inc(S("tr_ang"), 1)
                dve.wait_ge(S("tr_sin"), 3 * q + 3)
                dve.tensor_scalar(cos[:], cos[:], -2.0, 1.0, ALU.mult, ALU.add).then_inc(S("tr_cos"), 1)

        def trig_act(act):
            for q, (sin, cos) in enumerate(((SINR, COSR), (SINM, COSM))):
                act.wait_ge(S("tr_ang"), q + 1)
                act.activation(sin[:], ANG[:], ACT.Sin).then_inc(S("tr_sin"), 1)
                act.activation(cos[:], ANG[:], ACT.Sin, scale=0.5).then_inc(S("tr_sin"), 1)
                act.wait_ge(S("tr_sin"), 3 * q + 2)
                act.activation(cos[:], cos[:], ACT.Square).then_inc(S("tr_sin"), 1)

        stage("trig", dict(act=trig_act, pe=trig_pe, dve=trig_dve), dmas=[(POSI[0:1, :], A["positions"])])

        def swap_pe(pe, tag, i, tile, swap):
            if i >= 2:
                pe.wait_ge(S(tag + "_mul"), i - 1)
            for n in range(2):
                m = pe.matmul(M[i % 2][:, 512 * n:512 * n + 512], swap, tile[:, 512 * n:512 * n + 512],
                              start=True, stop=True)
            m.then_inc(S(tag + "_sw"), 1)

        def rope_dve(dve, tag, i, tile, cos, sin, tmp):
            dve.wait_ge(S(tag + "_sw"), i + 1)
            if i:
                dve.wait_ge(S(tag + "_rot"), 2 * i)
            dve.tensor_tensor(tmp, M[i % 2][:], sin, ALU.mult).then_inc(S(tag + "_mul"), 1)
            dve.tensor_tensor(tile, tile, cos, ALU.mult).then_inc(S(tag + "_rot"), 1)
            dve.wait_ge(S(tag + "_mul"), i + 1)
            dve.wait_ge(S(tag + "_rot"), 2 * i + 1)
            dve.tensor_tensor(tile, tile, tmp, ALU.add).then_inc(S(tag + "_rot"), 1)

        VT = Z("VT", [P, NT, 512], F32, 64)
        KZ = Z("KZ", [P, NT, 256], F32, 80)
        SWAPR = Z("SWAPR", [P, P], F32, 88)
        DECAY = Z("DECAY", [P, 512], F32, 89)
        XI = Z("XI", [P, 2, P], F32, 91)
        QX = [Z(f"QX{s}", [P, 2, P], F32, 92 + s) for s in range(2)]
        RTMP = Z("RTMP", [P, SEQ], F32, 120)
        STATE = [Z(f"STATE{s}", [P, 2, 256], F32, 112 + 2 * s) for s in range(2)]
        SCT = [Z(f"SCT{s}", [P, 512], F32, 116 + 2 * s) for s in range(2)]
        RTMP = Z("RTMP_", [P, SEQ], F32, 100)

        def rpre_pe(pe):
            pe.wait_ge(moved, info("rpre")["dma_end"])
            for i in range(4):
                swap_pe(pe, "rr", i, (RQ if i < 2 else RK)[:, i % 2, :], SWAPR[:])
            for j in range(4):
                pe.wait_ge(S("rr_mul"), min(3 + j, 4))
                if j >= 2:
                    pe.wait_ge(S("rv_out"), j - 1)
                for t in range(NT):
                    m = pe.transpose(M[j % 2][:, t * P:(t + 1) * P], RV[:, j, t * P:(t + 1) * P], IDENT[:])
                m.then_inc(S("rv_tr"), 1)
            pe.wait_ge(S("rr_rot"), 8)
            for j in range(2):
                pe.wait_ge(S("rv_out"), 3 + j)
                for t in range(NT):
                    m = pe.transpose(M[j][:, t * P:(t + 1) * P], RK[:, j, t * P:(t + 1) * P], IDENT[:])
                m.then_inc(S("rk_tr"), 1)

        def rpre_dve(dve):
            for i in range(4):
                rope_dve(dve, "rr", i, (RQ if i < 2 else RK)[:, i % 2, :], COSR[:], SINR[:], RTMP[:])
            for j in range(4):
                dve.wait_ge(S("rv_tr"), j + 1)
                dve.tensor_copy(VT[:, :, j * P:(j + 1) * P], M[j % 2][:].rearrange("p (t n) -> p t n", n=P))\
                   .then_inc(S("rv_out"), 1)

        def rpre_act(act):
            for j in range(2):
                act.wait_ge(S("rk_tr"), j + 1)
                for hh in range(2):
                    act.activation(KZ[:, :, j * P + 64 * hh:j * P + 64 * hh + 64],
                                   M[j][:].rearrange("p (t n) -> p t n", n=P)[:, :, 64 * hh:64 * hh + 64],
                                   ACT.Copy, scale=vec("zeta", 2 * j + hh)).then_inc(S("kz"), 1)

        stage("rpre", dict(act=rpre_act, pe=rpre_pe, dve=rpre_dve),
              dmas=[(SWAPR[:], A["swap_ret"]), (DECAY[:], A["decay"]), (XI[:].rearrange("p a b -> p (a b)"), A["xi"])])

        def in_bank(ps, h):
            return ps[:, 512 * (h % 2) + P * (h // 2):512 * (h % 2) + P * (h // 2) + P]

        def ret_pe(pe):
            def scores(c):
                if c >= 2:
                    pe.wait_ge(S("ret_dec"), c - 1)
                    pe.wait_ge(S("ret_state"), 2 * c - 2)
                for p in range(2):
                    pe.matmul(G[c % 2][:, 512 * p + 256:512 * p + 512], KZ[:, c, p * P:(p + 1) * P],
                              VT[:, c, p * 256:(p + 1) * 256], start=True, stop=True)
                t = slice(c * P, (c + 1) * P)
                for h in range(RET_HEADS):
                    r = slice(64 * (h % 2), 64 * (h % 2) + 64)
                    m = pe.matmul(in_bank(G[c % 2], h), RK[r, h // 2, t], RQ[r, h // 2, t], start=True, stop=True)
                m.then_inc(S("ret_sc"), 1)
            scores(0)
            for c in range(NT):
                if c + 1 < NT:
                    scores(c + 1)
                pe.wait_ge(S("ret_dec"), c + 1)
                if c >= 2:
                    pe.wait_ge(S("ret_out"), c - 1)
                if c:
                    pe.wait_ge(S("ret_qx"), 2 * c)
                    pe.wait_ge(S("ret_state"), 2 * c)
                for h in range(RET_HEADS):
                    r = slice(64 * (h % 2), 64 * (h % 2) + 64)
                    q = 2 * (h % 2) + h // 2
                    m = pe.matmul(in_bank(M[c % 2], h), SCT[c % 2][:, q * P:(q + 1) * P], VT[:, c, h * P:(h + 1) * P],
                                  start=True, stop=(c == 0))
                    if c:
                        m = pe.matmul(in_bank(M[c % 2], h), QX[c % 2][r, h // 2, :],
                                      STATE[(c - 1) % 2][r, h // 2, P * (h % 2):P * (h % 2) + P], start=False,
                                      stop=True)
                m.then_inc(S("ret_o"), 1)

        def ret_dve(dve):
            for c in range(NT):
                dve.wait_ge(S("ret_sc"), c + 1)
                if c >= 2:
                    dve.wait_ge(S("ret_o"), c - 1)
                dve.tensor_tensor(SCT[c % 2][:].rearrange("p (o n) -> p o n", o=2),
                                  G[c % 2][:].rearrange("p (o n) -> p o n", o=2)[:, :, 0:256],
                                  DECAY[:].rearrange("p (o n) -> p o n", o=2), ALU.mult).then_inc(S("ret_dec"), 1)
                if c:
                    for p in range(2):
                        dve.tensor_tensor(QX[c % 2][:, p, :], RQ[:, p, c * P:(c + 1) * P], XI[:, p, :],
                                          ALU.mult).then_inc(S("ret_qx"), 1)
                if c + 1 < NT:
                    for p in range(2):
                        kv = G[c % 2][:, 512 * p + 256:512 * p + 512]
                        if c == 0:
                            dve.tensor_copy(STATE[0][:, p, :], kv).then_inc(S("ret_state"), 1)
                        else:
                            dve.wait_ge(S("ret_state"), 2 * c)
                            dve.wait_ge(S("ret_o"), c)
                            dve.scalar_tensor_tensor(out=STATE[c % 2][:, p, :], in0=STATE[(c - 1) % 2][:, p, :],
                                                     scalar=vec("g_chunk", p), in1=kv, op0=ALU.mult,
                                                     op1=ALU.add).then_inc(S("ret_state"), 1)
            for c in range(NT):
                dve.wait_ge(S("ret_out"), c + 1)
                for h in range(RET_HEADS):
                    dve.bn_stats(BNS[:, c, h, :], VT[:, c, h * P:(h + 1) * P]).then_inc(S("ret_st"), 1)
            dve.wait_ge(S("ret_st"), 32)
            for c in range(NT):
                for h in range(RET_HEADS):
                    dve.bn_aggr(MV[:, 4 * c + h, :], BNS[:, c, h, :]).then_inc(S("ret_mv"), 1)
            dve.wait_ge(S("ret_sd"), 1)
            dve.reciprocal(RS[:], SD[:]).then_inc(S("ret_rs"), 1)
            dve.wait_ge(S("ret_rs"), 1)
            for h in range(RET_HEADS):
                for c in range(NT):
                    o = VT[:, c, h * P:(h + 1) * P]
                    q = 4 * c + h
                    dve.tensor_scalar(o, o, MV[:, q, 0:1], RS[:, q:q + 1], ALU.subtract, ALU.mult)\
                       .then_inc(S("ret_n"), 1)
            for h in range(RET_HEADS):
                dve.wait_ge(S("ret_t32"), h + 1)
                dve.tensor_tensor(RG[:, h, :], T32R[h % 2][:], RG[:, h, :], ALU.mult).then_inc(S("ret_gate"), 1)
                dve.wait_ge(S("ret_hi"), h + 1)
                dve.tensor_tensor(HL[:, 4 + h, :], RG[:, h, :], HH[:, 4 + h, :].bitcast(F32),
                                  ALU.subtract).then_inc(S("ret_lo"), 1)

        T32R = [Z(f"T32R{s}", [P, SEQ], F32, 80 + 4 * s) for s in range(2)]

        def ret_act(act):
            for c in range(NT):
                act.wait_ge(S("ret_o"), c + 1)
                act.activation(VT[:, c, :].rearrange("q (p o n) -> q o p n", p=2, o=2),
                               M[c % 2][:].rearrange("q (o p n) -> q o p n", o=2, n=P)[:, :, 0:2, :], ACT.Copy)\
                   .then_inc(S("ret_out"), 1)
            act.wait_ge(S("ret_mv"), 32)
            act.activation(SD[:], MV[:, :, 1], ACT.Sqrt, bias=vec("eps1"), scale=1.0).then_inc(S("ret_sd"), 1)
            for h in range(RET_HEADS):
                act.wait_ge(S("ret_nt"), h + 1)
                if h >= 2:
                    act.wait_ge(S("ret_gate"), h - 1)
                act.activation(T32R[h % 2][:], M[h % 2][:], ACT.Identity, bias=vec("gn_b", h),
                               scale=vec("gn_g", h)).then_inc(S("ret_t32"), 1)
                act.wait_ge(S("ret_gate"), h + 1)
                act.activation(HH[:, 4 + h, :], RG[:, h, :], ACT.Copy).then_inc(S("ret_hi"), 1)

        def ret_pe2(pe):
            ret_pe(pe)
            for h in range(RET_HEADS):
                pe.wait_ge(S("ret_n"), 8 * h + 8)
                if h >= 2:
                    pe.wait_ge(S("ret_t32"), h - 1)
                for c in range(NT):
                    m = pe.transpose(M[h % 2][:, c * P:(c + 1) * P], VT[:, c, h * P:(h + 1) * P], IDENT[:])
                m.then_inc(S("ret_nt"), 1)

        stage("ret", dict(act=ret_act, pe=ret_pe2, dve=ret_dve))

        ATT = Z("ATT", [P, NT, 512], F32, 16)
        QH = [Z(f"QH{s}", [P, SEQ], F32, 32 + 4 * s) for s in range(2)]
        KH = [Z(f"KH{s}", [P, SEQ], F32, 40 + 4 * s) for s in range(2)]
        VH = [Z(f"VH{s}", [P, NT, MLA_V], F32, 48 + 2 * s) for s in range(2)]
        PR = [Z(f"PR{s}", [P, SEQ], F32, 52 + 4 * s) for s in range(2)]
        PT = [Z(f"PT{s}", [P, SEQ], F32, 60 + 4 * s) for s in range(2)]
        LTMP = Z("LTMP", [P, SEQ], F32, 68)
        LSQ = [Z(f"LSQ{s}", [P, SEQ], F32, 80 + 4 * s) for s in range(3)]
        SWAPM = Z("SWAPM", [P, P], F32, 92)
        MWQ = [Z(f"MWQ{s}", [P, 2, MLA_QK], F32, 92.5 + s) for s in range(2)]
        MWK = [Z(f"MWK{s}", [P, P], F32, 94.5 + 0.5 * s) for s in range(2)]
        LR = [Z(f"LR{s}", [P, SEQ], F32, 112 + 4 * s) for s in range(2)]

        def lat_act(act):
            for i, t in enumerate((QC[:, 0, :], QC[:, 1, :], KVC[:])):
                act.activation(LSQ[i][:], t, ACT.Square).then_inc(S("lat_sq"), 1)
            for i, n in enumerate((256, 128)):
                act.wait_ge(S("lat_ms"), i + 1)
                act.activation(LR[i][:], M[i][:], ACT.Sqrt, bias=vec("eps1"), scale=1.0 / n).then_inc(S("lat_sd"), 1)

        def lat_pe(pe):
            pe.wait_ge(S("lat_sq"), 3)
            for i, tiles in enumerate(((0, 1), (2,))):
                for n in range(2):
                    for k in tiles:
                        m = pe.matmul(M[i][:, 512 * n:512 * n + 512], ONES[:], LSQ[k][:, 512 * n:512 * n + 512],
                                      start=(k == tiles[0]), stop=(k == tiles[-1]))
                m.then_inc(S("lat_ms"), 1)
            pe.wait_ge(moved, info("lat")["dma_end"])
            for n in range(2):
                m = pe.matmul(G[0][:, 512 * n:512 * n + 512], SWAPM[:], KR[:, 512 * n:512 * n + 512], start=True,
                              stop=True)
            m.then_inc(S("lat_sw"), 1)

        def lat_dve(dve):
            for i in range(2):
                dve.wait_ge(S("lat_sd"), i + 1)
                dve.reciprocal(LR[i][:], LR[i][:]).then_inc(S("lat_r"), 1)
                dve.wait_ge(S("lat_r"), i + 1)
                for k, t in (((0, QC[:, 0, :]), (1, QC[:, 1, :])) if i == 0 else ((0, KVC[:]),)):
                    dve.scalar_tensor_tensor(out=t, in0=t, scalar=vec("q_norm" if i == 0 else "kv_norm", k),
                                             in1=LR[i][:], op0=ALU.mult, op1=ALU.mult).then_inc(S("lat_n"), 1)
            dve.wait_ge(S("lat_sw"), 1)
            r = slice(NOPE, MLA_QK)
            dve.tensor_tensor(LTMP[r, :], G[0][r, :], SINM[r, :], ALU.mult).then_inc(S("lat_k"), 1)
            dve.tensor_tensor(KR[r, :], KR[r, :], COSM[r, :], ALU.mult).then_inc(S("lat_k"), 1)
            dve.wait_ge(S("lat_k"), 2)
            for s in range(2):
                dve.tensor_tensor(KH[s][r, :], KR[r, :], LTMP[r, :], ALU.add).then_inc(S("lat_k"), 1)

        stage("lat", dict(act=lat_act, pe=lat_pe, dve=lat_dve), dmas=[(SWAPM[:], A["swap_mla"])])

        SCALE_M = MLA_QK ** -0.5
        causal, before = MASKS[:, P:2 * P], MASKS[:, 2 * P:3 * P]
        identb = MASKS[:, 0:P]

        def mla_head_pe(pe, i, s):
            h8 = (i * 2 + s) * 8
            need(pe, S(f"mla_w{s}"), i * 32 + 32)
            need(pe, S("mla_smax"), h8)
            need(pe, S("mla_exp"), h8)
            need(pe, S("mla_att"), h8)
            for n in range(2):
                for k in range(2):
                    m = pe.matmul(G[0][0:MLA_QK, 512 * n:512 * n + 512], MWQ[s][:, k, :],
                                  QC[:, k, 512 * n:512 * n + 512], start=(k == 0), stop=(k == 1))
            m.then_inc(S("mla_q"), 1)
            for n in range(2):
                m = pe.matmul(G[1][0:NOPE, 512 * n:512 * n + 512], MWK[s][:, 0:NOPE], KVC[:, 512 * n:512 * n + 512],
                              start=True, stop=True)
            m.then_inc(S("mla_k"), 1)
            for t in range(NT):
                m = pe.matmul(M[1][:, t * MLA_V:(t + 1) * MLA_V], KVC[:, t * P:(t + 1) * P], MWK[s][:, NOPE:P],
                              start=True, stop=True)
            m.then_inc(S("mla_v"), 1)
            need(pe, S("mla_qc"), (i * 2 + s) + 1)
            for n in range(2):
                m = pe.matmul(G[0][0:MLA_QK, 512 * n:512 * n + 512], SWAPM[0:MLA_QK, 0:MLA_QK],
                              QH[s][0:MLA_QK, 512 * n:512 * n + 512], start=True, stop=True)
            m.then_inc(S("mla_sw"), 1)
            need(pe, S("mla_kc"), (i * 2 + s) * 2 + 2)
            need(pe, S("mla_rot"), (i * 2 + s) * 3 + 3)

            def scores(t):
                if t >= 2:
                    need(pe, S("mla_exp"), h8 + (t - 1))
                for n in range(0, t * P + P, 512):
                    e = min(n + 512, t * P + P)
                    last = e == t * P + P
                    m = pe.matmul(G[t % 2][:, n:e], QH[s][0:MLA_QK, t * P:(t + 1) * P], KH[s][0:MLA_QK, n:e],
                                  start=True, stop=not last)
                m = pe.matmul(G[t % 2][:, t * P:(t + 1) * P], identb, causal, start=False, stop=True)
                m.then_inc(S("mla_sc"), 1)

            def turn(t):
                need(pe, S("mla_exp"), h8 + (t + 1))
                need(pe, S("mla_pt"), h8 + t)
                for b in range(t + 1):
                    m = pe.transpose(M[0][:, b * P:(b + 1) * P], PR[t % 2][:, b * P:(b + 1) * P], IDENT[:])
                m.then_inc(S("mla_tr"), 1)

            def values(t):
                need(pe, S("mla_pt"), h8 + (t + 1))
                if t >= 2:
                    need(pe, S("mla_att"), h8 + (t - 1))
                for b in range(t + 1):
                    m = pe.matmul(M[1][:, 512 * (t % 2):512 * (t % 2) + MLA_V], PT[t % 2][:, b * P:(b + 1) * P],
                                  VH[s][:, b, :], start=(b == 0), stop=(b == t))
                m.then_inc(S("mla_pv"), 1)
            scores(0)
            for t in range(NT):
                if t + 1 < NT:
                    scores(t + 1)
                if t:
                    values(t - 1)
                turn(t)
            values(NT - 1)

        def mla_pe(pe):
            turns(pe, MLA_HEADS // 2, lambda i: [mla_head_pe(pe, i, s) for s in range(2)])

        def mla_dve(dve):
            def pair(i):
                for s in range(2):
                    h = i * 2 + s
                    h8 = h * 8
                    r = slice(NOPE, MLA_QK)
                    need(dve, S("mla_sw"), h + 1)
                    need(dve, S("mla_rot"), h * 3)
                    dve.tensor_tensor(LTMP[r, :], G[0][r, :], SINM[r, :], ALU.mult).then_inc(S("mla_rot"), 1)
                    dve.tensor_tensor(QH[s][r, :], QH[s][r, :], COSM[r, :], ALU.mult).then_inc(S("mla_rot"), 1)
                    need(dve, S("mla_rot"), h * 3 + 2)
                    dve.tensor_tensor(QH[s][r, :], QH[s][r, :], LTMP[r, :], ALU.add).then_inc(S("mla_rot"), 1)

                    def smax(t):
                        need(dve, S("mla_sc"), h8 + (t + 1))
                        need(dve, S("mla_smax"), h8 + t)
                        dve.tensor_reduce(ROW["NMX"][:, t:t + 1], G[t % 2][:, 0:(t + 1) * P], AX.X, ALU.max)\
                           .then_inc(S("mla_mx"), 1)
                        need(dve, S("mla_mx"), h8 + (t + 1))
                        need(dve, S("mla_exp"), h8)
                        dve.tensor_scalar(ROW["NB"][:, t:t + 1], ROW["NMX"][:, t:t + 1], -SCALE_M, None, ALU.mult)\
                           .then_inc(S("mla_smax"), 1)

                    def tail(t):
                        need(dve, S("mla_tr"), h8 + (t + 1))
                        need(dve, S("mla_pv"), h8 + (t - 1) if t else h8)
                        dve.tensor_copy(PT[t % 2][:, 0:(t + 1) * P], M[0][:, 0:(t + 1) * P]).then_inc(S("mla_pt"), 1)
                        need(dve, S("mla_rd"), h8 + t)
                        dve.reciprocal(ROW["RDEN"][:, t:t + 1], ROW["SUM"][:, t:t + 1]).then_inc(S("mla_rd"), 1)

                    def put(t):
                        need(dve, S("mla_pv"), h8 + (t + 1))
                        need(dve, S("mla_rd"), h8 + (t + 1))
                        dve.tensor_scalar(ATT[:, t, bass.ds(h * MLA_V, MLA_V)],
                                          M[1][:, 512 * (t % 2):512 * (t % 2) + MLA_V], ROW["RDEN"][:, t:t + 1],
                                          None, ALU.mult).then_inc(S("mla_att"), 1)
                    smax(0)
                    for t in range(NT):
                        if t + 1 < NT:
                            smax(t + 1)
                        if t:
                            put(t - 1)
                        tail(t)
                    put(NT - 1)
            turns(dve, MLA_HEADS // 2, pair)

        def mla_act(act):
            def pair(i):
                for s in range(2):
                    h = i * 2 + s
                    h8 = h * 8
                    need(act, S("mla_q"), h + 1)
                    act.activation(QH[s][0:MLA_QK, :], G[0][0:MLA_QK, :], ACT.Copy).then_inc(S("mla_qc"), 1)
                    need(act, S("mla_k"), h + 1)
                    act.activation(KH[s][0:NOPE, :], G[1][0:NOPE, :], ACT.Copy).then_inc(S("mla_kc"), 1)
                    need(act, S("mla_v"), h + 1)
                    act.activation(VH[s][:].rearrange("p t n -> p (t n)"), M[1][:, 0:512], ACT.Copy)\
                       .then_inc(S("mla_kc"), 1)
                    for t in range(NT):
                        need(act, S("mla_smax"), h8 + (t + 1))
                        need(act, S("mla_tr"), h8 + (t - 1) if t else h8)
                        need(act, S("mla_rd"), h8)
                        act.activation(PR[t % 2][:, 0:(t + 1) * P], G[t % 2][:, 0:(t + 1) * P], ACT.Exp,
                                       bias=ROW["NB"][:, t:t + 1], scale=SCALE_M,
                                       accum_out=ROW["SUM"][:, t:t + 1]).then_inc(S("mla_exp"), 1)
            turns(act, MLA_HEADS // 2, pair)

        def mla_sp(sp):
            def pair(i):
                for s in range(2):
                    need(sp, S("mla_v"), i * 2)
                    h = i * 2 + s
                    sp.dma_start(MWQ[s][:], A["w_uq"][:, bass.ds(h * MLA_QK, MLA_QK)]
                                 .rearrange("(k p) n -> p k n", p=P)).then_inc(S(f"mla_w{s}"), 16)
                    sp.dma_start(MWK[s][:], A["w_ukv"][:, bass.ds(h * P, P)]).then_inc(S(f"mla_w{s}"), 16)
            turns(sp, MLA_HEADS // 2, pair)

        stage("mla", dict(act=mla_act, pe=mla_pe, dve=mla_dve, sp_gated=mla_sp))

        def turn_stage(tag, att, tile0, gate=None, tmp=None):
            tmp = tmp or T32

            def pe_(pe):
                for j in range(4):
                    if j >= 2:
                        pe.wait_ge(S(tag + "_out"), j - 1)
                    for t in range(NT):
                        m = pe.transpose(M[j % 2][:, t * P:(t + 1) * P], att[:, t, j * P:(j + 1) * P], IDENT[:])
                    m.then_inc(S(tag + "_tr"), 1)

            def dve_(dve):
                for j in range(4):
                    dve.wait_ge(S(tag + "_tr"), j + 1)
                    if j >= 2:
                        dve.wait_ge(S(tag + "_hi"), j - 1)
                        dve.wait_ge(S(tag + "_lo"), j - 1)
                    if gate is None:
                        dve.tensor_copy(tmp[j % 2][:], M[j % 2][:]).then_inc(S(tag + "_out"), 1)
                    else:
                        dve.tensor_tensor(tmp[j % 2][:], M[j % 2][:], gate[:, j, :], ALU.mult)\
                           .then_inc(S(tag + "_out"), 1)
                    dve.wait_ge(S(tag + "_hi"), j + 1)
                    dve.tensor_tensor(HL[:, tile0 + j, :], tmp[j % 2][:], HH[:, tile0 + j, :].bitcast(F32),
                                      ALU.subtract).then_inc(S(tag + "_lo"), 1)

            def act_(act):
                for j in range(4):
                    act.wait_ge(S(tag + "_out"), j + 1)
                    act.activation(HH[:, tile0 + j, :], tmp[j % 2][:], ACT.Copy).then_inc(S(tag + "_hi"), 1)
            stage(tag, dict(act=act_, pe=pe_, dve=dve_))

        turn_stage("mturn", ATT, 0)

        def add_gated(dve, U, f, T, X_, gate):
            unit_ready(dve, U)
            dve.scalar_tensor_tensor(out=X_[:, f, :T], in0=G[U % 2][:, :T], scalar=gate, in1=X_[:, f, :T],
                                     op0=ALU.mult, op1=ALU.add).then_inc(unit_freed[U % 2], 1)

        def out_stage(name, w, T, X_, gate, led, first_ada=None):
            along = first_ada is not None

            def dve_(dve):
                u0 = info(name)["u0"]
                if along:
                    mod_begin(dve)
                for f in range(KT):
                    if along:
                        ada_rows(dve, name, f)
                    add_gated(dve, u0 + f, f, T, X_, gate(f))
                    if along:
                        ada_add(dve, first_ada, f)

            def pe_(pe):
                gemm_pairs(pe, info(name)["u0"], 4, T, (HH, HL), led=True,
                           after=(lambda pe, i, s: mod_sum(pe, s, i, 1)) if along else None)

            def sp_(sp, r0):
                with_ada(sp, r0, KT, lambda j: w[:, j * P:(j + 1) * P].rearrange("(k p) n -> p k n", p=P), first_ada)
            progs = dict(lead=lead_in(name, T, *led), pe=pe_, dve=dve_)
            if along:
                stage(name, dict(sp_free=sp_, **progs), raw=[(8, None)], units=8, per_unit=2)
            else:
                stage(name, progs, raw=[(4, cols(w, 0))], units=8)

        out_stage("wout", A["w_out"], SEQ, X, lambda f: MODA[:, 16 + f:17 + f],
                  ("mturn_lo", range(4)), first_ada=40)

        NSQ = [Z(f"NSQ{s}", [P, SEQ], F32, 4 * s) for s in range(2)]
        NR = Z("NR", [P, SEQ], F32, 8)

        def ones_sum(pe, dst, T, tiles, ready=None, used=None):
            nt = max(1, T // 512)
            w = T // nt
            for k in range(len(tiles)):
                if ready:
                    pe.wait_ge(ready, k + 1)
                for n in range(nt):
                    m = pe.matmul(dst[:, n * w:(n + 1) * w], ONES[:], tiles[k][:, n * w:(n + 1) * w],
                                  start=(k == 0), stop=(k == len(tiles) - 1))
                if used and k < len(tiles) - 1:
                    m.then_inc(used, 1)
            return m

        def norm_stage(tag, X_, T, mean, eps, finish_dve, finish_act, n_tiles=KT, sq=NSQ, r=NR):
            tiles = [X_[:, f, :T] for f in range(n_tiles)]
            width = n_tiles * P

            def pe_(pe):
                if mean:
                    ones_sum(pe, M[0], T, tiles).then_inc(S(tag + "_mean"), 1)
                ones_sum(pe, M[1], T, [sq[k % 2] for k in range(n_tiles)], ready=S(tag + "_sq"),
                         used=S(tag + "_squ")).then_inc(S(tag + "_var"), 1)

            def dve_(dve):
                if mean:
                    dve.wait_ge(S(tag + "_mean"), 1)
                    for f in range(n_tiles):
                        dve.scalar_tensor_tensor(out=tiles[f], in0=M[0][:, :T], scalar=-1.0 / width, in1=tiles[f],
                                                 op0=ALU.mult, op1=ALU.add).then_inc(S(tag + "_c"), 1)
                dve.wait_ge(S(tag + "_sd"), 1)
                dve.reciprocal(r[:, :T], r[:, :T]).then_inc(S(tag + "_r"), 1)
                dve.wait_ge(S(tag + "_r"), 1)
                finish_dve(dve, tag, r)

            def act_(act):
                for f in range(n_tiles):
                    if mean:
                        act.wait_ge(S(tag + "_c"), f + 1)
                    if f >= 2:
                        act.wait_ge(S(tag + "_squ"), f - 1)
                    act.activation(sq[f % 2][:, :T], tiles[f], ACT.Square).then_inc(S(tag + "_sq"), 1)
                act.wait_ge(S(tag + "_var"), 1)
                act.activation(r[:, :T], M[1][:, :T], ACT.Sqrt, bias=vec(eps), scale=1.0 / width)\
                   .then_inc(S(tag + "_sd"), 1)
                finish_act(act, tag)
            stage(tag, dict(act=act_, pe=pe_, dve=dve_))

        def ln_finish(g, b, scale=None, shift=None):
            def dve_(dve, tag, r):
                for f in range(KT + 1):
                    if f < KT:
                        dve.scalar_tensor_tensor(out=X[:, f, :], in0=X[:, f, :], scalar=vec(g, f), in1=r[:],
                                                 op0=ALU.mult, op1=ALU.mult).then_inc(S(tag + "_g"), 1)
                    if f < KT and scale is not None:
                        dve.wait_ge(S(tag + "_g"), f + 1)
                        dve.tensor_scalar(X[:, f, :], X[:, f, :], vec(b, f), None, ALU.add).then_inc(S(tag + "_x"), 1)
                    if f and scale is not None:
                        h_low(dve, tag, f - 1, SEQ)

            def act_(act, tag):
                if scale is not None:
                    h_act(act, tag, S(tag + "_x"), SEQ, lambda f: X[:, f, :], scale, shift)
                    return
                for f in range(KT):
                    act.wait_ge(S(tag + "_g"), f + 1)
                    act.activation(X[:, f, :], X[:, f, :], ACT.Identity, bias=vec(b, f), scale=1.0)\
                       .then_inc(S(tag + "_x"), 1)
            return dve_, act_

        norm_stage("ln1", X, SEQ, True, "eps1", *ln_finish("ln1_g", "ln1_b", lambda f: MODA[:, 32 + f:33 + f],
                                                           lambda f: MODA[:, 24 + f:25 + f]))

        FH = Z("FH", [P, KT, SEQ], F32R, 0)
        FL = Z("FL", [P, KT, SEQ], F32R, 32)
        T2 = [Z(f"T2_{s}", [P, SEQ], F32, 64 + 4 * s) for s in range(2)]

        PER_CHUNK = 3 * KT // N_CHUNK

        def ff_mod(q):
            if q >= 2 * PER_CHUNK:
                return None
            return (("e_w_mod", "e_b", MODE) if q < PER_CHUNK else ("o_w_mod", "o_b", MODO)) + (q % PER_CHUNK,)

        def ff_r2(c, q):
            return c * (8 + PER_CHUNK) + (info("ff")["r0"] // 2 + min(q // 2, PER_CHUNK) + q // 2)

        def ff_mod_rows(dve, c, q):
            if ff_mod(q):
                mod_rows(dve, q % 2, ff_r2(c, q) + 1, c * (4 * PER_CHUNK) + 2 * q, [C2ACT[:, :, 0], C2ACT[:, :, 1]])

        def ff_mod_sum(pe, c, q):
            if ff_mod(q):
                mod_sum(pe, q % 2, c * PER_CHUNK + q // 2, 2)

        def ff_mod_add(dve, c, q):
            if ff_mod(q):
                _, bias, dst, j = ff_mod(q)
                mod_add(dve, q % 2, c * PER_CHUNK + q // 2,
                        dst[:, bass.ds(c * PER_CHUNK + j, 1), :].rearrange("p a b -> p (a b)"),
                        V[:, bass.ds(c * PER_CHUNK + (VEC[bias] + j), 1)])

        def ff_pool(pool):
            u0 = info("ff")["u0"]

            def chunk(c):
                for q in range(2 * KT):
                    split_unit(pool, q % 2, ff_r2(c, q), c * 8 + (u0 // 2 + q // 2))
            turns(pool, N_CHUNK, chunk)

        def ff_pe(pe):
            u0 = info("ff")["u0"]

            def chunk(c):
                for q in range(2 * KT):
                    ready = {k: (S("ff_lo"), c * 8 + (k + 2)) for k in range(KT)} if q == KT else None
                    if q or not isinstance(c, int):
                        gemm_unit(pe, q % 2, c * 8 + (u0 // 2 + q // 2), SEQ, (FH, FL) if q >= KT else (HH, HL),
                                  ready=ready)
                    ff_mod_sum(pe, c, q)
            turns(pe, N_CHUNK, chunk)

        def ff_act(act):
            u0 = info("ff")["u0"]
            with act.Fori(0, N_CHUNK) as c:
                for j in range(KT):
                    s = j % 2
                    act.wait_ge(unit_done[s], c * 8 + (u0 // 2 + j // 2 + 1))
                    act.wait_ge(S("ff_lo"), c * 8 + (max(j - 1, 0) + 1))
                    act.activation(T2[s][:], G[s][:], ACT.Relu).then_inc(unit_freed[s], 1)
                    act.wait_ge(unit_freed[s], c * 8 + (u0 // 2 + j // 2 + 1))
                    act.activation(T2[s][:], T2[s][:], ACT.Square).then_inc(S("ff_sq"), 1)
                    act.wait_ge(S("ff_sq"), c * 8 + (j + 1))
                    act.activation(FH[:, j, :], T2[s][:], ACT.Copy).then_inc(S("ff_hi"), 1)

        def ff_dve(dve):
            u0 = info("ff")["u0"]
            dve.sem_inc(S("ff_lo"), 1)
            mod_begin(dve)
            with dve.Fori(0, N_CHUNK) as c:
                for j in range(KT):
                    ff_mod_rows(dve, c, j)
                    dve.wait_ge(S("ff_hi"), c * 8 + (j + 1))
                    dve.tensor_tensor(FL[:, j, :], T2[j % 2][:], FH[:, j, :].bitcast(F32),
                                      ALU.subtract).then_inc(S("ff_lo"), 1)
                    ff_mod_add(dve, c, j)
                for f in range(KT):
                    s = f % 2
                    ff_mod_rows(dve, c, KT + f)
                    dve.wait_ge(unit_done[s], c * 8 + (u0 // 2 + 4 + f // 2 + 1))
                    dve.wait_ge(unit_freed[s], c * 8 + (u0 // 2 + 4 + f // 2))
                    dve.scalar_tensor_tensor(out=X[:, f, :], in0=G[s][:], scalar=MODA[:, 40 + f:41 + f],
                                             in1=X[:, f, :], op0=ALU.mult, op1=ALU.add).then_inc(unit_freed[s], 1)
                    ff_mod_add(dve, c, KT + f)
            for s in range(2):
                dve.wait_ge(S(f"mod_read{s}"), N_CHUNK * PER_CHUNK + 1)
            for l, (mod, gain) in enumerate(((MODE, "e_norm"), (MODO, "o_norm"))):
                for c in range(2):
                    dve.scalar_tensor_tensor(out=GS[:, l, :, c], in0=mod[:, 8:16, c], scalar=1.0,
                                             in1=vec(gain, 0, 8), op0=ALU.add, op1=ALU.mult).then_inc(S("gs"), 1)

        def ff_sp(sp, r0):
            with sp.Fori(0, N_CHUNK) as c:
                for q in range(2 * KT):
                    s, f = q % 2, q % KT
                    src = A["w_ff1"][:, bass.ds(c * D + f * P, P)] if q < KT else \
                        A["w_ff2"][bass.ds(c * D, D), f * P:(f + 1) * P]
                    load_unit(sp, ff_r2(c, q), s, src.rearrange("(k p) n -> p k n", p=P), RAW[s][:])
                    if ff_mod(q):
                        w, _, _, j = ff_mod(q)
                        load_unit(sp, ff_r2(c, q) + 1, s, A[w][:, bass.ds(c * (PER_CHUNK * P) + j * P, P)]
                                  .rearrange("(k p) n -> p k n", p=P), RAW[s][:])

        stage("ff", dict(lead=lead_in("ff", SEQ, "ln1_lo"), act=ff_act, pe=ff_pe, dve=ff_dve, sp_free=ff_sp, pool=ff_pool),
              raw=[((8 + PER_CHUNK) * N_CHUNK, None)], units=16 * N_CHUNK)
        norm_stage("ln2", X, SEQ, True, "eps1", *ln_finish("ln2_g", "ln2_b"))

        def rms_h(tag, X_, T, layer, c):
            mod = (MODE, MODO)[layer]
            XN = [Z(f"XN{tag}{s}", [P, T], F32, 12 + 4 * s) for s in range(2)]

            def dve_(dve, tag, r):
                for f in range(KT + 1):
                    if f < KT:
                        if f >= 2:
                            dve.wait_ge(S(tag + "_t32"), f - 1)
                        dve.tensor_tensor(XN[f % 2][:], X_[:, f, :T], r[:, :T], ALU.mult).then_inc(S(tag + "_xn"), 1)
                    if f:
                        h_low(dve, tag, f - 1, T)

            def act_(act, tag):
                h_act(act, tag, S(tag + "_xn"), T, lambda f: XN[f % 2][:], lambda f: GS[:, layer, f, c:c + 1],
                      lambda f: mod[:, f, c:c + 1])
            norm_stage(tag, X_, T, False, "eps2", dve_, act_)

        def even_layer(tag, X_, T, c):
            rms_h(tag + "n", X_, T, 0, c)
            w = T + 2 * PAD
            U = Z(tag + "U", [P, 4, w], F32, 0)
            GA = Z(tag + "GA", [P, 4, T], F32, 17)
            VB = Z(tag + "VB", [P, 4, T], F32, 33)
            GB = Z(tag + "GB", [P, 4, T], F32, 49)
            ACC = Z(tag + "ACC", [P, T], F32, 65)
            SG = [Z(f"{tag}SG{s}", [P, T], F32, 69 + 3.5 * 0 + 4 * s) for s in range(1)]
            name = tag + "in"
            unit_cols = [x for j in range(4) for x in (512 + P * j, P * j)] + \
                [1536 + P * j for j in range(4)] + [2048 + P * j for j in range(4)] + [1024 + P * j for j in range(4)]

            def conv(dve, a, b):
                for q in range(a, b):
                    j, k = divmod(q, CONV_W)
                    src, wk = U[:, j, k:k + T], V[:, VEC["conv_w"] + j * CONV_W + k:VEC["conv_w"] + j * CONV_W + k + 1]
                    if q:
                        dve.wait_ge(S(name + "_tap"), q)
                    if k == 0:
                        dve.wait_ge(S(name + "_u"), 1 + j + 1)
                        if j:
                            dve.wait_ge(S(name + "_cv"), j)
                        dve.tensor_scalar(ACC[:], src, wk, vec("conv_b", j), ALU.mult, ALU.add)\
                           .then_inc(S(name + "_tap"), 1)
                    else:
                        dve.scalar_tensor_tensor(out=ACC[:], in0=src, scalar=wk, in1=ACC[:], op0=ALU.mult,
                                                 op1=ALU.add).then_inc(S(name + "_tap"), 1)
                    if k == CONV_W - 1:
                        dve.wait_ge(S(name + "_tap"), q + 1)
                        dve.tensor_copy(U[:, j, 0:T], ACC[:]).then_inc(S(name + "_cv"), 1)

            def in_dve(dve):
                u0 = info(name)["u0"]
                dve.memset(U[:, :, 0:PAD], 0.0).then_inc(S(name + "_pad"), 1)
                dve.memset(U[:, :, PAD + T:w], 0.0).then_inc(S(name + "_u"), 1)
                step = 0
                for j in range(4):
                    unit_ready(dve, u0 + 2 * j + 1)
                    dve.wait_ge(unit_freed[0], u0 // 2 + j + 1)
                    dve.tensor_tensor(U[:, j, PAD:PAD + T], G[1][:, :T], SG[0][:], ALU.mult)\
                       .then_inc(S(name + "_u"), 1)
                    dve.wait_ge(S(name + "_u"), j + 2)
                    dve.sem_inc(unit_freed[1], 1)
                    if j < 3:
                        conv(dve, step, step + 12)
                        step += 12
                conv(dve, step, 4 * CONV_W)

            def in_act(act):
                u0 = info(name)["u0"]
                for j in range(4):
                    unit_ready(act, u0 + 2 * j)
                    if j:
                        act.wait_ge(S(name + "_u"), j + 1)
                    act.activation(SG[0][:], G[0][:, :T], ACT.Sigmoid).then_inc(unit_freed[0], 1)
                for j in range(12):
                    U_ = u0 + 8 + j
                    unit_ready(act, U_)
                    dst = (VB, GB, GA)[j // 4][:, j % 4, :]
                    act.activation(dst, G[U_ % 2][:, :T], ACT.Copy if j < 4 else ACT.Silu)\
                       .then_inc(unit_freed[U_ % 2], 1)

            def unit_src(j):
                return A["e_w_in"][:, unit_cols[j]:unit_cols[j] + P].rearrange("(k p) n -> p k n", p=P)
            stage(name, dict(lead=lead_in(name, T, tag + "n_lo"), act=in_act, dve=in_dve,
                             pe=lambda pe: gemm_pairs(pe, info(name)["u0"], 10, T, (HH, HL), led=True)),
                  raw=[(1, lambda s, i, j=j: unit_src(2 * j + s)) for j in range(10)], units=20)

            n_tok = T // P
            half = T // 2
            VP = Z(tag + "VP", [P, n_tok, 512], F32, 80)
            VQ = Z(tag + "VQ", [P, n_tok, 512], F32, 112)
            FW = Z(tag + "FW", [P, 4, P], F32, 96)
            DFTD = Z(tag + "DFTD", [P, 256], F32, 98)
            PQ = Z(tag + "PQ", [P, 4, 2, P], F32, 99)
            EV = [Z(f"{tag}EV{s}", [P, half], F32, 69 + 2 * s) for s in range(2)]
            YB = Z(tag + "YB", [P, T], F32, 73)
            fn = tag + "fo"
            banks = [[G[j // 2][:, 512 * (j % 2):512 * (j % 2) + half] for j in range(4)],
                     [M[j // 2][:, 512 * (j % 2):512 * (j % 2) + half] for j in range(4)]]

            def fo_pe(pe):
                pe.wait_ge(moved, info(fn)["dma_end"])
                for q in range(2):
                    for g in range(4):
                        m = pe.matmul(M[q][:, g * P:(g + 1) * P], DFTD[:, q * P:(q + 1) * P], FW[:, g, :], start=True,
                                      stop=True)
                m.then_inc(S(fn + "_pq"), 1)
                pe.wait_ge(S(fn + "_pqs"), 2)
                for t in range(n_tok):
                    par, i = divmod(t, n_tok // 2)
                    if t >= 2:
                        pe.wait_ge(S(fn + "_v"), 2 * (t - 1))
                    first = 2 * P * i + par
                    for g in range(4):
                        m = pe.matmul(G[t % 2][:, g * 256:(g + 1) * 256], VB[:, g, first:first + 2 * P - 1:2],
                                      PQ[:, g, :, :].rearrange("p a b -> p (a b)"), start=True, stop=True)
                    m.then_inc(S(fn + "_vp"), 1)
                pe.wait_ge(S(fn + "_v"), 2 * n_tok)
                r0 = info(fn)["r0"]
                for t in range(n_tok):
                    par, i = divmod(t, n_tok // 2)
                    pe.wait_ge(raw_loaded[t % 2], 16 * ((r0 + t) // 2 + 1))
                    tab = RAW[t % 2][:].rearrange("p k n -> p (k n)")
                    for g in range(4):
                        for q, vv in enumerate((VP, VQ)):
                            m = pe.matmul(banks[par][g], vv[:, t, g * P:(g + 1) * P],
                                          tab[:, q * half:(q + 1) * half], start=(i == 0 and q == 0),
                                          stop=(i == n_tok // 2 - 1 and q == 1))
                    m.then_inc(raw_used[t % 2], 1)

            def fo_act(act):
                act.wait_ge(S(fn + "_pq"), 1)
                for q in range(2):
                    act.activation(PQ[:, :, q, :], M[q][:, 0:512].rearrange("p (g n) -> p g n", n=P), ACT.Copy,
                                   scale=float(T) ** -0.5).then_inc(S(fn + "_pqs"), 1)
                r0 = info(fn)["r0"]
                for s in range(2):
                    act.wait_ge(raw_used[s], (r0 + n_tok) // 2)
                for g in range(4):
                    if g >= 2:
                        act.wait_ge(S(fn + "_y"), 2 * (g - 1))
                    act.activation(EV[g % 2][:], banks[0][g], ACT.Copy).then_inc(S(fn + "_ev"), 1)
                    act.wait_ge(S(fn + "_gate"), g + 1)
                    act.activation(HH[:, 4 + g, :T], YB[:], ACT.Copy).then_inc(S(fn + "_hi"), 1)

            def fo_dve(dve):
                for t in range(n_tok):
                    dve.wait_ge(S(fn + "_vp"), t + 1)
                    both = G[t % 2][:].rearrange("p (g q n) -> p g q n", g=4, q=2)
                    for q, vv in enumerate((VP, VQ)):
                        dve.tensor_copy(vv[:, t, :].rearrange("p (g n) -> p g n", n=P), both[:, :, q, :])\
                           .then_inc(S(fn + "_v"), 1)
                r0 = info(fn)["r0"]
                for s in range(2):
                    dve.wait_ge(raw_used[s], (r0 + n_tok) // 2)
                for g in range(4):
                    dve.wait_ge(S(fn + "_ev"), g + 1)
                    if g:
                        dve.wait_ge(S(fn + "_lo"), g)
                    dve.tensor_tensor(YB[:, 0:half], banks[1][g], EV[g % 2][:], ALU.add).then_inc(S(fn + "_y"), 1)
                    dve.scalar_tensor_tensor(out=YB[:, half:T], in0=banks[1][g], scalar=-1.0, in1=EV[g % 2][:],
                                             op0=ALU.mult, op1=ALU.add).then_inc(S(fn + "_y"), 1)
                    dve.wait_ge(S(fn + "_y"), 2 * g + 2)
                    dve.tensor_tensor(YB[:], YB[:], GB[:, g, :], ALU.mult).then_inc(S(fn + "_gate"), 1)
                    dve.wait_ge(S(fn + "_hi"), g + 1)
                    dve.tensor_tensor(HL[:, 4 + g, :T], YB[:], HH[:, 4 + g, :T].bitcast(F32),
                                      ALU.subtract).then_inc(S(fn + "_lo"), 1)

            def dft_unit(t):
                return A[f"dft_{T}"][t * P:(t + 1) * P, :]

            def fo_sp(sp, r0):
                for t in range(n_tok):
                    load_unit(sp, (r0 + t) // 2, t % 2, dft_unit(t),
                              RAW[t % 2][:].rearrange("p k n -> p (k n)")[:, 0:T])
            stage(fn, dict(act=fo_act, pe=fo_pe, dve=fo_dve, sp_free=fo_sp), raw=[(n_tok // 2, None)],
                  dmas=[(FW[:], A["e_b_fw"].rearrange("g d e -> d g e")), (DFTD[:], A["dft_d"])])

            def ln_dve(dve, t_, r):
                for j in range(4):
                    dve.tensor_tensor(U[:, j, 0:T], U[:, j, 0:T], r[:, :T], ALU.mult).then_inc(S(t_ + "_xn"), 1)

            def ln_act(act, t_):
                for j in range(4):
                    act.wait_ge(S(t_ + "_xn"), j + 1)
                    act.activation(U[:, j, 0:T], U[:, j, 0:T], ACT.Silu, bias=vec("a_ln_b", j),
                                   scale=vec("a_ln_g", j)).then_inc(S(t_ + "_s"), 1)
            norm_stage(tag + "an", U, T, True, "eps2", ln_dve, ln_act, n_tiles=4,
                       sq=[Z(f"{tag}ASQ{s}", [P, T], F32, 33 + 4 * s) for s in range(2)],
                       r=Z(tag + "AR", [P, T], F32, 41))
            pn = tag + "pw"
            nt = max(1, T // 512)
            cw = T // nt

            def pw_pe(pe):
                r0 = info(pn)["r0"]
                for j in range(4):
                    pe.wait_ge(raw_loaded[j % 2], 16 * ((r0 + j) // 2 + 1))
                    if j >= 2:
                        pe.wait_ge(S(pn + "_g"), j - 1)
                    for k in range(4):
                        for n in range(nt):
                            m = pe.matmul(G[j % 2][:, n * cw:(n + 1) * cw], RAW[j % 2][:, k, :],
                                          U[:, k, n * cw:(n + 1) * cw], start=(k == 0), stop=(k == 3))
                    m.then_inc(raw_used[j % 2], 1)

            def pw_dve(dve):
                r0 = info(pn)["r0"]
                for j in range(4):
                    dve.wait_ge(raw_used[j % 2], (r0 + j) // 2 + 1)
                    dve.scalar_tensor_tensor(out=GA[:, j, :], in0=G[j % 2][:, :T], scalar=vec("pw_b", j),
                                             in1=GA[:, j, :], op0=ALU.add, op1=ALU.mult).then_inc(S(pn + "_g"), 1)
                    dve.wait_ge(S(pn + "_hi"), j + 1)
                    dve.tensor_tensor(HL[:, j, :T], GA[:, j, :], HH[:, j, :T].bitcast(F32),
                                      ALU.subtract).then_inc(S(pn + "_lo"), 1)

            def pw_act(act):
                for j in range(4):
                    act.wait_ge(S(pn + "_g"), j + 1)
                    act.activation(HH[:, j, :T], GA[:, j, :], ACT.Copy).then_inc(S(pn + "_hi"), 1)

            def pw_sp(sp, r0):
                for j in range(4):
                    load_unit(sp, (r0 + j) // 2, j % 2,
                              A["e_a_pw_w"][:, j * P:(j + 1) * P].rearrange("(k p) n -> p k n", p=P),
                              RAW[j % 2][:, 0:4, :])
            stage(pn, dict(act=pw_act, pe=pw_pe, dve=pw_dve, sp_free=pw_sp), raw=[(2, None)])
            out_stage(tag + "out", A["e_w_out"], T, X_, lambda f: MODE[:, 16 + f, c:c + 1],
                      (pn + "_lo", range(4), (pn + "_g", 3)))

        XC = Z("XC", [P, KT, CTX], F32, 22)
        CT = Z("CT", [P, 2, D], F32, 0)

        def cin_pe(pe):
            pe.wait_ge(moved, info("cin")["dma_end"])
            for q in range(4):
                if q >= 2:
                    pe.wait_ge(S("cin_x"), q - 1)
                for f in range(2 * q, 2 * q + 2):
                    for t in range(2):
                        m = pe.transpose(M[q % 2][:, 256 * (f % 2) + t * P:256 * (f % 2) + (t + 1) * P],
                                         CT[:, t, f * P:(f + 1) * P], IDENT[:])
                m.then_inc(S("cin_tr"), 1)

        def cin_dve(dve):
            for q in range(4):
                dve.wait_ge(S("cin_tr"), q + 1)
                dve.tensor_copy(XC[:, 2 * q:2 * q + 2, :].rearrange("p a b -> p (a b)"), M[q % 2][:, 0:512])\
                   .then_inc(S("cin_x"), 1)

        stage("cin", dict(pe=cin_pe, dve=cin_dve), dmas=[(CT[:, t, :], A["ctx"][t * P:(t + 1) * P, :]) for t in range(2)])

        O_Q, O_K, O_V, O_AG = 2048, 2560, 2688, 2816
        even_layer("c", XC, CTX, 1)
        rms_h("ckn", XC, CTX, 1, 1)
        CV = Z("CV", [P, CTX], F32, 0)

        def ckv_act(act):
            u0 = info("ckv")["u0"]
            for j, dst in enumerate((KC, CV)):
                unit_ready(act, u0 + j)
                act.activation(dst[:], G[j][:, 0:CTX], ACT.Copy).then_inc(unit_freed[j], 1)
            act.wait_ge(S("ckv_tr"), 1)
            act.activation(VC[:].rearrange("p a b -> p (a b)"), M[0][:, 0:CTX], ACT.Copy).then_inc(S("ckv_v"), 1)

        def ckv_pe(pe):
            u0 = info("ckv")["u0"]
            gemm_pairs(pe, u0, 1, CTX, (HH, HL), led=True)
            pe.wait_ge(unit_freed[1], u0 // 2 + 1)
            for t in range(2):
                m = pe.transpose(M[0][:, t * P:(t + 1) * P], CV[:, t * P:(t + 1) * P], IDENT[:])
            m.then_inc(S("ckv_tr"), 1)

        stage("ckv", dict(lead=lead_in("ckv", CTX, "ckn_lo"), act=ckv_act, pe=ckv_pe), raw=[(1, cols(A["o_w_in"], O_K))], units=2)

        even_layer("e", X, SEQ, 0)

        rms_h("on", X, SEQ, 1, 0)
        SX = Z("SX", [P, 4, SEQ + 2], F32, 0)
        CB = Z("CB", [P, 4, SEQ], F32, 16.25)
        OQ = Z("OQ", [P, 4, SEQ], F32, 32.25)
        OK = Z("OK", [P, SEQ], F32, 48.25)
        OV = Z("OV", [P, SEQ], F32, 52.25)
        AG = Z("AG", [P, 4, SEQ], F32, 56.25)
        TG = Z("TG", [P, SEQ], F32, 72.25)
        odd_units = [("s", c0 + P * j) for j in range(4) for c0 in (512, 1024)] + \
            [("b", c0 + P * j) for j in range(4) for c0 in (1536, 0)] + \
            [("q", O_Q + HEAD * j) for j in range(4)] + [("k", O_K), ("v", O_V)] + \
            [("g", O_AG + P * j) for j in range(4)]

        def odd_unit(j):
            kind, c0 = odd_units[j]
            w = A["o_w_in"]
            return w[:, c0:c0 + P].rearrange("(k p) n -> p k n", p=P)

        def odd_act(act):
            u0 = info("odd")["u0"]
            for j in range(26):
                kind = odd_units[j][0]
                if j < 16 and j % 2:
                    continue
                unit_ready(act, u0 + j)
                if j < 16:
                    if j:
                        act.wait_ge(S("odd_p"), j // 2)
                    act.activation(TG[:], G[0][:], ACT.Copy if kind == "s" else ACT.Silu).then_inc(unit_freed[0], 1)
                elif j < 22:
                    dst = OQ[:, j - 16, :] if j < 20 else (OK, OV)[j - 20][:]
                    act.activation(dst, G[j % 2][:], ACT.Copy).then_inc(unit_freed[j % 2], 1)
                else:
                    act.activation(AG[:, j - 22, :], G[j % 2][:], ACT.Silu).then_inc(unit_freed[j % 2], 1)

        def odd_dve(dve):
            u0 = info("odd")["u0"]
            dve.memset(SX[:, :, 0:1], 0.0).then_inc(S("odd_z"), 1)
            dve.memset(SX[:, :, SEQ + 1:SEQ + 2], 0.0).then_inc(S("odd_z"), 1)
            for j in range(8):
                unit_ready(dve, u0 + 2 * j + 1)
                dve.wait_ge(unit_freed[0], u0 // 2 + j + 1)
                dst = SX[:, j, 1:SEQ + 1] if j < 4 else CB[:, j - 4, :]
                dve.tensor_tensor(dst, G[1][:], TG[:], ALU.mult).then_inc(S("odd_p"), 1)
                dve.wait_ge(S("odd_p"), j + 1)
                dve.sem_inc(unit_freed[1], 1)

        def odd_sp(sp, r0):
            for j in range(26):
                view = RAW[j % 2][:]
                kind, c0 = odd_units[j]
                if kind == "q":
                    sp.wait_ge(raw_used[j % 2], (r0 + j) // 2)
                    sp.dma_start(view[:, :, 0:HEAD], A["o_w_in"][:, c0:c0 + HEAD].rearrange("(k p) n -> p k n", p=P))\
                      .then_inc(q_half, 16)
                    sp.wait_ge(q_half, 16 * (j - 15))
                    c0 += 4 * HEAD
                    sp.dma_start(view[:, :, HEAD:P], A["o_w_in"][:, c0:c0 + HEAD].rearrange("(k p) n -> p k n", p=P))\
                      .then_inc(raw_loaded[j % 2], 16)
                else:
                    load_unit(sp, (r0 + j) // 2, j % 2, odd_unit(j), view)

        stage("odd", dict(lead=lead_in("odd", SEQ, "on_lo"), act=odd_act, dve=odd_dve,
                          pe=lambda pe: gemm_pairs(pe, info("odd")["u0"], 13, SEQ, (HH, HL), led=True),
                          sp_free=odd_sp), raw=[(13, None)], units=26)

        WC, WS = Z("WC", [P, SEQ], F32, 96), Z("WS", [P, SEQ], F32, 100)
        OTMP = Z("OTMP", [P, SEQ], F32, 104)
        SWAPW = Z("SWAPW", [P, P], F32, 108)
        WVT = Z("WVT", [P, NT, P], F32, 72.25)
        YC = [Z(f"YC{s}", [P, SEQ], F32, 132 + 4 * s) for s in range(2)]
        QA = [Z(f"QA{h}", [P, SEQ], F32R, 4 * h) for h in range(N_Q)]
        KH2 = [Z(f"KH2_{g}", [P, SEQ], F32R, 128 + 4 * g) for g in range(2)]
        KL2 = [Z(f"KL2_{g}", [P, SEQ], F32R, 136 + 4 * g) for g in range(2)]
        KCH2 = [Z(f"KCH2_{g}", [P, CTX], F32R, 76.25 + g) for g in range(2)]
        KCL2 = [Z(f"KCL2_{g}", [P, CTX], F32R, 109 + g) for g in range(2)]

        def opre_pe(pe):
            for t in range(NT):
                m = pe.transpose(M[1][:, t * P:(t + 1) * P], OV[:, t * P:(t + 1) * P], IDENT[:])
            m.then_inc(S("ov_tr"), 1)
            pe.wait_ge(moved, info("opre")["dma_end"])
            for i in range(5):
                if i == 1:
                    pe.wait_ge(S("ov_out"), 1)
                swap_pe(pe, "or", i, OQ[:, i - 1, :] if i else OK[:], SWAPW[:])
            for s in range(2):
                pe.wait_ge(S(f"oj_moved{s}"), 32 * 4)
            pe.wait_ge(S("oj_last"), 8 * 16)

        def split_parts(j):
            if j == 0:
                return OK[:], KH2[0], KL2[0][:]
            if j == 1:
                return KC[:], KCH2[0], KCL2[0][:]
            return OQ[:, j - 2, :], QA[j - 2], OQ[:, j - 2, :].bitcast(F32R)

        def opre_dve(dve):
            for j in range(4):
                y = YC[j % 2][:]
                wk = [V[:, VEC["c_conv"] + 3 * j + k:VEC["c_conv"] + 3 * j + k + 1] for k in range(3)]
                if j >= 2:
                    dve.wait_ge(S("oc_lo"), j - 1)
                dve.tensor_scalar(y, SX[:, j, 0:SEQ], wk[0], None, ALU.mult).then_inc(S("oc_t"), 1)
                for k in (1, 2):
                    dve.wait_ge(S("oc_t"), 3 * j + k)
                    dve.scalar_tensor_tensor(out=y, in0=SX[:, j, k:k + SEQ], scalar=wk[k], in1=y, op0=ALU.mult,
                                             op1=ALU.add).then_inc(S("oc_t"), 1)
                dve.wait_ge(S("oc_t"), 3 * j + 3)
                dve.tensor_tensor(y, y, CB[:, j, :], ALU.mult).then_inc(S("oc_y"), 1)
                dve.wait_ge(S("oc_hi"), j + 1)
                dve.tensor_tensor(HL[:, j, :], y, HH[:, j, :].bitcast(F32), ALU.subtract).then_inc(S("oc_lo"), 1)
            dve.wait_ge(S("oc_lo"), 4)

            def low(j):
                src, hi, lo = split_parts(j)
                dve.wait_ge(S("oj_hi"), j + 1)
                dve.tensor_tensor(lo, src, hi[:].bitcast(F32), ALU.subtract).then_inc(S("oj_lo"), 1)
            rope_dve(dve, "or", 0, OK[:], WC[:], WS[:], OTMP[:])
            for j in range(4):
                rope_dve(dve, "or", j + 1, OQ[:, j, :], WC[:], WS[:], OTMP[:])
                for q in ((0, 1) if j == 0 else (j + 1,)):
                    low(q)
            low(5)

        def opre_act(act):
            act.wait_ge(S("ov_tr"), 1)
            act.activation(WVT[:].rearrange("p t n -> p (t n)"), M[1][:], ACT.Copy).then_inc(S("ov_out"), 1)

            for j in range(4):
                act.wait_ge(S("oc_y"), j + 1)
                act.activation(HH[:, j, :], YC[j % 2][:], ACT.Copy).then_inc(S("oc_hi"), 1)
            act.wait_ge(S("oc_lo"), 4)
            for j in range(6):
                src, hi, _ = split_parts(j)
                act.wait_ge(S("or_rot"), 2 if j < 2 else 2 * j)
                act.activation(hi[:], src, ACT.Copy).then_inc(S("oj_hi"), 1)

        def opre_sp(sp):
            low, high = slice(0, 64), slice(64, P)

            def move(dst, dst_rows, src, src_rows, signal):
                sp.dma_start(dst[dst_rows, :].bitcast(F32), src[src_rows, :].bitcast(F32)).then_inc(signal, 16)

            def out_of(j):
                sp.wait_ge(S("oj_lo"), j + 1)
                moved_j = S(f"oj_moved{j % 2}")
                if j < 2:
                    for two in ((KH2, KL2), (KCH2, KCL2))[j]:
                        move(two[1], high, two[0], high, moved_j)
                        move(two[1], low, two[0], high, moved_j)
                else:
                    move(QA[j + 2], high, QA[j - 2], high, moved_j)
                    move(QA[j + 2], low, OQ[:, j - 2, :], high, moved_j)

            def into(j):
                n = 64 + 32 * (j // 2) if j >= 2 else 64
                sp.wait_ge(S(f"oj_moved{j % 2}"), n)
                if j < 2:
                    for two in ((KH2, KL2), (KCH2, KCL2))[j]:
                        move(two[0], high, two[0], low, S("oj_last"))
                else:
                    move(QA[j - 2], high, OQ[:, j - 2, :], low, S("oj_last"))
            out_of(0)
            for j in range(1, 6):
                out_of(j)
                into(j - 1)
            into(5)

        stage("opre", dict(act=opre_act, pe=opre_pe, dve=opre_dve, sp_gated=opre_sp),
              dmas=[(WC[:], A["cos_win"]), (WS[:], A["sin_win"]), (SWAPW[:], A["swap_win"])])

        WATT = Z("WATT", [P, NT, 512], F32, 32.25)
        WP = [Z(f"WP{s}", [P, 640], F32, 96 + 2.5 * s) for s in range(2)]
        WPT = [Z(f"WPT{s}", [P, 640], F32, 101 + 2.5 * s) for s in range(2)]
        WNEG, WSUM, WSINK, WRDEN = [Z(n, [P, 2, N_Q], F32, 106 + 0.0625 * i)
                                    for i, n in enumerate(("WNEG", "WSUM", "WSINK", "WRDEN"))]
        WMAX = Z("WMAX", [P, 2, N_Q], F32, 106.25)
        NSINK = Z("NSINK", [P, N_Q], F32, 106.3125)
        SCALE_W = HEAD ** -0.5
        steps = [(n, h) for n in range(NT) for h in range(N_Q)]

        def span(n):
            return list(range(max(n - 1, 0), min(n + 2, NT)))

        def wa_pe(pe):
            def scores(i):
                n, h = steps[i]
                g = h // 4
                q = QA[h][:, n * P:(n + 1) * P]
                blocks = span(n)
                a = 512 - P * len(blocks)
                keys = slice(blocks[0] * P, (blocks[-1] + 1) * P)
                ps = G[i % 2]
                if i >= 2:
                    pe.wait_ge(S("wa_exp"), i - 1)
                pe.matmul(ps[:, a:512], q, KH2[g][:, keys], start=True, stop=False)
                pe.matmul(ps[:, a:512], q, KL2[g][:, keys], start=False, stop=False)
                pe.matmul(ps[:, 512:768], q, KCH2[g][:], start=True, stop=False)
                pe.matmul(ps[:, 512:768], q, KCL2[g][:], start=False, stop=True)
                if n > 0:
                    m = pe.matmul(ps[:, a:a + P], identb, before, start=False, stop=(n == NT - 1))
                if n < NT - 1:
                    m = pe.matmul(ps[:, 512 - P:512], identb, causal, start=False, stop=True)
                m.then_inc(S("wa_sc"), 1)

            def turn(i):
                n, h = steps[i]
                nb = len(span(n)) + 2
                pe.wait_ge(S("wa_exp"), i + 1)
                if i:
                    pe.wait_ge(S("wa_pt"), i)
                for b in range(nb):
                    m = pe.transpose(M[0][:, b * P:(b + 1) * P], WP[i % 2][:, b * P:(b + 1) * P], IDENT[:])
                m.then_inc(S("wa_tr"), 1)

            def values(i):
                n, h = steps[i]
                g = h // 4
                blocks = span(n)
                pe.wait_ge(S("wa_pt"), i + 1)
                if h == 0 and n >= 2:
                    pe.wait_ge(S("wa_att"), n - 1)
                c0 = 512 * (n % 2) + h * HEAD
                for b in range(len(blocks) + 2):
                    v = WVT[:, blocks[b], 64 * g:64 * g + 64] if b < len(blocks) else \
                        VC[:, b - len(blocks), 64 * g:64 * g + 64]
                    m = pe.matmul(M[1][:, c0:c0 + HEAD], WPT[i % 2][:, b * P:(b + 1) * P], v,
                                  start=(b == 0), stop=(b == len(blocks) + 1))
                m.then_inc(S("wa_pv"), 1)
            scores(0)
            for i in range(len(steps)):
                if i + 1 < len(steps):
                    scores(i + 1)
                if i:
                    values(i - 1)
                turn(i)
            values(len(steps) - 1)

        def wa_dve(dve):
            dve.tensor_scalar(NSINK[:], vec("sink", 0, N_Q), -1.0, None, ALU.mult).then_inc(S("wa_nsink"), 1)
            dve.wait_ge(S("wa_nsink"), 1)

            def smax(i):
                n, h = steps[i]
                a = 512 - P * len(span(n))
                x, neg = WMAX[:, n % 2, h:h + 1], WNEG[:, n % 2, h:h + 1]
                dve.wait_ge(S("wa_sc"), i + 1)
                dve.tensor_reduce(x, G[i % 2][:, a:768], AX.X, ALU.max).then_inc(S("wa_mx"), 1)
                dve.wait_ge(S("wa_mx"), i + 1)
                dve.tensor_scalar(neg, x, -SCALE_W, NSINK[:, h:h + 1], ALU.mult, ALU.min).then_inc(S("wa_neg"), 1)
                if h == N_Q - 1:
                    dve.wait_ge(S("wa_neg"), i + 1)
                    dve.tensor_tensor(WSINK[:, n % 2, :], WNEG[:, n % 2, :], NSINK[:], ALU.subtract)\
                       .then_inc(S("wa_sink"), 1)

            def tail(i):
                n, h = steps[i]
                w = (len(span(n)) + 2) * P
                dve.wait_ge(S("wa_tr"), i + 1)
                if i >= 2:
                    dve.wait_ge(S("wa_pv"), i - 1)
                dve.tensor_copy(WPT[i % 2][:, 0:w], M[0][:, 0:w]).then_inc(S("wa_pt"), 1)

            def put(n):
                dve.wait_ge(S("wa_es"), n + 1)
                dve.tensor_tensor(WRDEN[:, n % 2, :], WSUM[:, n % 2, :], WSINK[:, n % 2, :], ALU.add)\
                   .then_inc(S("wa_den"), 1)
                dve.wait_ge(S("wa_den"), 2 * n + 1)
                dve.reciprocal(WRDEN[:, n % 2, :], WRDEN[:, n % 2, :]).then_inc(S("wa_den"), 1)
                dve.wait_ge(S("wa_den"), 2 * n + 2)
                dve.wait_ge(S("wa_pv"), N_Q * (n + 1))
                dve.tensor_tensor(WATT[:, n, :].rearrange("p (h d) -> p h d", d=HEAD),
                                  M[1][:, 512 * (n % 2):512 * (n % 2) + 512].rearrange("p (h d) -> p h d", d=HEAD),
                                  WRDEN[:, n % 2, :].unsqueeze(2).broadcast_to([P, N_Q, HEAD]), ALU.mult)\
                   .then_inc(S("wa_att"), 1)
            smax(0)
            for i in range(len(steps)):
                n, h = steps[i]
                if i + 1 < len(steps):
                    smax(i + 1)
                tail(i)
                if n and h == 1:
                    put(n - 1)
            put(NT - 1)

        def wa_act(act):
            for i in range(len(steps)):
                n, h = steps[i]
                w = (len(span(n)) + 2) * P
                act.wait_ge(S("wa_neg"), i + 1)
                if i >= 2:
                    act.wait_ge(S("wa_tr"), i - 1)
                if h == 0 and n >= 2:
                    act.wait_ge(S("wa_att"), n - 1)
                act.activation(WP[i % 2][:, 0:w], G[i % 2][:, 768 - w:768], ACT.Exp, bias=WNEG[:, n % 2, h:h + 1],
                               scale=SCALE_W, accum_out=WSUM[:, n % 2, h:h + 1]).then_inc(S("wa_exp"), 1)
                if h == N_Q - 1:
                    act.wait_ge(S("wa_sink"), n + 1)
                    act.activation(WSINK[:, n % 2, :], WSINK[:, n % 2, :], ACT.Exp).then_inc(S("wa_es"), 1)

        stage("wa", dict(act=wa_act, pe=wa_pe, dve=wa_dve))
        turn_stage("oturn", WATT, 4, gate=AG, tmp=[Z(f"OT{s}", [P, SEQ], F32, 16.25 + 4 * s) for s in range(2)])
        out_stage("oout", A["o_w_out"], SEQ, X, lambda f: MODO[:, 16 + f, 0:1],
                  ("oturn_lo", range(4, KT)))

        OT = [Z(f"OUT{s}", [P, D], F32, 16 + 4 * s) for s in range(2)]

        def fin_dve(dve, tag, r):
            for f in range(KT):
                dve.scalar_tensor_tensor(out=X[:, f, :], in0=X[:, f, :], scalar=vec("final", f), in1=r[:],
                                         op0=ALU.mult, op1=ALU.mult).then_inc(S("fin_x"), 1)
        norm_stage("fin", X, SEQ, False, "eps2", fin_dve, lambda act, tag: None)

        def st_pe(pe):
            for t in range(NT):
                if t >= 2:
                    pe.wait_ge(S("st_o"), t - 1)
                for f in range(KT):
                    m = pe.transpose(M[t % 2][:, f * P:(f + 1) * P], X[:, f, t * P:(t + 1) * P], IDENT[:])
                m.then_inc(S("st_tr"), 1)

        def st_dve(dve):
            for t in range(NT):
                dve.wait_ge(S("st_tr"), t + 1)
                if t >= 2:
                    dve.wait_ge(S(f"stored{t % 2}"), 16 * (t // 2))
                dve.tensor_copy(OT[t % 2][:], M[t % 2][:]).then_inc(S("st_o"), 1)

        def st_act(act):
            for t in range(NT):
                act.wait_ge(S("st_o"), t + 1)
                act.dma_start(out[t * P:(t + 1) * P, :], OT[t % 2][:]).then_inc(S(f"stored{t % 2}"), 16)
            for s in range(2):
                act.wait_ge(S(f"stored{s}"), 16 * (NT // 2))

        stage("store", dict(act=st_act, pe=st_pe, dve=st_dve))

        block = ctx.enter_context(nc.Block())

        def gate(eng, n):
            for k in left:
                eng.wait_ge(left[k], n)

        def walk(eng, key):
            for n, st in enumerate(stages):
                current[0] = n
                if n:
                    gate(eng, n)
                    if key == "dve":
                        first = banks_of_signals[(n - 1) % 2][0].num
                        eng.sem_clear(range(first, first + BANK))
                if key in st["progs"]:
                    st["progs"][key](eng)
                if key == "pe" and n + 1 < len(stages) and "lead" in stages[n + 1]["progs"]:
                    stages[n + 1]["progs"]["lead"](eng)
                eng.drain().then_inc(left[key], 1)

        @block.sync
        def _(sp):
            for n, st in enumerate(stages):
                current[0] = n
                if "sp_gated" in st["progs"]:
                    gate(sp, n)
                    st["progs"]["sp_gated"](sp)
                if "sp_free" in st["progs"]:
                    st["progs"]["sp_free"](sp, st["r0"])
                    continue
                r = st["r0"]
                for n_pairs, src in st["raw"]:
                    if n_pairs == 1:
                        for s in range(2):
                            load_unit(sp, r // 2, s, src(s, 0), RAW[s][:])
                    else:
                        def pair(i, r=r, src=src):
                            for s in range(2):
                                load_unit(sp, i + r // 2, s, src(s, i), RAW[s][:])
                        turns(sp, n_pairs, pair)
                    r += 2 * n_pairs

        @block.gpsimd
        def _(pool):
            for n, st in enumerate(stages):
                current[0] = n
                if st["dmas"]:
                    if n:
                        gate(pool, n)
                    for dst, src in st["dmas"]:
                        pool.dma_start(dst, src).then_inc(moved, 16)
                if "pool" in st["progs"]:
                    st["progs"]["pool"](pool)
                elif st["units"]:
                    split_pairs(pool, st["r0"], st["u0"], st["units"] // 2, st["per_unit"])

        @block.scalar
        def _(act):
            walk(act, "act")

        @block.vector
        def _(dve):
            walk(dve, "dve")

        @block.tensor
        def _(pe):
            walk(pe, "pe")


def kernel(**inputs):
    import concourse.bacc as _bacc
    from concourse.bass_utils import run_bass_kernel_spmd as _run

    def tiles(a):
        a = np.asarray(a)
        return np.ascontiguousarray(a.reshape(-1, P).T)

    g = {k: np.asarray(v) for k, v in inputs.items()}
    const = shape_constants()
    two = np.stack([tiles(g["c_2"]), tiles(g["c_ctx_2"])], 2).reshape(P, 16)
    taps = lambda w: np.ascontiguousarray(w[0].reshape(w.shape[1], 4, P).transpose(2, 1, 0).reshape(P, -1))
    parts = {
        "c": tiles(g["c"]), "c2": two, "ln_in_g": tiles(g["ln_in_g"]), "ln_in_b": tiles(g["ln_in_b"]),
        "ln1_g": tiles(g["ln1_g"]), "ln1_b": tiles(g["ln1_b"]), "ln2_g": tiles(g["ln2_g"]),
        "ln2_b": tiles(g["ln2_b"]), "e_norm": tiles(g["e_norm_2"]), "o_norm": tiles(g["o_norm_2"]),
        "final": tiles(g["final_norm_2"]), "b_ada": tiles(g["b_ada"]), "e_b": tiles(g["e_b_mod_2"]),
        "o_b": tiles(g["o_b_mod_2"]), "q_norm": tiles(g["mla_q_norm"]), "kv_norm": tiles(g["mla_kv_norm"]),
        "gn_g": tiles(g["ret_gn_g"]), "gn_b": tiles(g["ret_gn_b"]), "conv_w": taps(g["e_a_conv_w_2"]),
        "conv_b": tiles(g["e_a_conv_b_2"]), "a_ln_g": tiles(g["e_a_ln_g_2"]), "a_ln_b": tiles(g["e_a_ln_b_2"]),
        "pw_b": tiles(g["e_a_pw_b_2"]), "c_conv": taps(g["o_c_conv_w_2"]),
        "sink": np.broadcast_to(g["o_sink_2"], (P, 8)), "zeta": const["cols"][:, 0:4],
        "inv_ret": const["cols"][:, 4:5], "inv_mla": const["cols"][:, 5:6], "g_chunk": const["cols"][:, 6:8],
        "eps1": const["cols"][:, 8:9], "eps2": const["cols"][:, 9:10],
    }
    arrays = {
        "vecs": np.concatenate([parts[n] for n, _ in VEC_PARTS], 1),
        "masks": mask_constants(),
        "x": g["x"][0], "ctx": g["ctx_2"][0], "positions": g["positions"],
        "w_ada": g["w_ada"][0], "w_in": g["w_in"][0], "w_uq": g["w_uq"][0], "w_ukv": g["w_ukv"][0],
        "w_out": g["w_out"][0], "w_ff1": g["w_ff1"][0], "w_ff2": g["w_ff2"][0],
        "e_w_mod": g["e_w_mod_2"][0], "e_w_in": g["e_w_in_2"][0], "e_a_pw_w": g["e_a_pw_w_2"][0],
        "e_b_fw": g["e_b_fw_2"][0], "e_w_out": g["e_w_out_2"][0], "o_w_mod": g["o_w_mod_2"][0],
        "o_w_in": g["o_w_in_2"][0], "o_w_out": g["o_w_out_2"][0],
    }
    arrays.update({k: v for k, v in const.items() if k != "cols"})
    nc = _bacc.Bacc("TRN2", target_bir_lowering=False, num_devices=1)
    named, args = {}, {}
    for name, a in arrays.items():
        a = np.ascontiguousarray(a)
        named[f"in_{name}"] = a
        args[name] = nc.dram_tensor(f"in_{name}", a.shape, mybir.dt.from_np(a.dtype), kind="ExternalInput").ap()
    out = nc.dram_tensor("out_0", (SEQ, D), F32, kind="ExternalOutput").ap()
    build_program(nc, args, out)
    r = _run(nc, [named], core_ids=[0])
    return r.results[0]["out_0"].reshape(1, SEQ, D)
```

```python
from contextlib import ExitStack

import concourse.bass as bass
import numpy as np
from concourse import mybir

F32 = mybir.dt.float32
F32R = mybir.dt.float32r
BF16 = mybir.dt.bfloat16
I32 = mybir.dt.int32
ALU = mybir.AluOpType
ACT = mybir.ActivationFunctionType
AX = mybir.AxisListType

P = 128
D = 1024
KT = D // P
SEQ = 1024
CTX = 256
D_FF = 4096
N_CHUNK = D_FF // D
MLA_HEADS, NOPE, ROPE, MLA_V = 8, 64, 32, 64
MLA_QK = NOPE + ROPE
RET_HEADS, RET_DK = 4, 64
N_Q, HEAD = 8, 64
GRID_W = 64
CONV_W = 31
PAD = CONV_W // 2
EPS_1, EPS_2 = 1e-5, 1e-6
ALPHA = 2.0 ** 0.25
IN_KR = 320
MAGIC = 1.5 * 2.0 ** 23
TWO_PI_PARTS = (6.28125, 0.0019350051879882812, 3.0199157663446e-07)
PI_SAFE = 3.1415925
NEG = -1e30

VEC_PARTS = [
    ("c", 8), ("c2", 16), ("ln_in_g", 8), ("ln_in_b", 8), ("ln1_g", 8), ("ln1_b", 8), ("ln2_g", 8), ("ln2_b", 8),
    ("e_norm", 8), ("o_norm", 8), ("b_ada", 48), ("e_b", 24), ("o_b", 24), ("q_norm", 2),
    ("kv_norm", 1), ("gn_g", 4), ("gn_b", 4), ("conv_w", 4 * CONV_W), ("conv_b", 4), ("a_ln_g", 4), ("a_ln_b", 4),
    ("pw_b", 4), ("c_conv", 12), ("sink", 8), ("zeta", 4), ("inv_ret", 1), ("inv_mla", 1), ("g_chunk", 2),
    ("eps1", 1), ("eps2", 1),
]
VEC, _at = {}, 0
for _name, _n in VEC_PARTS:
    VEC[_name] = _at
    _at += _n
N_VEC = _at


def shape_constants():
    f = np.float64
    out = {}
    out["ident"] = np.eye(P, dtype=np.float32)

    def pairs(period, half, lo, hi):
        m = np.zeros((P, P), np.float32)
        for d in range(lo, hi):
            if (d - lo) % period < half:
                m[d + half, d] = -1.0
            else:
                m[d - half, d] = 1.0
        return m

    out["swap_ret"] = pairs(64, 32, 0, P)
    out["swap_mla"] = pairs(32, 16, NOPE, MLA_QK)
    out["swap_win"] = pairs(32, 16, 0, P)
    log_g = np.log(1.0 - 2.0 ** (-5.0 - np.arange(RET_HEADS, dtype=f)))
    idx = np.arange(P, dtype=f)
    k_scale = RET_DK ** -0.5
    dec = np.zeros((P, RET_HEADS, P), f)
    for h in range(RET_HEADS):
        diff = idx[None, :] - idx[:, None]
        dec[:, 2 * (h % 2) + h // 2] = np.where(diff >= 0, np.exp(log_g[h] * np.maximum(diff, 0)), 0.0) * k_scale
    out["decay"] = dec.reshape(P, -1).astype(np.float32)
    xi = np.zeros((P, 2, P), f)
    for p in range(2):
        for hh in range(2):
            xi[64 * hh:64 * hh + 64, p] = np.exp(log_g[2 * p + hh] * (idx + 1.0))[None]
    out["xi"] = xi.reshape(P, -1).astype(np.float32)
    cols = np.zeros((P, 11), f)
    for h in range(RET_HEADS):
        cols[:, h] = np.exp(log_g[h] * (P - 1 - idx)) * k_scale
    inv32 = (np.float32(10000.0) ** (-np.arange(32, dtype=np.float32) / np.float32(32))).astype(np.float32)
    inv16 = (np.float32(10000.0) ** (-np.arange(16, dtype=np.float32) / np.float32(16))).astype(np.float32)
    cols[:, 4] = inv32[np.arange(P) % 32]
    cols[:, 5] = inv16[np.arange(P) % 16]
    for p in range(2):
        for hh in range(2):
            cols[64 * hh:64 * hh + 64, 6 + p] = np.exp(log_g[2 * p + hh] * P)
    cols[:, 8], cols[:, 9] = EPS_1, EPS_2
    out["cols"] = cols[:, :10].astype(np.float32)
    tok = np.arange(SEQ)
    where = np.stack([tok // GRID_W, tok % GRID_W]).astype(np.float32)
    d = np.arange(P) % HEAD
    ang = (where[d // 32] * inv16[d % 16][:, None]).astype(np.float32).astype(f)
    out["cos_win"], out["sin_win"] = np.cos(ang).astype(np.float32), np.sin(ang).astype(np.float32)
    n = np.arange(P, dtype=f)
    th = 2 * np.pi * (np.outer(n, n) % P) / P
    out["dft_d"] = np.concatenate([np.cos(th), -np.sin(th)], 1).astype(f) / np.sqrt(P)
    out["dft_d"] = out["dft_d"].astype(np.float32)
    for length in (SEQ, CTX):
        tiles = []
        for parity in range(2):
            for m in range(length // 2 // P):
                l = 2 * (m * P + np.arange(P)) + parity
                a = 2 * np.pi * (np.outer(l, np.arange(length // 2)) % length) / length
                tiles.append(np.concatenate([np.cos(a), np.sin(a)], 1))
        out[f"dft_{length}"] = np.concatenate(tiles).astype(np.float32)
    return out


def mask_constants():
    q, k = np.arange(P)[:, None], np.arange(P)[None, :]
    return np.concatenate([np.eye(P), np.where(k > q, NEG, 0.0), np.where(k < q, NEG, 0.0)], 1).astype(np.float32)


def build_program(nc, A, out):
    ctx = ExitStack()
    with ctx:
        BANK = 40
        banks_of_signals = [[ctx.enter_context(nc.semaphore(f"stage_signal_{b}_{i}")) for i in range(BANK)]
                            for b in range(2)]
        named = {}
        current = [0]

        def S(name):
            mine = named.setdefault(current[0], {})
            if name not in mine:
                mine[name] = banks_of_signals[current[0] % 2][len(mine)]
            return mine[name]

        def whole(name):
            return ctx.enter_context(nc.semaphore(name))

        base = 16640
        kb = 1024

        def at(name, shape, dt, offset):
            return nc.alloc_sbuf_tensor_at(name, shape, dt, offset=base + offset)

        X = at("X", [P, KT, SEQ], F32, 0)
        RAW = [at(f"RAW{s}", [P, KT, P], F32, 32 * kb + 4 * kb * s) for s in range(2)]
        WH = [at(f"WH{s}", [P, KT, P], F32R, 40 * kb + 4 * kb * s) for s in range(2)]
        WL = [at(f"WL{s}", [P, KT, P], F32R, 48 * kb + 4 * kb * s) for s in range(2)]
        small = [56 * kb]

        def keep(name, shape, dt):
            n = int(np.prod(shape[1:])) * (2 if dt == BF16 else 4)
            t = at(name, shape, dt, small[0])
            small[0] += (n + 31) // 32 * 32
            return t

        IDENT = keep("IDENT", [P, P], F32)
        ONES = keep("ONES", [P, P], F32)
        MASKS = keep("MASKS", [P, 3 * P], BF16)
        V = keep("V", [P, N_VEC], F32)
        MODA = keep("MODA", [P, 48], F32)
        MODE = keep("MODE", [P, 24, 2], F32)
        MODO = keep("MODO", [P, 24, 2], F32)
        CACT = keep("CACT", [P, 8], F32)
        C2ACT = keep("C2ACT", [P, 8, 2], F32)
        GS = keep("GS", [P, 2, 8, 2], F32)
        KC = keep("KC", [P, CTX], F32)
        VC = keep("VC", [P, 2, P], F32)
        BNS = keep("BNS", [P, 8, 4, 6], F32)
        MV = keep("MV", [P, 32, 2], F32)
        SD = keep("SD", [P, 32], F32)
        RS = keep("RS", [P, 32], F32)
        assert small[0] <= 64 * kb, small[0]
        z0 = small[0]
        assert base + z0 + 144 * kb <= 229368, base + z0 + 144 * kb

        def Z(name, shape, dt, offset_kb):
            return at(name, shape, dt, z0 + int(offset_kb * kb))

        HH = Z("HH", [P, KT, SEQ], F32R, 80)
        HL = Z("HL", [P, KT, SEQ], F32R, 112)
        T32 = [Z(f"T32_{s}", [P, SEQ], F32, 72 + 4 * s) for s in range(2)]

        G = [ctx.enter_context(nc.psum_tensor(f"G{s}", [P, 1024], F32)) for s in range(2)]
        M = [ctx.enter_context(nc.psum_tensor(f"M{s}", [P, 1024], F32)) for s in range(2)]

        raw_loaded = [whole(f"raw_loaded{s}") for s in range(2)]
        raw_used = [whole(f"raw_used{s}") for s in range(2)]
        w_split = [whole(f"w_split{s}") for s in range(2)]
        unit_done = [whole(f"unit_done{s}") for s in range(2)]
        unit_freed = [whole(f"unit_freed{s}") for s in range(2)]
        left = {k: whole(f"stages_left_by_{k}") for k in ("act", "pe", "dve")}
        w_high = whole("w_high")
        split_begun = whole("split_begun")
        q_half = whole("q_half")
        moved = whole("moved")

        def vec(name, i=0, n=1):
            return V[:, VEC[name] + i:VEC[name] + i + n]

        stages = []
        count = {"raw": 0, "unit": 0, "dma": 0}

        def stage(name, progs, raw=None, units=0, dmas=(), per_unit=1):
            n_raw = sum(2 * n for n, _ in raw or [])
            stages.append(dict(name=name, progs=progs, raw=raw or [], r0=count["raw"], u0=count["unit"],
                               units=units, per_unit=per_unit, dmas=list(dmas), dma_end=count["dma"] + 16 * len(dmas)))
            count["raw"] += n_raw
            count["unit"] += units
            count["dma"] += 16 * len(dmas)

        def info(name):
            return next(s for s in stages if s["name"] == name)

        def cols(w, c0):
            return lambda s, i: w[:, bass.ds(c0 + i * 256 + s * P, P)].rearrange("(k p) n -> p k n", p=P)

        def load_unit(sp, r2, s, src, view):
            need(sp, raw_used[s], r2)
            sp.dma_start(view, src).then_inc(raw_loaded[s], 16)

        def split_unit(pool, s, r2, u2):
            pool.wait_ge(raw_loaded[s], r2 * 16 + 16)
            need(pool, unit_done[s], u2)
            pool.sem_inc(split_begun, 1)
            pool.tensor_scalar(WH[s][:], RAW[s][:], 1.0, 0.0, ALU.mult, ALU.add).then_inc(w_high, 1)
            pool.wait_ge(w_high, u2 * 2 + s + 1)
            need(pool, w_split[s], u2)
            pool.tensor_tensor(WL[s][:], RAW[s][:], WH[s][:].bitcast(F32), ALU.subtract).then_inc(w_split[s], 1)
            pool.wait_ge(w_split[s], u2 + 1)
            pool.sem_inc(raw_used[s], 1)

        def split_pairs(pool, r0, u0, n_pairs, per_unit):
            turns(pool, n_pairs, lambda i: [split_unit(pool, s, i * per_unit + r0 // 2, i + u0 // 2)
                                            for s in range(2)])

        def gemm_unit(pe, s, u2, T, acts, order=range(KT), ready=None):
            hi, lo = acts
            nt = max(1, T // 512)
            w = T // nt
            pe.wait_ge(w_split[s], u2 + 1)
            need(pe, unit_freed[s], u2)
            for j, k in enumerate(order):
                if ready and k in ready:
                    pe.wait_ge(*ready[k])
                for part, moving in ((WH, hi), (WH, lo), (WL, hi)):
                    for n in range(nt):
                        m = pe.matmul(G[s][:, n * w:(n + 1) * w], part[s][:, k, :],
                                      moving[:, k, n * w:(n + 1) * w], start=(j == 0 and part is WH and moving is hi),
                                      stop=(j == KT - 1 and part is WL))
            m.then_inc(unit_done[s], 1)

        def lead_in(name, T, signal, tiles=range(KT), freed=None):
            def first_unit(pe):
                ready = {k: (S(signal), i + 1) for i, k in enumerate(tiles)}
                if freed:
                    pe.wait_ge(S(freed[0]), freed[1])
                gemm_unit(pe, 0, info(name)["u0"] // 2, T, (HH, HL),
                          [k for k in range(KT) if k not in ready] + list(tiles), ready)
            return first_unit

        def gemm_pairs(pe, u0, n_pairs, T, acts, after=None, led=False):
            def pair(i):
                for s in range(2):
                    if not (led and isinstance(i, int) and s == 0):
                        gemm_unit(pe, s, i + u0 // 2, T, acts)
                    if after:
                        after(pe, i, s)
            turns(pe, n_pairs, pair)

        def turns(eng, n, body):
            body(0)
            if n > 1:
                with eng.Fori(1, n) as i:
                    body(i)

        def need(eng, signal, value):
            if not isinstance(value, int) or value > 0:
                eng.wait_ge(signal, value)

        def unit_ready(eng, U):
            eng.wait_ge(unit_done[U % 2], U // 2 + 1)

        MP = Z("MP", [P, KT, P], F32, 72)
        MS = [Z(f"MS{s}", [P, 2, P], F32, 76 + s) for s in range(2)]

        def mod_begin(dve):
            dve.sem_inc(S("mod_rows"), 1)
            for s in range(2):
                dve.sem_inc(S(f"mod_read{s}"), 1)

        def mod_rows(dve, s, r2, n, xs):
            for c, x in enumerate(xs):
                dve.wait_ge(raw_loaded[s], r2 * 16 + 16)
                dve.wait_ge(S("mod_rows"), 2 * (n + c) + 1)
                dve.tensor_tensor(MP[:], RAW[s][:], x.unsqueeze(2).broadcast_to([P, KT, P]), ALU.mult)\
                   .then_inc(S("mod_rows"), 1)
                dve.wait_ge(S("mod_rows"), 2 * (n + c) + 2)
                dve.tensor_reduce(MS[s][:, c, :], MP[:].rearrange("p k n -> p n k"), AX.X, ALU.add)\
                   .then_inc(S("mod_rows"), 1)
            dve.sem_inc(raw_used[s], 1)
            dve.wait_ge(S("mod_rows"), 2 * (n + len(xs)) + 1)
            dve.sem_inc(S(f"mod_part{s}"), 1)

        def mod_sum(pe, s, n, width):
            pe.wait_ge(S(f"mod_part{s}"), n + 1)
            pe.wait_ge(S(f"mod_read{s}"), n + 1)
            for c in range(width):
                m = pe.matmul(M[s][:, c:c + 1], MS[s][:, c, :], ONES[:, 0:1], start=True, stop=True)
            m.then_inc(S(f"mod_sum{s}"), 1)

        def mod_add(dve, s, n, dst, bias):
            dve.wait_ge(S(f"mod_sum{s}"), n + 1)
            dve.tensor_scalar(dst, M[s][:, 0:dst.shape[-1]], bias, None, ALU.add).then_inc(S(f"mod_read{s}"), 1)

        def late_sum(pe, i, s):
            if s:
                mod_sum(pe, 0, i, 1)
            elif not isinstance(i, int):
                mod_sum(pe, 1, i - 1, 1)

        def ada_rows(dve, name, j):
            mod_rows(dve, j % 2, info(name)["r0"] // 2 + 2 * (j // 2) + 1, j, [CACT[:]])

        def ada_add(dve, first, j):
            mod_add(dve, j % 2, j // 2, MODA[:, first + j:first + j + 1], vec("b_ada", first + j))

        def with_ada(sp, r0, n, unit, first):
            for j in range(n):
                r2 = r0 // 2 + 2 * (j // 2)
                load_unit(sp, r2, j % 2, unit(j), RAW[j % 2][:])
                c0 = (first + j) * P
                load_unit(sp, r2 + 1, j % 2, A["w_ada"][:, c0:c0 + P].rearrange("(k p) n -> p k n", p=P),
                          RAW[j % 2][:])

        def h_act(act, tag, ready, T, src, scale, shift, hh=None):
            for f in range(KT):
                act.wait_ge(ready, f + 1)
                if f >= 2:
                    act.wait_ge(S(tag + "_lo"), f - 1)
                act.activation(T32[f % 2][:, :T], src(f), ACT.Identity, bias=shift(f),
                               scale=scale(f)).then_inc(S(tag + "_t32"), 1)
                act.wait_ge(S(tag + "_t32"), f + 1)
                act.activation(HH[:, f, :T], T32[f % 2][:, :T], ACT.Copy).then_inc(S(tag + "_hi"), 1)

        def h_low(dve, tag, f, T):
            dve.wait_ge(S(tag + "_hi"), f + 1)
            dve.tensor_tensor(HL[:, f, :T], T32[f % 2][:, :T], HH[:, f, :T].bitcast(F32),
                              ALU.subtract).then_inc(S(tag + "_lo"), 1)

        XT = Z("XT", [P, KT, D], F32, 0)
        NT = SEQ // P
        MASK32 = Z("MASK32", [P, 3 * P], F32, 128)
        ADA = [Z(f"ADA{g}", [P, KT, 512], F32, 64 + 16 * g if g < 4 else 32 + 16 * (g - 4)) for g in range(6)]

        def start_sp(sp, r0):
            for t in range(NT):
                sp.dma_start(XT[:, t, :], A["x"][t * P:(t + 1) * P, :]).then_inc(S("x_in"), 16)
            for g in range(6):
                sp.dma_start(ADA[g][:], A["w_ada"][:, 512 * g:512 * g + 512].rearrange("(k p) n -> p k n", p=P))\
                  .then_inc(S(f"ada{g}"), 16)

        def start_dve(dve):
            dve.memset(ONES[:], 1.0).then_inc(S("ones"), 1)
            dve.wait_ge(moved, info("start")["dma_end"])
            dve.wait_ge(S("c_act"), 2)
            dve.tensor_copy(MASKS[:], MASK32[:]).then_inc(S("masks"), 1)
            g4 = V[:, VEC["ln_in_g"]:VEC["ln_in_g"] + 4 * KT]
            dve.tensor_scalar(g4, g4, ALPHA, None, ALU.mult).then_inc(S("masks"), 1)
            dve.wait_ge(S("x_in"), 16 * NT)
            for t in range(NT):
                for j in range(2):
                    dve.bn_stats(BNS[:, t, j, :], XT[:, t, 512 * j:512 * j + 512]).then_inc(S("li_st"), 1)
                dve.wait_ge(S("li_st"), 2 * t + 2)
                dve.bn_aggr(MV[:, t, :], BNS[:, t, 0:2, :].rearrange("p a b -> p (a b)")).then_inc(S("li_mv"), 1)
            dve.wait_ge(S("li_sd"), 1)
            dve.reciprocal(RS[:, 0:NT], SD[:, 0:NT]).then_inc(S("li_rs"), 1)
            dve.wait_ge(S("li_rs"), 1)
            for t in range(NT):
                dve.tensor_scalar(XT[:, t, :], XT[:, t, :], MV[:, t, 0:1], RS[:, t:t + 1], ALU.subtract,
                                  ALU.mult).then_inc(S("li_xn"), 1)
            prod = X[:, 0:4, :].rearrange("p a (b n) -> p (a b) n", n=512)
            for i, g in enumerate((0, 3)):
                dve.wait_ge(S(f"ada{g}"), 16)
                if i:
                    dve.wait_ge(S("ada_rows"), 2)
                dve.tensor_tensor(prod, ADA[g][:], CACT[:].unsqueeze(2).broadcast_to([P, KT, 512]), ALU.mult)\
                   .then_inc(S("ada_rows"), 1)
                dve.wait_ge(S("ada_rows"), 2 * i + 1)
                dve.tensor_reduce(X[:, 4 + i, 0:512], prod.rearrange("p k n -> p n k"), AX.X, ALU.add)\
                   .then_inc(S("ada_rows"), 1)
            dve.wait_ge(S("ada_sum"), 4)
            dve.tensor_tensor(MODA[:, 0:16], G[0][:, 0:16], vec("b_ada", 0, 16), ALU.add).then_inc(S("mod_in"), 1)
            dve.wait_ge(S("mod_in"), 1)
            dve.tensor_scalar(MODA[:, 8:16], MODA[:, 8:16], 1.0, 1.0 / ALPHA, ALU.add, ALU.mult).then_inc(S("mod_in"), 1)
            for f in range(KT):
                dve.wait_ge(S("li_tr"), f + 1)
                dve.tensor_scalar(X[:, f, :], M[f % 2][:], vec("ln_in_g", f), vec("ln_in_b", f), ALU.mult,
                                  ALU.add).then_inc(S("li_x"), 1)
                if f:
                    h_low(dve, "li", f - 1, SEQ)
            h_low(dve, "li", KT - 1, SEQ)
            dve.wait_ge(S("ada_sum"), 6)
            dve.tensor_tensor(MODA[:, 16:24], G[1][:, 0:8], vec("b_ada", 16, 8), ALU.add).then_inc(S("mod_in"), 1)

        def start_act(act):
            act.wait_ge(moved, info("start")["dma_end"])
            act.activation(CACT[:], vec("c", 0, 8), ACT.Silu).then_inc(S("c_act"), 1)
            act.activation(C2ACT[:].rearrange("p k c -> p (k c)"), vec("c2", 0, 16), ACT.Silu).then_inc(S("c_act"), 1)
            act.wait_ge(S("li_mv"), NT)
            act.activation(SD[:, 0:NT], MV[:, 0:NT, 1], ACT.Sqrt, bias=vec("eps1"), scale=1.0).then_inc(S("li_sd"), 1)
            act.wait_ge(S("mod_in"), 2)
            h_act(act, "li", S("li_x"), SEQ, lambda f: X[:, f, :], lambda f: MODA[:, 8 + f:9 + f],
                  lambda f: MODA[:, f:f + 1])

        def start_pe(pe):
            def ada(g):
                pe.wait_ge(S(f"ada{g}"), 16)
                for u in range(4):
                    col = 4 * (g % 4) + u
                    for k in range(KT):
                        m = pe.matmul(G[g // 4][:, col:col + 1], ADA[g][:, k, u * P:(u + 1) * P], CACT[:, k:k + 1],
                                      start=(k == 0), stop=(k == KT - 1))
                m.then_inc(S("ada_sum"), 1)
            pe.wait_ge(S("c_act"), 2)
            for g in (1, 2):
                ada(g)
            for i, g in enumerate((0, 3)):
                pe.wait_ge(S("ada_rows"), 2 * i + 2)
                for u in range(4):
                    m = pe.matmul(G[0][:, 4 * g + u:4 * g + u + 1], X[:, 4 + i, u * P:(u + 1) * P], ONES[:, 0:1],
                                  start=True, stop=True)
                m.then_inc(S("ada_sum"), 1)
            pe.wait_ge(S("li_xn"), NT)
            for f in range(KT):
                if f >= 2:
                    pe.wait_ge(S("li_x"), f - 1)
                for t in range(NT):
                    m = pe.transpose(M[f % 2][:, t * P:(t + 1) * P], XT[:, t, f * P:(f + 1) * P], IDENT[:])
                m.then_inc(S("li_tr"), 1)
            for g in (4, 5):
                ada(g)

        stage("start", dict(act=start_act, pe=start_pe, dve=start_dve, sp_free=start_sp), raw=[(0, None)],
              dmas=[(V[:], A["vecs"]), (IDENT[:], A["ident"]), (MASK32[:], A["masks"])])

        QC = Z("QC", [P, 2, SEQ], F32, 0)
        KVC = Z("KVC", [P, SEQ], F32, 8)
        KR = Z("KR", [P, SEQ], F32, 12)
        RQ = Z("RQ", [P, 2, SEQ], F32, 16)
        RK = Z("RK", [P, 2, SEQ], F32, 24)
        RV = Z("RV", [P, 4, SEQ], F32, 32)
        RG = Z("RG", [P, 4, SEQ], F32, 48)
        WIN_COLS = [0, 128, 256, IN_KR, 416, 544, 672, 800] + [928 + 128 * i for i in range(4)] + \
            [1440 + 128 * i for i in range(4)]
        win_dst = [QC[:, 0, :], QC[:, 1, :], KVC[:], KR[:], RQ[:, 0, :], RQ[:, 1, :], RK[:, 0, :], RK[:, 1, :]] + \
            [RV[:, i, :] for i in range(4)]

        ANGR, ANGM = Z("ANGR", [P, SEQ], F32, 64), Z("ANGM", [P, SEQ], F32, 68)
        POSI = Z("POSI", [P, SEQ], I32, 68)
        TURN = Z("TURN", [P, 512], F32, 78)

        def angles(dve, q, half):
            inv, ang = (("inv_ret", ANGR), ("inv_mla", ANGM))[q]
            c = slice(512 * half, 512 * half + 512)
            n = [8 * (2 * q + half)]

            def step(ins):
                ins.then_inc(S("ang"), 1)
                n[0] += 1
                dve.wait_ge(S("ang"), n[0])
            step(dve.tensor_copy(TURN[:], POSI[:, c]))
            step(dve.tensor_scalar(ang[:, c], TURN[:], vec(inv), None, ALU.mult))
            step(dve.tensor_scalar(TURN[:], ang[:, c], 1.0 / (2.0 * np.pi), MAGIC, ALU.mult, ALU.add))
            step(dve.tensor_scalar(TURN[:], TURN[:], -MAGIC, None, ALU.add))
            for part in TWO_PI_PARTS:
                step(dve.scalar_tensor_tensor(out=ang[:, c], in0=TURN[:], scalar=-part, in1=ang[:, c], op0=ALU.mult,
                                              op1=ALU.add))
            step(dve.tensor_scalar(ang[:, c], ang[:, c], PI_SAFE, -PI_SAFE, ALU.min, ALU.max))

        def win_dve(dve):
            u0 = info("win")["u0"]
            mod_begin(dve)
            for j, dst in enumerate(win_dst):
                ada_rows(dve, "win", j)
                unit_ready(dve, u0 + j)
                dve.tensor_copy(dst, G[j % 2][:]).then_inc(unit_freed[j % 2], 1)
                if j:
                    ada_add(dve, 24, j - 1)
                if j == 4:
                    dve.wait_ge(S("pos_in"), 16)
                if 4 <= j < 8:
                    angles(dve, (j - 4) // 2, j % 2)
            for j in range(12, 16):
                ada_rows(dve, "win", j)
                ada_add(dve, 24, j - 1)
            ada_add(dve, 24, 15)
            for s in range(2):
                dve.wait_ge(S(f"mod_read{s}"), 8 + 1)
            dve.tensor_scalar(MODA[:, 32:40], MODA[:, 32:40], 1.0, 1.0 / ALPHA, ALU.add, ALU.mult).then_inc(S("one_plus"), 1)

        def win_act(act):
            u0 = info("win")["u0"]
            act.dma_start(POSI[:], A["positions"].broadcast_to([P, SEQ])).then_inc(S("pos_in"), 16)
            for j in range(12, 16):
                unit_ready(act, u0 + j)
                act.activation(RG[:, j - 12, :], G[j % 2][:], ACT.Silu).then_inc(unit_freed[j % 2], 1)

        def win_unit(j):
            return A["w_in"][:, WIN_COLS[j]:WIN_COLS[j] + P].rearrange("(k p) n -> p k n", p=P)

        def win_pe(pe):
            gemm_pairs(pe, info("win")["u0"], 8, SEQ, (HH, HL), led=True, after=late_sum)
            mod_sum(pe, 1, 7, 1)

        stage("win", dict(lead=lead_in("win", SEQ, "li_lo"), act=win_act, pe=win_pe, dve=win_dve, sp_free=lambda sp, r0: with_ada(sp, r0, 16, win_unit, 24)),
              raw=[(16, None)], units=16, per_unit=2)

        COSR, SINR = Z("COSR", [P, SEQ], F32, 112), Z("SINR", [P, SEQ], F32, 116)
        COSM, SINM = Z("COSM", [P, SEQ], F32, 120), Z("SINM", [P, SEQ], F32, 124)
        LSQ = [Z(f"LSQ{s}", [P, SEQ], F32, 96 + 4 * s) for s in range(3)]
        LR = [Z(f"LR{s}", [P, SEQ], F32, 80 + 4 * s) for s in range(2)]
        SWAPR = Z("SWAPR", [P, P], F32, 88)
        DECAY = Z("DECAY", [P, 512], F32, 89)
        XI = Z("XI", [P, 2, P], F32, 91)
        SWAPM = Z("SWAPM", [P, P], F32, 92)

        def trig_act(act):
            for i, t in enumerate((QC[:, 0, :], QC[:, 1, :], KVC[:])):
                act.activation(LSQ[i][:], t, ACT.Square).then_inc(S("lat_sq"), 1)
            for q, (ang, sin, cos) in enumerate(((ANGR, SINR, COSR), (ANGM, SINM, COSM))):
                act.activation(sin[:], ang[:], ACT.Sin).then_inc(S("tr_sin"), 1)
                act.activation(cos[:], ang[:], ACT.Sin, scale=0.5).then_inc(S("tr_sin"), 1)
                act.wait_ge(S("tr_sin"), 3 * q + 2)
                act.activation(cos[:], cos[:], ACT.Square).then_inc(S("tr_sin"), 1)
            for i, n in enumerate((256, 128)):
                act.wait_ge(S("lat_ms"), i + 1)
                act.activation(LR[i][:], M[i][:], ACT.Sqrt, bias=vec("eps1"), scale=1.0 / n).then_inc(S("lat_sd"), 1)

        def trig_pe(pe):
            for i, tiles in enumerate(((0, 1), (2,))):
                pe.wait_ge(S("lat_sq"), 2 + i)
                for n in range(2):
                    for k in tiles:
                        m = pe.matmul(M[i][:, 512 * n:512 * n + 512], ONES[:], LSQ[k][:, 512 * n:512 * n + 512],
                                      start=(k == tiles[0]), stop=(k == tiles[-1]))
                m.then_inc(S("lat_ms"), 1)

        def trig_dve(dve):
            for q, cos in enumerate((COSR, COSM)):
                dve.wait_ge(S("tr_sin"), 3 * q + 3)
                dve.tensor_scalar(cos[:], cos[:], -2.0, 1.0, ALU.mult, ALU.add).then_inc(S("tr_cos"), 1)
            for i in range(2):
                dve.wait_ge(S("lat_sd"), i + 1)
                dve.reciprocal(LR[i][:], LR[i][:]).then_inc(S("lat_r"), 1)
                dve.wait_ge(S("lat_r"), i + 1)
                for k, t in (((0, QC[:, 0, :]), (1, QC[:, 1, :])) if i == 0 else ((0, KVC[:]),)):
                    dve.scalar_tensor_tensor(out=t, in0=t, scalar=vec("q_norm" if i == 0 else "kv_norm", k),
                                             in1=LR[i][:], op0=ALU.mult, op1=ALU.mult).then_inc(S("lat_n"), 1)

        stage("trig", dict(act=trig_act, pe=trig_pe, dve=trig_dve),
              dmas=[(SWAPR[:], A["swap_ret"]), (DECAY[:], A["decay"]), (XI[:].rearrange("p a b -> p (a b)"), A["xi"]),
                    (SWAPM[:], A["swap_mla"])])

        def swap_pe(pe, tag, i, tile, swap):
            if i >= 2:
                pe.wait_ge(S(tag + "_mul"), i - 1)
            for n in range(2):
                m = pe.matmul(M[i % 2][:, 512 * n:512 * n + 512], swap, tile[:, 512 * n:512 * n + 512],
                              start=True, stop=True)
            m.then_inc(S(tag + "_sw"), 1)

        def rope_dve(dve, tag, i, tile, cos, sin, tmp):
            dve.wait_ge(S(tag + "_sw"), i + 1)
            if i:
                dve.wait_ge(S(tag + "_rot"), 2 * i)
            dve.tensor_tensor(tmp, M[i % 2][:], sin, ALU.mult).then_inc(S(tag + "_mul"), 1)
            dve.tensor_tensor(tile, tile, cos, ALU.mult).then_inc(S(tag + "_rot"), 1)
            dve.wait_ge(S(tag + "_mul"), i + 1)
            dve.wait_ge(S(tag + "_rot"), 2 * i + 1)
            dve.tensor_tensor(tile, tile, tmp, ALU.add).then_inc(S(tag + "_rot"), 1)

        VT = Z("VT", [P, NT, 512], F32, 64)
        KZ = Z("KZ", [P, NT, 256], F32, 80)
        QX = [Z(f"QX{s}", [P, 2, P], F32, 104 + s) for s in range(2)]
        STATE = [Z(f"STATE{s}", [P, 2, 256], F32, 112 + 2 * s) for s in range(2)]
        SCT = [Z(f"SCT{s}", [P, 512], F32, 116 + 2 * s) for s in range(2)]
        RTMP = Z("RTMP", [P, SEQ], F32, 100)

        turned = [(t[:, j, :], SWAPR, COSR, SINR) for t in (RQ, RK) for j in range(2)] + [(KR[:], SWAPM, COSM, SINM)]

        def rpre_pe(pe):
            pe.wait_ge(moved, info("trig")["dma_end"])
            for i, (tile, swap, _, _) in enumerate(turned):
                swap_pe(pe, "rr", i, tile, swap[:])
            for j in range(4):
                pe.wait_ge(S("rr_mul"), 5 if j == 0 else 4)
                if j >= 2:
                    pe.wait_ge(S("rv_out"), j - 1)
                for t in range(NT):
                    m = pe.transpose(M[j % 2][:, t * P:(t + 1) * P], RV[:, j, t * P:(t + 1) * P], IDENT[:])
                m.then_inc(S("rv_tr"), 1)
            pe.wait_ge(S("rr_rot"), 8)
            for j in range(2):
                pe.wait_ge(S("rv_out"), 3 + j)
                for t in range(NT):
                    m = pe.transpose(M[j][:, t * P:(t + 1) * P], RK[:, j, t * P:(t + 1) * P], IDENT[:])
                m.then_inc(S("rk_tr"), 1)

        def rpre_dve(dve):
            for i, (tile, _, cos, sin) in enumerate(turned):
                rope_dve(dve, "rr", i, tile, cos[:], sin[:], RTMP[:])
            for j in range(4):
                dve.wait_ge(S("rv_tr"), j + 1)
                dve.tensor_copy(VT[:, :, j * P:(j + 1) * P], M[j % 2][:].rearrange("p (t n) -> p t n", n=P))\
                   .then_inc(S("rv_out"), 1)

        def rpre_act(act):
            for j in range(2):
                act.wait_ge(S("rk_tr"), j + 1)
                for hh in range(2):
                    act.activation(KZ[:, :, j * P + 64 * hh:j * P + 64 * hh + 64],
                                   M[j][:].rearrange("p (t n) -> p t n", n=P)[:, :, 64 * hh:64 * hh + 64],
                                   ACT.Copy, scale=vec("zeta", 2 * j + hh)).then_inc(S("kz"), 1)

        stage("rpre", dict(act=rpre_act, pe=rpre_pe, dve=rpre_dve))

        def in_bank(ps, h):
            return ps[:, 512 * (h % 2) + P * (h // 2):512 * (h % 2) + P * (h // 2) + P]

        def ret_pe(pe):
            def scores(c):
                if c >= 2:
                    pe.wait_ge(S("ret_dec"), c - 1)
                    pe.wait_ge(S("ret_state"), 2 * c - 2)
                for p in range(2):
                    pe.matmul(G[c % 2][:, 512 * p + 256:512 * p + 512], KZ[:, c, p * P:(p + 1) * P],
                              VT[:, c, p * 256:(p + 1) * 256], start=True, stop=True)
                t = slice(c * P, (c + 1) * P)
                for h in range(RET_HEADS):
                    r = slice(64 * (h % 2), 64 * (h % 2) + 64)
                    m = pe.matmul(in_bank(G[c % 2], h), RK[r, h // 2, t], RQ[r, h // 2, t], start=True, stop=True)
                m.then_inc(S("ret_sc"), 1)
            scores(0)
            for c in range(NT):
                if c + 1 < NT:
                    scores(c + 1)
                pe.wait_ge(S("ret_dec"), c + 1)
                if c >= 2:
                    pe.wait_ge(S("ret_out"), c - 1)
                if c:
                    pe.wait_ge(S("ret_qx"), 2 * c)
                    pe.wait_ge(S("ret_state"), 2 * c)
                for h in range(RET_HEADS):
                    r = slice(64 * (h % 2), 64 * (h % 2) + 64)
                    q = 2 * (h % 2) + h // 2
                    m = pe.matmul(in_bank(M[c % 2], h), SCT[c % 2][:, q * P:(q + 1) * P], VT[:, c, h * P:(h + 1) * P],
                                  start=True, stop=(c == 0))
                    if c:
                        m = pe.matmul(in_bank(M[c % 2], h), QX[c % 2][r, h // 2, :],
                                      STATE[(c - 1) % 2][r, h // 2, P * (h % 2):P * (h % 2) + P], start=False,
                                      stop=True)
                m.then_inc(S("ret_o"), 1)

        def ret_dve(dve):
            def statistics(c):
                dve.wait_ge(S("ret_out"), c + 1)
                for h in range(RET_HEADS):
                    dve.bn_stats(BNS[:, c, h, :], VT[:, c, h * P:(h + 1) * P]).then_inc(S("ret_st"), 1)
                dve.wait_ge(S("ret_st"), 4 * c + 4)
                for h in range(RET_HEADS):
                    dve.bn_aggr(MV[:, 4 * c + h, :], BNS[:, c, h, :]).then_inc(S("ret_mv"), 1)

            for c in range(NT):
                dve.wait_ge(S("ret_sc"), c + 1)
                if c >= 2:
                    dve.wait_ge(S("ret_o"), c - 1)
                dve.tensor_tensor(SCT[c % 2][:].rearrange("p (o n) -> p o n", o=2),
                                  G[c % 2][:].rearrange("p (o n) -> p o n", o=2)[:, :, 0:256],
                                  DECAY[:].rearrange("p (o n) -> p o n", o=2), ALU.mult).then_inc(S("ret_dec"), 1)
                if c:
                    for p in range(2):
                        dve.tensor_tensor(QX[c % 2][:, p, :], RQ[:, p, c * P:(c + 1) * P], XI[:, p, :],
                                          ALU.mult).then_inc(S("ret_qx"), 1)
                if c + 1 < NT:
                    for p in range(2):
                        kv = G[c % 2][:, 512 * p + 256:512 * p + 512]
                        if c == 0:
                            dve.tensor_copy(STATE[0][:, p, :], kv).then_inc(S("ret_state"), 1)
                        else:
                            dve.wait_ge(S("ret_state"), 2 * c)
                            dve.wait_ge(S("ret_o"), c)
                            dve.scalar_tensor_tensor(out=STATE[c % 2][:, p, :], in0=STATE[(c - 1) % 2][:, p, :],
                                                     scalar=vec("g_chunk", p), in1=kv, op0=ALU.mult,
                                                     op1=ALU.add).then_inc(S("ret_state"), 1)
                if c > 1:
                    statistics(c - 2)
            for c in (NT - 2, NT - 1):
                statistics(c)
            dve.wait_ge(S("ret_sd"), 1)
            dve.reciprocal(RS[:], SD[:]).then_inc(S("ret_rs"), 1)
            dve.wait_ge(S("ret_rs"), 1)
            for h in range(RET_HEADS):
                for c in range(NT):
                    o = VT[:, c, h * P:(h + 1) * P]
                    q = 4 * c + h
                    dve.tensor_scalar(o, o, MV[:, q, 0:1], RS[:, q:q + 1], ALU.subtract, ALU.mult)\
                       .then_inc(S("ret_n"), 1)
            for h in range(RET_HEADS):
                dve.wait_ge(S("ret_t32"), h + 1)
                dve.tensor_tensor(RG[:, h, :], T32R[h % 2][:], RG[:, h, :], ALU.mult).then_inc(S("ret_gate"), 1)
                dve.wait_ge(S("ret_hi"), h + 1)
                dve.tensor_tensor(HL[:, 4 + h, :], RG[:, h, :], HH[:, 4 + h, :].bitcast(F32),
                                  ALU.subtract).then_inc(S("ret_lo"), 1)

        T32R = [Z(f"T32R{s}", [P, SEQ], F32, 80 + 4 * s) for s in range(2)]

        def ret_act(act):
            for c in range(NT):
                act.wait_ge(S("ret_o"), c + 1)
                act.activation(VT[:, c, :].rearrange("q (p o n) -> q o p n", p=2, o=2),
                               M[c % 2][:].rearrange("q (o p n) -> q o p n", o=2, n=P)[:, :, 0:2, :], ACT.Copy)\
                   .then_inc(S("ret_out"), 1)
            act.wait_ge(S("ret_mv"), 32)
            act.activation(SD[:], MV[:, :, 1], ACT.Sqrt, bias=vec("eps1"), scale=1.0).then_inc(S("ret_sd"), 1)
            for h in range(RET_HEADS):
                act.wait_ge(S("ret_nt"), h + 1)
                if h >= 2:
                    act.wait_ge(S("ret_gate"), h - 1)
                act.activation(T32R[h % 2][:], M[h % 2][:], ACT.Identity, bias=vec("gn_b", h),
                               scale=vec("gn_g", h)).then_inc(S("ret_t32"), 1)
                act.wait_ge(S("ret_gate"), h + 1)
                act.activation(HH[:, 4 + h, :], RG[:, h, :], ACT.Copy).then_inc(S("ret_hi"), 1)

        def ret_turn_pe(pe):
            ret_pe(pe)
            for h in range(RET_HEADS):
                pe.wait_ge(S("ret_n"), 8 * h + 8)
                if h >= 2:
                    pe.wait_ge(S("ret_t32"), h - 1)
                for c in range(NT):
                    m = pe.transpose(M[h % 2][:, c * P:(c + 1) * P], VT[:, c, h * P:(h + 1) * P], IDENT[:])
                m.then_inc(S("ret_nt"), 1)

        stage("ret", dict(act=ret_act, pe=ret_turn_pe, dve=ret_dve))

        ATT = Z("ATT", [P, NT, 512], F32, 16)
        QH = [Z(f"QH{s}", [P, SEQ], F32, 32 + 4 * s) for s in range(2)]
        KH = [Z(f"KH{s}", [P, SEQ], F32, 40 + 4 * s) for s in range(2)]
        VH = [Z(f"VH{s}", [P, NT, MLA_V], F32, 48 + 2 * s) for s in range(2)]
        PR = [Z(f"PR{s}", [P, SEQ], F32, 52 + 4 * s) for s in range(2)]
        PT = [Z(f"PT{s}", [P, SEQ], F32, 60 + 4 * s) for s in range(2)]
        LTMP = Z("LTMP", [P, SEQ], F32, 68)
        MWQ = [Z(f"MWQ{s}", [P, 2, MLA_QK], F32, 92.5 + s) for s in range(2)]
        MWK = [Z(f"MWK{s}", [P, P], F32, 94.5 + 0.5 * s) for s in range(2)]
        SCALE_M = MLA_QK ** -0.5
        causal, before = MASKS[:, P:2 * P], MASKS[:, 2 * P:3 * P]
        identb = MASKS[:, 0:P]

        PARTS = [("q", 0), ("q", 1), ("swap", 0), ("k", 0), ("swap", 1), ("k", 1), ("v", 0)]
        N_PARTS = len(PARTS)
        PART = M[1][:, 512:1024]
        MNEG, MSUM, MRDEN, MMAX = [Z(n, [P, 2, NT], F32, 95.5 + 0.0625 * j)
                                   for j, n in enumerate(("MNEG", "MSUM", "MRDEN", "MMAX"))]

        def head_pairs(eng, body):
            n = MLA_HEADS // 2
            body(0)
            with eng.Fori(1, n - 1) as i:
                body(i)
            body(n - 1)

        def head_steps(i):
            last_pair = isinstance(i, int) and i == MLA_HEADS // 2 - 1
            for s in range(2):
                for t in range(NT):
                    no_next = last_pair and s == 1
                    yield (i * 16 + (8 * s + t), i * 2 + s, t, s, None if no_next else i * 2 + (s + 1),
                           i + 1 if s and not no_next else i, not (no_next and t == NT - 1))

        def mla_part_pe(pe, h, i, s, part):
            kind, n = PARTS[part]
            c = slice(512 * n, 512 * n + 512)
            if part == 0:
                need(pe, S(f"mla_w{s}"), i * 32 + 32)
            need(pe, S("mla_part_used"), h * N_PARTS + part)
            if kind == "q":
                for k in range(2):
                    m = pe.matmul(PART[0:MLA_QK, :], MWQ[s][:, k, :], QC[:, k, c], start=(k == 0), stop=(k == 1))
            elif kind == "k":
                m = pe.matmul(PART[0:NOPE, :], MWK[s][:, 0:NOPE], KVC[:, c], start=True, stop=True)
            elif kind == "swap":
                m = pe.matmul(PART[0:MLA_QK, :], SWAPM[0:MLA_QK, 0:MLA_QK], QH[s][0:MLA_QK, c], start=True, stop=True)
            else:
                for t in range(NT):
                    m = pe.matmul(PART[:, t * MLA_V:(t + 1) * MLA_V], KVC[:, t * P:(t + 1) * P], MWK[s][:, NOPE:P],
                                  start=True, stop=True)
            m.then_inc(S("mla_part"), 1)

        def mla_pe(pe):
            def scores(g, h, t, s):
                if t == 0:
                    need(pe, S("mla_rot"), h * 4 + 4)
                    need(pe, S("mla_part_used"), h * N_PARTS + N_PARTS)
                need(pe, S("mla_exp"), g - 1)
                for n in range(0, t * P + P, 512):
                    e = min(n + 512, t * P + P)
                    pe.matmul(G[t % 2][:, n:e], QH[s][0:MLA_QK, t * P:(t + 1) * P], KH[s][0:MLA_QK, n:e],
                              start=True, stop=(e < t * P + P))
                m = pe.matmul(G[t % 2][:, t * P:(t + 1) * P], identb, causal, start=False, stop=True)
                m.then_inc(S("mla_sc"), 1)

            def turn(g, t):
                need(pe, S("mla_exp"), g + 1)
                need(pe, S("mla_pt"), g)
                for b in range(t + 1):
                    m = pe.transpose(M[0][:, b * P:(b + 1) * P], PR[t % 2][:, b * P:(b + 1) * P], IDENT[:])
                m.then_inc(S("mla_tr"), 1)

            def values(g, h, t, s):
                need(pe, S("mla_pt"), g + 1)
                if t == 0:
                    need(pe, S("mla_att"), h)
                for b in range(t + 1):
                    m = pe.matmul(M[1][:, t * MLA_V:(t + 1) * MLA_V], PT[t % 2][:, b * P:(b + 1) * P], VH[s][:, b, :],
                                  start=(b == 0), stop=(b == t))
                m.then_inc(S("mla_pv"), 1)

            def pair(i):
                for g, h, t, s, nxt, i2, more in head_steps(i):
                    if more:
                        scores(g + 1, h if t < NT - 1 else nxt, (t + 1) % NT, s if t < NT - 1 else 1 - s)
                    if nxt is not None and t < N_PARTS:
                        mla_part_pe(pe, nxt, i2, 1 - s, t)
                    if t:
                        values(g - 1, h, t - 1, s)
                    elif not (isinstance(g, int) and g == 0):
                        values(g - 1, h - 1, NT - 1, 1 - s)
                    turn(g, t)
            for part in range(N_PARTS):
                mla_part_pe(pe, 0, 0, 0, part)
            pe.wait_ge(S("mla_kr"), 2)
            scores(0, 0, 0, 0)
            head_pairs(pe, pair)
            values(MLA_HEADS * NT - 1, MLA_HEADS - 1, NT - 1, 1)

        def mla_dve(dve):
            for s in range(2):
                dve.tensor_copy(KH[s][NOPE:MLA_QK, :], KR[NOPE:MLA_QK, :]).then_inc(S("mla_kr"), 1)

            def rope_part(h, s, part):
                n = PARTS[part][1]
                r, c = slice(NOPE, MLA_QK), slice(512 * n, 512 * n + 512)
                need(dve, S("mla_part"), h * N_PARTS + (part + 1))
                need(dve, S("mla_rot"), h * 4 + 2 * n)
                dve.tensor_tensor(LTMP[r, c], PART[r, :], SINM[r, c], ALU.mult).then_inc(S("mla_part_used"), 1)
                dve.tensor_tensor(QH[s][r, c], QH[s][r, c], COSM[r, c], ALU.mult).then_inc(S("mla_rot"), 1)
                need(dve, S("mla_part_used"), h * N_PARTS + (part + 1))
                need(dve, S("mla_rot"), h * 4 + (2 * n + 1))
                dve.tensor_tensor(QH[s][r, c], QH[s][r, c], LTMP[r, c], ALU.add).then_inc(S("mla_rot"), 1)

            def smax(g, t, s):
                need(dve, S("mla_sc"), g + 1)
                dve.tensor_reduce(MMAX[:, s, t:t + 1], G[t % 2][:, 0:(t + 1) * P], AX.X, ALU.max)\
                   .then_inc(S("mla_mx"), 1)
                need(dve, S("mla_mx"), g + 1)
                dve.tensor_scalar(MNEG[:, s, t:t + 1], MMAX[:, s, t:t + 1], -SCALE_M, None, ALU.mult)\
                   .then_inc(S("mla_smax"), 1)

            def tail(g, t):
                need(dve, S("mla_tr"), g + 1)
                need(dve, S("mla_pv"), g - 1)
                dve.tensor_copy(PT[t % 2][:, 0:(t + 1) * P], M[0][:, 0:(t + 1) * P]).then_inc(S("mla_pt"), 1)

            def put(h, s):
                need(dve, S("mla_exp"), h * NT + NT)
                dve.reciprocal(MRDEN[:, s, :], MSUM[:, s, :]).then_inc(S("mla_rd"), 1)
                need(dve, S("mla_rd"), h + 1)
                need(dve, S("mla_pv"), h * NT + NT)
                dve.tensor_tensor(ATT[:, :, bass.ds(h * MLA_V, MLA_V)],
                                  M[1][:, 0:512].rearrange("p (t d) -> p t d", d=MLA_V),
                                  MRDEN[:, s, :].unsqueeze(2).broadcast_to([P, NT, MLA_V]), ALU.mult)\
                   .then_inc(S("mla_att"), 1)

            def pair(i):
                for g, h, t, s, nxt, i2, more in head_steps(i):
                    if more:
                        smax(g + 1, (t + 1) % NT, s if t < NT - 1 else 1 - s)
                    tail(g, t)
                    if nxt is not None and t < N_PARTS and PARTS[t][0] == "swap":
                        rope_part(nxt, 1 - s, t)
                    if t == 0 and not (isinstance(g, int) and g == 0):
                        put(h - 1, 1 - s)
            for part in range(N_PARTS):
                if PARTS[part][0] == "swap":
                    rope_part(0, 0, part)
            smax(0, 0, 0)
            head_pairs(dve, pair)
            put(MLA_HEADS - 1, 1)

        def mla_act(act):
            def copy_part(h, s, part):
                kind, n = PARTS[part]
                if kind == "swap":
                    return
                c = slice(512 * n, 512 * n + 512)
                need(act, S("mla_part"), h * N_PARTS + (part + 1))
                if kind == "q":
                    dst, src = QH[s][0:MLA_QK, c], PART[0:MLA_QK, :]
                elif kind == "k":
                    dst, src = KH[s][0:NOPE, c], PART[0:NOPE, :]
                else:
                    need(act, S("mla_pv"), h * NT - NT)
                    dst, src = VH[s][:].rearrange("p t n -> p (t n)"), PART
                act.activation(dst, src, ACT.Copy).then_inc(S("mla_part_used"), 1)

            def pair(i):
                for g, h, t, s, nxt, i2, more in head_steps(i):
                    need(act, S("mla_smax"), g + 1)
                    need(act, S("mla_tr"), g - 1)
                    if t == 0:
                        need(act, S("mla_att"), h - 1)
                    act.activation(PR[t % 2][:, 0:(t + 1) * P], G[t % 2][:, 0:(t + 1) * P], ACT.Exp,
                                   bias=MNEG[:, s, t:t + 1], scale=SCALE_M,
                                   accum_out=MSUM[:, s, t:t + 1]).then_inc(S("mla_exp"), 1)
                    if nxt is not None and t < N_PARTS:
                        copy_part(nxt, 1 - s, t)
            for part in range(N_PARTS):
                copy_part(0, 0, part)
            head_pairs(act, pair)

        def mla_sp(sp):
            def pair(i):
                for s in range(2):
                    need(sp, S("mla_part"), i * (2 * N_PARTS) + (s - 1) * N_PARTS)
                    h = i * 2 + s
                    sp.dma_start(MWQ[s][:], A["w_uq"][:, bass.ds(h * MLA_QK, MLA_QK)]
                                 .rearrange("(k p) n -> p k n", p=P)).then_inc(S(f"mla_w{s}"), 16)
                    sp.dma_start(MWK[s][:], A["w_ukv"][:, bass.ds(h * P, P)]).then_inc(S(f"mla_w{s}"), 16)
            turns(sp, MLA_HEADS // 2, pair)

        stage("mla", dict(act=mla_act, pe=mla_pe, dve=mla_dve, sp_gated=mla_sp))

        def turn_stage(tag, att, tile0, gate=None, tmp=None):
            tmp = tmp or T32

            def pe_(pe):
                for j in range(4):
                    if j >= 2:
                        pe.wait_ge(S(tag + "_out"), j - 1)
                    for t in range(NT):
                        m = pe.transpose(M[j % 2][:, t * P:(t + 1) * P], att[:, t, j * P:(j + 1) * P], IDENT[:])
                    m.then_inc(S(tag + "_tr"), 1)

            def dve_(dve):
                for j in range(4):
                    dve.wait_ge(S(tag + "_tr"), j + 1)
                    if j >= 2:
                        dve.wait_ge(S(tag + "_hi"), j - 1)
                        dve.wait_ge(S(tag + "_lo"), j - 1)
                    if gate is None:
                        dve.tensor_copy(tmp[j % 2][:], M[j % 2][:]).then_inc(S(tag + "_out"), 1)
                    else:
                        dve.tensor_tensor(tmp[j % 2][:], M[j % 2][:], gate[:, j, :], ALU.mult)\
                           .then_inc(S(tag + "_out"), 1)
                    dve.wait_ge(S(tag + "_hi"), j + 1)
                    dve.tensor_tensor(HL[:, tile0 + j, :], tmp[j % 2][:], HH[:, tile0 + j, :].bitcast(F32),
                                      ALU.subtract).then_inc(S(tag + "_lo"), 1)

            def act_(act):
                for j in range(4):
                    act.wait_ge(S(tag + "_out"), j + 1)
                    act.activation(HH[:, tile0 + j, :], tmp[j % 2][:], ACT.Copy).then_inc(S(tag + "_hi"), 1)
            stage(tag, dict(act=act_, pe=pe_, dve=dve_))

        turn_stage("mturn", ATT, 0)

        def add_gated(dve, U, f, T, X_, gate):
            unit_ready(dve, U)
            dve.scalar_tensor_tensor(out=X_[:, f, :T], in0=G[U % 2][:, :T], scalar=gate, in1=X_[:, f, :T],
                                     op0=ALU.mult, op1=ALU.add).then_inc(unit_freed[U % 2], 1)

        NSQ = [Z(f"NSQ{s}", [P, SEQ], F32, 4 * s) for s in range(2)]
        NR = Z("NR", [P, SEQ], F32, 8)

        def out_stage(name, w, T, X_, gate, led, squares, first_ada=None):
            along = first_ada is not None

            def gather(dve, f):
                src = [NSQ[i % 2][:, :T] if squares else X_[:, i, :T] for i in range(KT)]
                if squares:
                    dve.wait_ge(S(name + "_sq"), f + 1)
                else:
                    U = info(name)["u0"] + f
                    dve.wait_ge(unit_freed[U % 2], U // 2 + 1)
                if f == 0:
                    return
                if f > 1:
                    dve.wait_ge(S(name + "_acc"), f - 1)
                dve.tensor_tensor(NR[:, :T], src[0] if f == 1 else NR[:, :T], src[f], ALU.add)\
                   .then_inc(S(name + "_acc"), 1)

            def dve_(dve):
                u0 = info(name)["u0"]
                if along:
                    mod_begin(dve)
                for f in range(KT):
                    if along:
                        ada_rows(dve, name, f)
                    add_gated(dve, u0 + f, f, T, X_, gate(f))
                    if along and f:
                        ada_add(dve, first_ada, f - 1)
                    if f:
                        gather(dve, f - 1)
                gather(dve, KT - 1)
                if along:
                    ada_add(dve, first_ada, KT - 1)

            def act_(act):
                u0 = info(name)["u0"]
                for f in range(KT if squares else 0):
                    act.wait_ge(unit_freed[(u0 + f) % 2], (u0 + f) // 2 + 1)
                    if f >= 2:
                        act.wait_ge(S(name + "_acc"), max(f - 2, 1))
                    act.activation(NSQ[f % 2][:, :T], X_[:, f, :T], ACT.Square).then_inc(S(name + "_sq"), 1)

            def pe_(pe):
                gemm_pairs(pe, info(name)["u0"], 4, T, (HH, HL), led=True,
                           after=late_sum if along else None)
                if along:
                    mod_sum(pe, 1, 3, 1)

            def sp_(sp, r0):
                with_ada(sp, r0, KT, lambda j: w[:, j * P:(j + 1) * P].rearrange("(k p) n -> p k n", p=P), first_ada)
            progs = dict(lead=lead_in(name, T, *led), pe=pe_, dve=dve_, act=act_)
            if along:
                stage(name, dict(sp_free=sp_, **progs), raw=[(8, None)], units=8, per_unit=2)
            else:
                stage(name, progs, raw=[(4, cols(w, 0))], units=8)

        out_stage("wout", A["w_out"], SEQ, X, lambda f: MODA[:, 16 + f:17 + f],
                  ("mturn_lo", range(4)), squares=False, first_ada=40)


        def ones_sum(pe, dst, T, tiles, ready=None, used=None):
            nt = max(1, T // 512)
            w = T // nt
            for k in range(len(tiles)):
                if ready:
                    pe.wait_ge(ready, k + 1)
                for n in range(nt):
                    m = pe.matmul(dst[:, n * w:(n + 1) * w], ONES[:], tiles[k][:, n * w:(n + 1) * w],
                                  start=(k == 0), stop=(k == len(tiles) - 1))
                if used and k < len(tiles) - 1:
                    m.then_inc(used, 1)
            return m

        def norm_stage(tag, X_, T, mean, eps, finish_dve, finish_act, n_tiles=KT, sq=NSQ, r=NR, gathered=False,
                       dmas=()):
            tiles = [X_[:, f, :T] for f in range(n_tiles)]
            width = n_tiles * P
            squares = mean or not gathered

            def pe_(pe):
                if mean:
                    ones_sum(pe, M[0], T, [r] if gathered else tiles).then_inc(S(tag + "_mean"), 1)
                if squares:
                    ones_sum(pe, M[1], T, [sq[k % 2] for k in range(n_tiles)], ready=S(tag + "_sq"),
                             used=S(tag + "_squ")).then_inc(S(tag + "_var"), 1)
                else:
                    ones_sum(pe, M[1], T, [r]).then_inc(S(tag + "_var"), 1)

            def dve_(dve):
                if mean:
                    dve.wait_ge(S(tag + "_mean"), 1)
                    for f in range(n_tiles):
                        dve.scalar_tensor_tensor(out=tiles[f], in0=M[0][:, :T], scalar=-1.0 / width, in1=tiles[f],
                                                 op0=ALU.mult, op1=ALU.add).then_inc(S(tag + "_c"), 1)
                dve.wait_ge(S(tag + "_sd"), 1)
                dve.reciprocal(r[:, :T], r[:, :T]).then_inc(S(tag + "_r"), 1)
                dve.wait_ge(S(tag + "_r"), 1)
                finish_dve(dve, tag, r)

            def act_(act):
                for f in range(n_tiles if squares else 0):
                    if mean:
                        act.wait_ge(S(tag + "_c"), f + 1)
                    if f >= 2:
                        act.wait_ge(S(tag + "_squ"), f - 1)
                    act.activation(sq[f % 2][:, :T], tiles[f], ACT.Square).then_inc(S(tag + "_sq"), 1)
                act.wait_ge(S(tag + "_var"), 1)
                act.activation(r[:, :T], M[1][:, :T], ACT.Sqrt, bias=vec(eps), scale=1.0 / width)\
                   .then_inc(S(tag + "_sd"), 1)
                finish_act(act, tag)
            stage(tag, dict(act=act_, pe=pe_, dve=dve_), dmas=dmas)

        ER = Z("ER", [P, SEQ], F32, 56)

        def ln_finish(g, b, scale=None, shift=None):
            def dve_(dve, tag, r):
                for f in range(KT + 1):
                    if f < KT:
                        dve.scalar_tensor_tensor(out=X[:, f, :], in0=X[:, f, :], scalar=vec(g, f), in1=r[:],
                                                 op0=ALU.mult, op1=ALU.mult).then_inc(S(tag + "_g"), 1)
                    if f < KT and scale is not None:
                        dve.wait_ge(S(tag + "_g"), f + 1)
                        dve.tensor_scalar(X[:, f, :], X[:, f, :], vec(b, f), None, ALU.add).then_inc(S(tag + "_x"), 1)
                    if f and scale is not None:
                        h_low(dve, tag, f - 1, SEQ)
                    if f and scale is None:
                        dve.wait_ge(S(tag + "_xsq"), f)
                        if f > 1:
                            if f > 2:
                                dve.wait_ge(S(tag + "_acc"), f - 2)
                            dve.tensor_tensor(ER[:], NSQ[0][:] if f == 2 else ER[:], NSQ[(f - 1) % 2][:], ALU.add)\
                               .then_inc(S(tag + "_acc"), 1)

            def act_(act, tag):
                if scale is not None:
                    h_act(act, tag, S(tag + "_x"), SEQ, lambda f: X[:, f, :], scale, shift)
                    return
                for f in range(KT):
                    act.wait_ge(S(tag + "_g"), f + 1)
                    act.activation(X[:, f, :], X[:, f, :], ACT.Identity, bias=vec(b, f), scale=1.0)\
                       .then_inc(S(tag + "_x"), 1)
                    act.wait_ge(S(tag + "_x"), f + 1)
                    if f >= 2:
                        act.wait_ge(S(tag + "_acc"), max(f - 2, 1))
                    act.activation(NSQ[f % 2][:], X[:, f, :], ACT.Square).then_inc(S(tag + "_xsq"), 1)
            return dve_, act_

        norm_stage("ln1", X, SEQ, True, "eps1", *ln_finish("ln1_g", "ln1_b", lambda f: MODA[:, 32 + f:33 + f],
                                                           lambda f: MODA[:, 24 + f:25 + f]), gathered=True)

        FH = Z("FH", [P, KT, SEQ], F32R, 0)
        FL = Z("FL", [P, KT, SEQ], F32R, 32)
        T2 = [Z(f"T2_{s}", [P, SEQ], F32, 64 + 4 * s) for s in range(2)]

        PER_CHUNK = 3 * KT // N_CHUNK

        def ff_mod(q):
            if q >= 2 * PER_CHUNK:
                return None
            return (("e_w_mod", "e_b", MODE) if q < PER_CHUNK else ("o_w_mod", "o_b", MODO)) + (q % PER_CHUNK,)

        def ff_r2(c, q):
            return c * (8 + PER_CHUNK) + (info("ff")["r0"] // 2 + min(q // 2, PER_CHUNK) + q // 2)

        def ff_mod_rows(dve, c, q):
            if ff_mod(q):
                mod_rows(dve, q % 2, ff_r2(c, q) + 1, c * (4 * PER_CHUNK) + 2 * q, [C2ACT[:, :, 0], C2ACT[:, :, 1]])

        def ff_mod_sum(pe, c, q):
            if ff_mod(q):
                mod_sum(pe, q % 2, c * PER_CHUNK + q // 2, 2)

        def ff_mod_add(dve, c, q):
            if ff_mod(q):
                _, bias, dst, j = ff_mod(q)
                mod_add(dve, q % 2, c * PER_CHUNK + q // 2,
                        dst[:, bass.ds(c * PER_CHUNK + j, 1), :].rearrange("p a b -> p (a b)"),
                        V[:, bass.ds(c * PER_CHUNK + (VEC[bias] + j), 1)])

        def ff_pool(pool):
            u0 = info("ff")["u0"]

            def chunk(c):
                for q in range(2 * KT):
                    split_unit(pool, q % 2, ff_r2(c, q), c * 8 + (u0 // 2 + q // 2))
            turns(pool, N_CHUNK, chunk)

        def ff_pe(pe):
            u0 = info("ff")["u0"]

            def chunk(c):
                for q in range(2 * KT):
                    ready = {k: (S("ff_lo"), c * 8 + (k + 2)) for k in range(KT)} if q == KT else None
                    if q or not isinstance(c, int):
                        gemm_unit(pe, q % 2, c * 8 + (u0 // 2 + q // 2), SEQ, (FH, FL) if q >= KT else (HH, HL),
                                  ready=ready)
                    if q:
                        ff_mod_sum(pe, c, q - 1)
            turns(pe, N_CHUNK, chunk)

        def ff_act(act):
            u0 = info("ff")["u0"]
            with act.Fori(0, N_CHUNK) as c:
                for j in range(KT):
                    s = j % 2
                    act.wait_ge(unit_done[s], c * 8 + (u0 // 2 + j // 2 + 1))
                    act.wait_ge(S("ff_lo"), c * 8 + (max(j - 1, 0) + 1))
                    act.activation(T2[s][:], G[s][:], ACT.Relu).then_inc(unit_freed[s], 1)
                    act.wait_ge(unit_freed[s], c * 8 + (u0 // 2 + j // 2 + 1))
                    act.activation(T2[s][:], T2[s][:], ACT.Square).then_inc(S("ff_sq"), 1)
                    act.wait_ge(S("ff_sq"), c * 8 + (j + 1))
                    act.activation(FH[:, j, :], T2[s][:], ACT.Copy).then_inc(S("ff_hi"), 1)

        def ff_dve(dve):
            u0 = info("ff")["u0"]
            dve.sem_inc(S("ff_lo"), 1)
            mod_begin(dve)
            with dve.Fori(0, N_CHUNK) as c:
                for j in range(KT):
                    ff_mod_rows(dve, c, j)
                    dve.wait_ge(S("ff_hi"), c * 8 + (j + 1))
                    dve.tensor_tensor(FL[:, j, :], T2[j % 2][:], FH[:, j, :].bitcast(F32),
                                      ALU.subtract).then_inc(S("ff_lo"), 1)
                    if j:
                        ff_mod_add(dve, c, j - 1)
                for f in range(KT):
                    s = f % 2
                    ff_mod_rows(dve, c, KT + f)
                    dve.wait_ge(unit_done[s], c * 8 + (u0 // 2 + 4 + f // 2 + 1))
                    dve.wait_ge(unit_freed[s], c * 8 + (u0 // 2 + 4 + f // 2))
                    dve.scalar_tensor_tensor(out=X[:, f, :], in0=G[s][:], scalar=MODA[:, 40 + f:41 + f],
                                             in1=X[:, f, :], op0=ALU.mult, op1=ALU.add).then_inc(unit_freed[s], 1)
                    ff_mod_add(dve, c, KT + f - 1)
            for s in range(2):
                dve.wait_ge(S(f"mod_read{s}"), N_CHUNK * PER_CHUNK + 1)
            for l, (mod, gain) in enumerate(((MODE, "e_norm"), (MODO, "o_norm"))):
                for c in range(2):
                    dve.scalar_tensor_tensor(out=GS[:, l, :, c], in0=mod[:, 8:16, c], scalar=1.0,
                                             in1=vec(gain, 0, 8), op0=ALU.add, op1=ALU.mult).then_inc(S("gs"), 1)

        def ff_sp(sp, r0):
            with sp.Fori(0, N_CHUNK) as c:
                for q in range(2 * KT):
                    s, f = q % 2, q % KT
                    src = A["w_ff1"][:, bass.ds(c * D + f * P, P)] if q < KT else \
                        A["w_ff2"][bass.ds(c * D, D), f * P:(f + 1) * P]
                    load_unit(sp, ff_r2(c, q), s, src.rearrange("(k p) n -> p k n", p=P), RAW[s][:])
                    if ff_mod(q):
                        w, _, _, j = ff_mod(q)
                        load_unit(sp, ff_r2(c, q) + 1, s, A[w][:, bass.ds(c * (PER_CHUNK * P) + j * P, P)]
                                  .rearrange("(k p) n -> p k n", p=P), RAW[s][:])

        stage("ff", dict(lead=lead_in("ff", SEQ, "ln1_lo"), act=ff_act, pe=ff_pe, dve=ff_dve, sp_free=ff_sp, pool=ff_pool),
              raw=[((8 + PER_CHUNK) * N_CHUNK, None)], units=16 * N_CHUNK)
        CT = Z("CT", [P, 2, D], F32, 44)
        norm_stage("ln2", X, SEQ, True, "eps1", *ln_finish("ln2_g", "ln2_b"),
                   dmas=[(CT[:, t, :], A["ctx"][t * P:(t + 1) * P, :]) for t in range(2)])

        def rms_h(tag, X_, T, layer, c, gathered=True, r_known=None):
            mod = (MODE, MODO)[layer]
            XN = [Z(f"XN{tag}{s}", [P, T], F32, 12 + 4 * s) for s in range(2)]

            def dve_(dve, tag, r):
                for f in range(KT + 1):
                    if f < KT:
                        if f >= 2:
                            dve.wait_ge(S(tag + "_t32"), f - 1)
                        dve.tensor_tensor(XN[f % 2][:], X_[:, f, :T], r[:, :T], ALU.mult).then_inc(S(tag + "_xn"), 1)
                    if f:
                        h_low(dve, tag, f - 1, T)

            def act_(act, tag):
                h_act(act, tag, S(tag + "_xn"), T, lambda f: XN[f % 2][:], lambda f: GS[:, layer, f, c:c + 1],
                      lambda f: mod[:, f, c:c + 1])
            if r_known is None:
                norm_stage(tag, X_, T, False, "eps2", dve_, act_, gathered=gathered)
            else:
                stage(tag, dict(act=lambda act: act_(act, tag), dve=lambda dve: dve_(dve, tag, r_known)))

        def even_layer(tag, X_, T, c, r_known=None):
            rms_h(tag + "n", X_, T, 0, c, gathered=False, r_known=r_known)
            w = T + 2 * PAD
            U = Z(tag + "U", [P, 4, w], F32, 0)
            GA = Z(tag + "GA", [P, 4, T], F32, 17)
            VB = Z(tag + "VB", [P, 4, T], F32, 33)
            GB = Z(tag + "GB", [P, 4, T], F32, 49)
            ACC = Z(tag + "ACC", [P, T], F32, 65)
            SG = Z(tag + "SG", [P, T], F32, 69)
            name = tag + "in"
            unit_cols = [x for j in range(4) for x in (512 + P * j, P * j)] + \
                [1536 + P * j for j in range(4)] + [2048 + P * j for j in range(4)] + [1024 + P * j for j in range(4)]

            def conv(dve, a, b):
                for q in range(a, b):
                    j, k = divmod(q, CONV_W)
                    src, wk = U[:, j, k:k + T], V[:, VEC["conv_w"] + j * CONV_W + k:VEC["conv_w"] + j * CONV_W + k + 1]
                    if q:
                        dve.wait_ge(S(name + "_tap"), q)
                    if k == 0:
                        dve.wait_ge(S(name + "_u"), 1 + j + 1)
                        if j:
                            dve.wait_ge(S(name + "_cv"), j)
                        dve.tensor_scalar(ACC[:], src, wk, vec("conv_b", j), ALU.mult, ALU.add)\
                           .then_inc(S(name + "_tap"), 1)
                    else:
                        dve.scalar_tensor_tensor(out=ACC[:], in0=src, scalar=wk, in1=ACC[:], op0=ALU.mult,
                                                 op1=ALU.add).then_inc(S(name + "_tap"), 1)
                    if k == CONV_W - 1:
                        dve.wait_ge(S(name + "_tap"), q + 1)
                        dve.tensor_copy(U[:, j, 0:T], ACC[:]).then_inc(S(name + "_cv"), 1)

            def in_dve(dve):
                u0 = info(name)["u0"]
                dve.memset(U[:, :, 0:PAD], 0.0).then_inc(S(name + "_pad"), 1)
                dve.memset(U[:, :, PAD + T:w], 0.0).then_inc(S(name + "_u"), 1)
                step = 0
                for j in range(4):
                    unit_ready(dve, u0 + 2 * j + 1)
                    dve.wait_ge(unit_freed[0], u0 // 2 + j + 1)
                    dve.tensor_tensor(U[:, j, PAD:PAD + T], G[1][:, :T], SG[:], ALU.mult)\
                       .then_inc(S(name + "_u"), 1)
                    dve.wait_ge(S(name + "_u"), j + 2)
                    dve.sem_inc(unit_freed[1], 1)
                    if j < 3:
                        conv(dve, step, step + 12)
                        step += 12
                conv(dve, step, 4 * CONV_W)

            def in_act(act):
                u0 = info(name)["u0"]
                for j in range(4):
                    unit_ready(act, u0 + 2 * j)
                    if j:
                        act.wait_ge(S(name + "_u"), j + 1)
                    act.activation(SG[:], G[0][:, :T], ACT.Sigmoid).then_inc(unit_freed[0], 1)
                for j in range(12):
                    U_ = u0 + 8 + j
                    unit_ready(act, U_)
                    dst = (VB, GB, GA)[j // 4][:, j % 4, :]
                    act.activation(dst, G[U_ % 2][:, :T], ACT.Copy if j < 4 else ACT.Silu)\
                       .then_inc(unit_freed[U_ % 2], 1)

            def unit_src(j):
                return A["e_w_in"][:, unit_cols[j]:unit_cols[j] + P].rearrange("(k p) n -> p k n", p=P)
            stage(name, dict(lead=lead_in(name, T, tag + "n_lo"), act=in_act, dve=in_dve,
                             pe=lambda pe: gemm_pairs(pe, info(name)["u0"], 10, T, (HH, HL), led=True)),
                  raw=[(1, lambda s, i, j=j: unit_src(2 * j + s)) for j in range(10)], units=20)

            n_tok = T // P
            half = T // 2
            VP = Z(tag + "VP", [P, n_tok, 512], F32, 80)
            VQ = Z(tag + "VQ", [P, n_tok, 512], F32, 112)
            FW = Z(tag + "FW", [P, 4, P], F32, 96)
            DFTD = Z(tag + "DFTD", [P, 256], F32, 98)
            PQ = Z(tag + "PQ", [P, 4, 2, P], F32, 99)
            EV = [Z(f"{tag}EV{s}", [P, half], F32, 69 + 2 * s) for s in range(2)]
            YB = Z(tag + "YB", [P, T], F32, 73)
            fn = tag + "fo"
            AR = Z(tag + "AR", [P, T], F32, 65)
            ASQ = [T32[s][:, :T] for s in range(2)]
            banks = [[G[j // 2][:, 512 * (j % 2):512 * (j % 2) + half] for j in range(4)],
                     [M[j // 2][:, 512 * (j % 2):512 * (j % 2) + half] for j in range(4)]]

            def fo_pe(pe):
                pe.wait_ge(moved, info(fn)["dma_end"])
                for q in range(2):
                    for g in range(4):
                        m = pe.matmul(M[q][:, g * P:(g + 1) * P], DFTD[:, q * P:(q + 1) * P], FW[:, g, :], start=True,
                                      stop=True)
                m.then_inc(S(fn + "_pq"), 1)
                pe.wait_ge(S(fn + "_pqs"), 2)
                pe.wait_ge(S(fn + "_sum"), 3)
                ones_sum(pe, M[0], T, [AR]).then_inc(S(fn + "_mean"), 1)
                for t in range(n_tok):
                    par, i = divmod(t, n_tok // 2)
                    if t >= 2:
                        pe.wait_ge(S(fn + "_v"), 2 * (t - 1))
                    first = 2 * P * i + par
                    for g in range(4):
                        m = pe.matmul(G[t % 2][:, g * 256:(g + 1) * 256], VB[:, g, first:first + 2 * P - 1:2],
                                      PQ[:, g, :, :].rearrange("p a b -> p (a b)"), start=True, stop=True)
                    m.then_inc(S(fn + "_vp"), 1)
                pe.wait_ge(S(fn + "_v"), 2 * n_tok)
                r0 = info(fn)["r0"]
                for t in range(n_tok):
                    par, i = divmod(t, n_tok // 2)
                    pe.wait_ge(raw_loaded[t % 2], 16 * ((r0 + t) // 2 + 1))
                    if t == n_tok // 2:
                        pe.wait_ge(S(fn + "_cen"), 4)
                    tab = RAW[t % 2][:].rearrange("p k n -> p (k n)")
                    for g in range(4):
                        for q, vv in enumerate((VP, VQ)):
                            m = pe.matmul(banks[par][g], vv[:, t, g * P:(g + 1) * P],
                                          tab[:, q * half:(q + 1) * half], start=(i == 0 and q == 0),
                                          stop=(i == n_tok // 2 - 1 and q == 1))
                    m.then_inc(raw_used[t % 2], 1)

            def fo_act(act):
                act.wait_ge(S(fn + "_pq"), 1)
                for q in range(2):
                    act.activation(PQ[:, :, q, :], M[q][:, 0:512].rearrange("p (g n) -> p g n", n=P), ACT.Copy,
                                   scale=float(T) ** -0.5).then_inc(S(fn + "_pqs"), 1)
                for j in range(4):
                    act.wait_ge(S(fn + "_cen"), j + 1)
                    if j >= 2:
                        act.wait_ge(S(fn + "_acc"), max(j - 2, 1))
                    act.activation(ASQ[j % 2], U[:, j, 0:T], ACT.Square).then_inc(S(fn + "_sq"), 1)
                r0 = info(fn)["r0"]
                for s in range(2):
                    act.wait_ge(raw_used[s], (r0 + n_tok) // 2)
                for g in range(4):
                    if g >= 2:
                        act.wait_ge(S(fn + "_y"), 2 * (g - 1))
                    act.activation(EV[g % 2][:], banks[0][g], ACT.Copy).then_inc(S(fn + "_ev"), 1)
                    act.wait_ge(S(fn + "_gate"), g + 1)
                    act.activation(HH[:, 4 + g, :T], YB[:], ACT.Copy).then_inc(S(fn + "_hi"), 1)

            def fo_dve(dve):
                for j in range(1, 4):
                    if j > 1:
                        dve.wait_ge(S(fn + "_sum"), j - 1)
                    dve.tensor_tensor(AR[:], U[:, 0, 0:T] if j == 1 else AR[:], U[:, j, 0:T], ALU.add)\
                       .then_inc(S(fn + "_sum"), 1)
                for t in range(n_tok):
                    dve.wait_ge(S(fn + "_vp"), t + 1)
                    both = G[t % 2][:].rearrange("p (g q n) -> p g q n", g=4, q=2)
                    for q, vv in enumerate((VP, VQ)):
                        dve.tensor_copy(vv[:, t, :].rearrange("p (g n) -> p g n", n=P), both[:, :, q, :])\
                           .then_inc(S(fn + "_v"), 1)
                dve.wait_ge(S(fn + "_mean"), 1)
                for j in range(4):
                    dve.scalar_tensor_tensor(out=U[:, j, 0:T], in0=M[0][:, :T], scalar=-1.0 / (4 * P),
                                             in1=U[:, j, 0:T], op0=ALU.mult, op1=ALU.add).then_inc(S(fn + "_cen"), 1)
                for j in range(1, 4):
                    dve.wait_ge(S(fn + "_sq"), j + 1)
                    if j > 1:
                        dve.wait_ge(S(fn + "_acc"), j - 1)
                    dve.tensor_tensor(AR[:], ASQ[0] if j == 1 else AR[:], ASQ[j % 2], ALU.add)\
                       .then_inc(S(fn + "_acc"), 1)
                dve.wait_ge(S(fn + "_acc"), 3)
                r0 = info(fn)["r0"]
                for s in range(2):
                    dve.wait_ge(raw_used[s], (r0 + n_tok) // 2)
                for g in range(4):
                    dve.wait_ge(S(fn + "_ev"), g + 1)
                    if g:
                        dve.wait_ge(S(fn + "_lo"), g)
                    dve.tensor_tensor(YB[:, 0:half], banks[1][g], EV[g % 2][:], ALU.add).then_inc(S(fn + "_y"), 1)
                    dve.scalar_tensor_tensor(out=YB[:, half:T], in0=banks[1][g], scalar=-1.0, in1=EV[g % 2][:],
                                             op0=ALU.mult, op1=ALU.add).then_inc(S(fn + "_y"), 1)
                    dve.wait_ge(S(fn + "_y"), 2 * g + 2)
                    dve.tensor_tensor(YB[:], YB[:], GB[:, g, :], ALU.mult).then_inc(S(fn + "_gate"), 1)
                    dve.wait_ge(S(fn + "_hi"), g + 1)
                    dve.tensor_tensor(HL[:, 4 + g, :T], YB[:], HH[:, 4 + g, :T].bitcast(F32),
                                      ALU.subtract).then_inc(S(fn + "_lo"), 1)

            def dft_unit(t):
                return A[f"dft_{T}"][t * P:(t + 1) * P, :]

            def fo_sp(sp, r0):
                for t in range(n_tok):
                    load_unit(sp, (r0 + t) // 2, t % 2, dft_unit(t),
                              RAW[t % 2][:].rearrange("p k n -> p (k n)")[:, 0:T])
            stage(fn, dict(act=fo_act, pe=fo_pe, dve=fo_dve, sp_free=fo_sp), raw=[(n_tok // 2, None)],
                  dmas=[(FW[:], A["e_b_fw"].rearrange("g d e -> d g e")), (DFTD[:], A["dft_d"])])

            def ln_dve(dve, t_, r):
                for j in range(4):
                    dve.tensor_tensor(U[:, j, 0:T], U[:, j, 0:T], r[:, :T], ALU.mult).then_inc(S(t_ + "_xn"), 1)

            def ln_act(act, t_):
                for j in range(4):
                    act.wait_ge(S(t_ + "_xn"), j + 1)
                    act.activation(U[:, j, 0:T], U[:, j, 0:T], ACT.Silu, bias=vec("a_ln_b", j),
                                   scale=vec("a_ln_g", j)).then_inc(S(t_ + "_s"), 1)
            norm_stage(tag + "an", U, T, False, "eps2", ln_dve, ln_act, n_tiles=4, r=AR, gathered=True)
            pn = tag + "pw"
            nt = max(1, T // 512)
            cw = T // nt

            def pw_pe(pe):
                r0 = info(pn)["r0"]
                for j in range(4):
                    pe.wait_ge(raw_loaded[j % 2], 16 * ((r0 + j) // 2 + 1))
                    if j >= 2:
                        pe.wait_ge(S(pn + "_g"), j - 1)
                    for k in range(4):
                        for n in range(nt):
                            m = pe.matmul(G[j % 2][:, n * cw:(n + 1) * cw], RAW[j % 2][:, k, :],
                                          U[:, k, n * cw:(n + 1) * cw], start=(k == 0), stop=(k == 3))
                    m.then_inc(raw_used[j % 2], 1)

            def pw_dve(dve):
                r0 = info(pn)["r0"]
                for j in range(4):
                    dve.wait_ge(raw_used[j % 2], (r0 + j) // 2 + 1)
                    dve.scalar_tensor_tensor(out=GA[:, j, :], in0=G[j % 2][:, :T], scalar=vec("pw_b", j),
                                             in1=GA[:, j, :], op0=ALU.add, op1=ALU.mult).then_inc(S(pn + "_g"), 1)
                    dve.wait_ge(S(pn + "_hi"), j + 1)
                    dve.tensor_tensor(HL[:, j, :T], GA[:, j, :], HH[:, j, :T].bitcast(F32),
                                      ALU.subtract).then_inc(S(pn + "_lo"), 1)

            def pw_act(act):
                for j in range(4):
                    act.wait_ge(S(pn + "_g"), j + 1)
                    act.activation(HH[:, j, :T], GA[:, j, :], ACT.Copy).then_inc(S(pn + "_hi"), 1)

            def pw_sp(sp, r0):
                for j in range(4):
                    load_unit(sp, (r0 + j) // 2, j % 2,
                              A["e_a_pw_w"][:, j * P:(j + 1) * P].rearrange("(k p) n -> p k n", p=P),
                              RAW[j % 2][:, 0:4, :])
            stage(pn, dict(act=pw_act, pe=pw_pe, dve=pw_dve, sp_free=pw_sp), raw=[(2, None)])
            out_stage(tag + "out", A["e_w_out"], T, X_, lambda f: MODE[:, 16 + f, c:c + 1],
                      (pn + "_lo", range(4), (pn + "_g", 3)), squares=True)

        XC = Z("XC", [P, KT, CTX], F32, 22)

        def cin_pe(pe):
            ones_sum(pe, G[0], SEQ, [ER]).then_inc(S("er_sum"), 1)
            pe.wait_ge(moved, info("ln2")["dma_end"])
            for q in range(4):
                if q >= 2:
                    pe.wait_ge(S("cin_x"), q - 1)
                for f in range(2 * q, 2 * q + 2):
                    for t in range(2):
                        m = pe.transpose(M[q % 2][:, 256 * (f % 2) + t * P:256 * (f % 2) + (t + 1) * P],
                                         CT[:, t, f * P:(f + 1) * P], IDENT[:])
                m.then_inc(S("cin_tr"), 1)

        def cin_dve(dve):
            for q in range(4):
                dve.wait_ge(S("cin_tr"), q + 1)
                dve.tensor_copy(XC[:, 2 * q:2 * q + 2, :].rearrange("p a b -> p (a b)"), M[q % 2][:, 0:512])\
                   .then_inc(S("cin_x"), 1)

        def cin_act(act):
            act.wait_ge(S("er_sum"), 1)
            act.activation(ER[:], G[0][:], ACT.Sqrt, bias=vec("eps2"), scale=1.0 / D).then_inc(S("er_sd"), 1)

        stage("cin", dict(act=cin_act, pe=cin_pe, dve=cin_dve))

        O_Q, O_K, O_V, O_AG = 2048, 2560, 2688, 2816
        even_layer("c", XC, CTX, 1)
        rms_h("ckn", XC, CTX, 1, 1)
        CV = Z("CV", [P, CTX], F32, 0)

        def ckv_act(act):
            u0 = info("ckv")["u0"]
            for j, dst in enumerate((KC, CV)):
                unit_ready(act, u0 + j)
                act.activation(dst[:], G[j][:, 0:CTX], ACT.Copy).then_inc(unit_freed[j], 1)
            act.wait_ge(S("ckv_tr"), 1)
            act.activation(VC[:].rearrange("p a b -> p (a b)"), M[0][:, 0:CTX], ACT.Copy).then_inc(S("ckv_v"), 1)

        def ckv_dve(dve):
            dve.reciprocal(ER[:], ER[:]).then_inc(S("er"), 1)

        def ckv_pe(pe):
            u0 = info("ckv")["u0"]
            gemm_pairs(pe, u0, 1, CTX, (HH, HL), led=True)
            pe.wait_ge(unit_freed[1], u0 // 2 + 1)
            for t in range(2):
                m = pe.transpose(M[0][:, t * P:(t + 1) * P], CV[:, t * P:(t + 1) * P], IDENT[:])
            m.then_inc(S("ckv_tr"), 1)

        stage("ckv", dict(lead=lead_in("ckv", CTX, "ckn_lo"), dve=ckv_dve, act=ckv_act, pe=ckv_pe), raw=[(1, cols(A["o_w_in"], O_K))], units=2)

        even_layer("e", X, SEQ, 0, r_known=ER)

        rms_h("on", X, SEQ, 1, 0)
        SX = Z("SX", [P, 4, SEQ + 2], F32, 0)
        CB = Z("CB", [P, 4, SEQ], F32, 16.25)
        OQ = Z("OQ", [P, 4, SEQ], F32, 32.25)
        OK = Z("OK", [P, SEQ], F32, 48.25)
        OV = Z("OV", [P, SEQ], F32, 52.25)
        AG = Z("AG", [P, 4, SEQ], F32, 56.25)
        TG = Z("TG", [P, SEQ], F32, 72.25)
        odd_units = [("s", c0 + P * j) for j in range(4) for c0 in (512, 1024)] + \
            [("b", c0 + P * j) for j in range(4) for c0 in (1536, 0)] + \
            [("q", O_Q + HEAD * j) for j in range(4)] + [("k", O_K), ("v", O_V)] + \
            [("g", O_AG + P * j) for j in range(4)]

        def odd_act(act):
            u0 = info("odd")["u0"]
            for j in range(26):
                kind = odd_units[j][0]
                if j < 16 and j % 2:
                    continue
                unit_ready(act, u0 + j)
                if j < 16:
                    if j:
                        act.wait_ge(S("odd_p"), j // 2)
                    act.activation(TG[:], G[0][:], ACT.Copy if kind == "s" else ACT.Silu).then_inc(unit_freed[0], 1)
                elif j < 22:
                    dst = OQ[:, j - 16, :] if j < 20 else (OK, OV)[j - 20][:]
                    act.activation(dst, G[j % 2][:], ACT.Copy).then_inc(unit_freed[j % 2], 1)
                else:
                    act.activation(AG[:, j - 22, :], G[j % 2][:], ACT.Silu).then_inc(unit_freed[j % 2], 1)

        CACC = Z("CACC", [P, 512], F32, 76.25)

        def three_taps(dve, j):
            wk = [V[:, VEC["c_conv"] + 3 * j + k:VEC["c_conv"] + 3 * j + k + 1] for k in range(3)]
            for half in range(2):
                n, t0 = 4 * (2 * j + half), 512 * half
                if n:
                    dve.wait_ge(S("odd_tap"), n)
                dve.tensor_scalar(CACC[:], SX[:, j, t0:t0 + 512], wk[0], None, ALU.mult).then_inc(S("odd_tap"), 1)
                for k in (1, 2):
                    dve.wait_ge(S("odd_tap"), n + k)
                    dve.scalar_tensor_tensor(out=CACC[:], in0=SX[:, j, k + t0:k + t0 + 512], scalar=wk[k], in1=CACC[:],
                                             op0=ALU.mult, op1=ALU.add).then_inc(S("odd_tap"), 1)
                dve.wait_ge(S("odd_tap"), n + 3)
                dve.tensor_tensor(CB[:, j, t0:t0 + 512], CB[:, j, t0:t0 + 512], CACC[:], ALU.mult)\
                   .then_inc(S("odd_tap"), 1)

        def odd_dve(dve):
            u0 = info("odd")["u0"]
            dve.memset(SX[:, :, 0:1], 0.0).then_inc(S("odd_z"), 1)
            dve.memset(SX[:, :, SEQ + 1:SEQ + 2], 0.0).then_inc(S("odd_z"), 1)
            for j in range(8):
                unit_ready(dve, u0 + 2 * j + 1)
                dve.wait_ge(unit_freed[0], u0 // 2 + j + 1)
                dst = SX[:, j, 1:SEQ + 1] if j < 4 else CB[:, j - 4, :]
                dve.tensor_tensor(dst, G[1][:], TG[:], ALU.mult).then_inc(S("odd_p"), 1)
                dve.wait_ge(S("odd_p"), j + 1)
                dve.sem_inc(unit_freed[1], 1)
                if j >= 4:
                    three_taps(dve, j - 4)

        def odd_sp(sp, r0):
            for j in range(26):
                view = RAW[j % 2][:]
                kind, c0 = odd_units[j]
                if kind == "q":
                    sp.wait_ge(raw_used[j % 2], (r0 + j) // 2)
                    sp.dma_start(view[:, :, 0:HEAD], A["o_w_in"][:, c0:c0 + HEAD].rearrange("(k p) n -> p k n", p=P))\
                      .then_inc(q_half, 16)
                    sp.wait_ge(q_half, 16 * (j - 15))
                    c0 += 4 * HEAD
                    sp.dma_start(view[:, :, HEAD:P], A["o_w_in"][:, c0:c0 + HEAD].rearrange("(k p) n -> p k n", p=P))\
                      .then_inc(raw_loaded[j % 2], 16)
                else:
                    load_unit(sp, (r0 + j) // 2, j % 2, A["o_w_in"][:, c0:c0 + P].rearrange("(k p) n -> p k n", p=P),
                              view)

        stage("odd", dict(lead=lead_in("odd", SEQ, "on_lo"), act=odd_act, dve=odd_dve,
                          pe=lambda pe: gemm_pairs(pe, info("odd")["u0"], 13, SEQ, (HH, HL), led=True),
                          sp_free=odd_sp), raw=[(13, None)], units=26)

        WC, WS = Z("WC", [P, SEQ], F32, 96), Z("WS", [P, SEQ], F32, 100)
        OTMP = Z("OTMP", [P, SEQ], F32, 104)
        SWAPW = Z("SWAPW", [P, P], F32, 108)
        WVT = Z("WVT", [P, NT, P], F32, 72.25)
        QA = [Z(f"QA{h}", [P, SEQ], F32R, 4 * h) for h in range(N_Q)]
        KH2 = [Z(f"KH2_{g}", [P, SEQ], F32R, 128 + 4 * g) for g in range(2)]
        KL2 = [Z(f"KL2_{g}", [P, SEQ], F32R, 136 + 4 * g) for g in range(2)]
        KCH2 = [Z(f"KCH2_{g}", [P, CTX], F32R, 76.25 + g) for g in range(2)]
        KCL2 = [Z(f"KCL2_{g}", [P, CTX], F32R, 109 + g) for g in range(2)]

        def opre_pe(pe):
            for t in range(NT):
                m = pe.transpose(M[1][:, t * P:(t + 1) * P], OV[:, t * P:(t + 1) * P], IDENT[:])
            m.then_inc(S("ov_tr"), 1)
            pe.wait_ge(moved, info("opre")["dma_end"])
            for i in range(5):
                if i == 1:
                    pe.wait_ge(S("ov_out"), 1)
                swap_pe(pe, "or", i, OQ[:, i - 1, :] if i else OK[:], SWAPW[:])
            for s in range(2):
                pe.wait_ge(S(f"oj_moved{s}"), 32 * 4)
            pe.wait_ge(S("oj_last"), 8 * 16)

        def split_parts(j):
            if j == 0:
                return OK[:], KH2[0], KL2[0][:]
            if j == 1:
                return KC[:], KCH2[0], KCL2[0][:]
            return OQ[:, j - 2, :], QA[j - 2], OQ[:, j - 2, :].bitcast(F32R)

        def opre_dve(dve):
            for j in range(4):
                dve.wait_ge(S("oc_hi"), j + 1)
                dve.tensor_tensor(HL[:, j, :], CB[:, j, :], HH[:, j, :].bitcast(F32), ALU.subtract)\
                   .then_inc(S("oc_lo"), 1)
            dve.wait_ge(S("oc_lo"), 4)

            def low(j):
                src, hi, lo = split_parts(j)
                dve.wait_ge(S("oj_hi"), j + 1)
                dve.tensor_tensor(lo, src, hi[:].bitcast(F32), ALU.subtract).then_inc(S("oj_lo"), 1)
            rope_dve(dve, "or", 0, OK[:], WC[:], WS[:], OTMP[:])
            for j in range(4):
                rope_dve(dve, "or", j + 1, OQ[:, j, :], WC[:], WS[:], OTMP[:])
                for q in ((0, 1) if j == 0 else (j + 1,)):
                    low(q)
            low(5)

        def opre_act(act):
            act.wait_ge(S("ov_tr"), 1)
            act.activation(WVT[:].rearrange("p t n -> p (t n)"), M[1][:], ACT.Copy).then_inc(S("ov_out"), 1)

            for j in range(4):
                act.activation(HH[:, j, :], CB[:, j, :], ACT.Copy).then_inc(S("oc_hi"), 1)
            act.wait_ge(S("oc_lo"), 4)
            for j in range(6):
                src, hi, _ = split_parts(j)
                act.wait_ge(S("or_rot"), 2 if j < 2 else 2 * j)
                act.activation(hi[:], src, ACT.Copy).then_inc(S("oj_hi"), 1)

        def opre_sp(sp):
            low, high = slice(0, 64), slice(64, P)

            def move(dst, dst_rows, src, src_rows, signal):
                sp.dma_start(dst[dst_rows, :].bitcast(F32), src[src_rows, :].bitcast(F32)).then_inc(signal, 16)

            def out_of(j):
                sp.wait_ge(S("oj_lo"), j + 1)
                moved_j = S(f"oj_moved{j % 2}")
                if j < 2:
                    for two in ((KH2, KL2), (KCH2, KCL2))[j]:
                        move(two[1], high, two[0], high, moved_j)
                        move(two[1], low, two[0], high, moved_j)
                else:
                    move(QA[j + 2], high, QA[j - 2], high, moved_j)
                    move(QA[j + 2], low, OQ[:, j - 2, :], high, moved_j)

            def into(j):
                n = 64 + 32 * (j // 2) if j >= 2 else 64
                sp.wait_ge(S(f"oj_moved{j % 2}"), n)
                if j < 2:
                    for two in ((KH2, KL2), (KCH2, KCL2))[j]:
                        move(two[0], high, two[0], low, S("oj_last"))
                else:
                    move(QA[j - 2], high, OQ[:, j - 2, :], low, S("oj_last"))
            out_of(0)
            for j in range(1, 6):
                out_of(j)
                into(j - 1)
            into(5)

        stage("opre", dict(act=opre_act, pe=opre_pe, dve=opre_dve, sp_gated=opre_sp),
              dmas=[(WC[:], A["cos_win"]), (WS[:], A["sin_win"]), (SWAPW[:], A["swap_win"])])

        WATT = Z("WATT", [P, NT, 512], F32, 32.25)
        WP = [Z(f"WP{s}", [P, 640], F32, 96 + 2.5 * s) for s in range(2)]
        WPT = [Z(f"WPT{s}", [P, 640], F32, 101 + 2.5 * s) for s in range(2)]
        WNEG, WSUM, WSINK, WRDEN = [Z(n, [P, 2, N_Q], F32, 106 + 0.0625 * i)
                                    for i, n in enumerate(("WNEG", "WSUM", "WSINK", "WRDEN"))]
        WMAX = Z("WMAX", [P, 2, N_Q], F32, 106.25)
        NSINK = Z("NSINK", [P, N_Q], F32, 106.3125)
        SCALE_W = HEAD ** -0.5
        steps = [(n, h) for n in range(NT) for h in range(N_Q)]

        def span(n):
            return list(range(max(n - 1, 0), min(n + 2, NT)))

        def wa_pe(pe):
            def scores(i):
                n, h = steps[i]
                g = h // 4
                q = QA[h][:, n * P:(n + 1) * P]
                blocks = span(n)
                a = 512 - P * len(blocks)
                keys = slice(blocks[0] * P, (blocks[-1] + 1) * P)
                ps = G[i % 2]
                if i >= 2:
                    pe.wait_ge(S("wa_exp"), i - 1)
                pe.matmul(ps[:, a:512], q, KH2[g][:, keys], start=True, stop=False)
                pe.matmul(ps[:, a:512], q, KL2[g][:, keys], start=False, stop=False)
                pe.matmul(ps[:, 512:768], q, KCH2[g][:], start=True, stop=False)
                pe.matmul(ps[:, 512:768], q, KCL2[g][:], start=False, stop=True)
                if n > 0:
                    m = pe.matmul(ps[:, a:a + P], identb, before, start=False, stop=(n == NT - 1))
                if n < NT - 1:
                    m = pe.matmul(ps[:, 512 - P:512], identb, causal, start=False, stop=True)
                m.then_inc(S("wa_sc"), 1)

            def turn(i):
                n, h = steps[i]
                nb = len(span(n)) + 2
                pe.wait_ge(S("wa_exp"), i + 1)
                if i:
                    pe.wait_ge(S("wa_pt"), i)
                for b in range(nb):
                    m = pe.transpose(M[0][:, b * P:(b + 1) * P], WP[i % 2][:, b * P:(b + 1) * P], IDENT[:])
                m.then_inc(S("wa_tr"), 1)

            def values(i):
                n, h = steps[i]
                g = h // 4
                blocks = span(n)
                pe.wait_ge(S("wa_pt"), i + 1)
                if h == 0 and n >= 2:
                    pe.wait_ge(S("wa_att"), n - 1)
                c0 = 512 * (n % 2) + h * HEAD
                for b in range(len(blocks) + 2):
                    v = WVT[:, blocks[b], 64 * g:64 * g + 64] if b < len(blocks) else \
                        VC[:, b - len(blocks), 64 * g:64 * g + 64]
                    m = pe.matmul(M[1][:, c0:c0 + HEAD], WPT[i % 2][:, b * P:(b + 1) * P], v,
                                  start=(b == 0), stop=(b == len(blocks) + 1))
                m.then_inc(S("wa_pv"), 1)
            scores(0)
            for i in range(len(steps)):
                if i + 1 < len(steps):
                    scores(i + 1)
                if i:
                    values(i - 1)
                turn(i)
            values(len(steps) - 1)

        def wa_dve(dve):
            dve.tensor_scalar(NSINK[:], vec("sink", 0, N_Q), -1.0, None, ALU.mult).then_inc(S("wa_nsink"), 1)
            dve.wait_ge(S("wa_nsink"), 1)

            def smax(i):
                n, h = steps[i]
                a = 512 - P * len(span(n))
                x, neg = WMAX[:, n % 2, h:h + 1], WNEG[:, n % 2, h:h + 1]
                dve.wait_ge(S("wa_sc"), i + 1)
                dve.tensor_reduce(x, G[i % 2][:, a:768], AX.X, ALU.max).then_inc(S("wa_mx"), 1)
                dve.wait_ge(S("wa_mx"), i + 1)
                dve.tensor_scalar(neg, x, -SCALE_W, NSINK[:, h:h + 1], ALU.mult, ALU.min).then_inc(S("wa_neg"), 1)
                if h == N_Q - 1:
                    dve.wait_ge(S("wa_neg"), i + 1)
                    dve.tensor_tensor(WSINK[:, n % 2, :], WNEG[:, n % 2, :], NSINK[:], ALU.subtract)\
                       .then_inc(S("wa_sink"), 1)

            def tail(i):
                n, h = steps[i]
                w = (len(span(n)) + 2) * P
                dve.wait_ge(S("wa_tr"), i + 1)
                if i >= 2:
                    dve.wait_ge(S("wa_pv"), i - 1)
                dve.tensor_copy(WPT[i % 2][:, 0:w], M[0][:, 0:w]).then_inc(S("wa_pt"), 1)

            def put(n):
                dve.wait_ge(S("wa_es"), n + 1)
                dve.tensor_tensor(WRDEN[:, n % 2, :], WSUM[:, n % 2, :], WSINK[:, n % 2, :], ALU.add)\
                   .then_inc(S("wa_den"), 1)
                dve.wait_ge(S("wa_den"), 2 * n + 1)
                dve.reciprocal(WRDEN[:, n % 2, :], WRDEN[:, n % 2, :]).then_inc(S("wa_den"), 1)
                dve.wait_ge(S("wa_den"), 2 * n + 2)
                dve.wait_ge(S("wa_pv"), N_Q * (n + 1))
                dve.tensor_tensor(WATT[:, n, :].rearrange("p (h d) -> p h d", d=HEAD),
                                  M[1][:, 512 * (n % 2):512 * (n % 2) + 512].rearrange("p (h d) -> p h d", d=HEAD),
                                  WRDEN[:, n % 2, :].unsqueeze(2).broadcast_to([P, N_Q, HEAD]), ALU.mult)\
                   .then_inc(S("wa_att"), 1)
            smax(0)
            for i in range(len(steps)):
                n, h = steps[i]
                if i + 1 < len(steps):
                    smax(i + 1)
                tail(i)
                if n and h == 1:
                    put(n - 1)
            put(NT - 1)

        def wa_act(act):
            for i in range(len(steps)):
                n, h = steps[i]
                w = (len(span(n)) + 2) * P
                act.wait_ge(S("wa_neg"), i + 1)
                if i >= 2:
                    act.wait_ge(S("wa_tr"), i - 1)
                if h == 0 and n >= 2:
                    act.wait_ge(S("wa_att"), n - 1)
                act.activation(WP[i % 2][:, 0:w], G[i % 2][:, 768 - w:768], ACT.Exp, bias=WNEG[:, n % 2, h:h + 1],
                               scale=SCALE_W, accum_out=WSUM[:, n % 2, h:h + 1]).then_inc(S("wa_exp"), 1)
                if h == N_Q - 1:
                    act.wait_ge(S("wa_sink"), n + 1)
                    act.activation(WSINK[:, n % 2, :], WSINK[:, n % 2, :], ACT.Exp).then_inc(S("wa_es"), 1)

        GF = Z("GF", [P, D], F32, 48.25)
        stage("wa", dict(act=wa_act, pe=wa_pe, dve=wa_dve), dmas=[(GF[:], A["final_gain"].broadcast_to([P, D]))])
        turn_stage("oturn", WATT, 4, gate=AG, tmp=[Z(f"OT{s}", [P, SEQ], F32, 16.25 + 4 * s) for s in range(2)])
        out_stage("oout", A["o_w_out"], SEQ, X, lambda f: MODO[:, 16 + f, 0:1],
                  ("oturn_lo", range(4, KT)), squares=True)

        N_OUT = 4
        OUT = [Z(f"OUT{s}", [P, D], F32, 16 + 4 * s) for s in range(N_OUT)]

        def st_pe(pe):
            for t in range(NT):
                m = pe.matmul(G[0][:, t:t + 1], NR[:, t * P:(t + 1) * P], ONES[:, 0:1], start=True, stop=True)
            m.then_inc(S("st_ms"), 1)
            for t in range(NT):
                if t >= 2:
                    pe.wait_ge(S("st_o"), t - 1)
                for f in range(KT):
                    m = pe.transpose(M[t % 2][:, f * P:(f + 1) * P], X[:, f, t * P:(t + 1) * P], IDENT[:])
                m.then_inc(S("st_tr"), 1)

        def st_dve(dve):
            dve.wait_ge(S("st_sd"), 1)
            dve.reciprocal(RS[:, 0:NT], SD[:, 0:NT]).then_inc(S("st_r"), 1)
            dve.wait_ge(S("st_r"), 1)
            dve.wait_ge(moved, info("wa")["dma_end"])
            for t in range(NT):
                dve.wait_ge(S("st_tr"), t + 1)
                if t >= N_OUT:
                    dve.wait_ge(S(f"stored{t % N_OUT}"), 16)
                dve.scalar_tensor_tensor(out=OUT[t % N_OUT][:], in0=M[t % 2][:], scalar=RS[:, t:t + 1], in1=GF[:],
                                         op0=ALU.mult, op1=ALU.mult).then_inc(S("st_o"), 1)

        def st_act(act):
            act.wait_ge(S("st_ms"), 1)
            act.activation(SD[:, 0:NT], G[0][:, 0:NT], ACT.Sqrt, bias=vec("eps2"), scale=1.0 / D)\
               .then_inc(S("st_sd"), 1)
            for t in range(NT):
                act.wait_ge(S("st_o"), t + 1)
                act.dma_start(out[t * P:(t + 1) * P, :], OUT[t % N_OUT][:]).then_inc(S(f"stored{t % N_OUT}"), 16)
            for s in range(N_OUT):
                act.wait_ge(S(f"stored{s}"), 16 * (NT // N_OUT))

        stage("store", dict(act=st_act, pe=st_pe, dve=st_dve))

        block = ctx.enter_context(nc.Block())

        def gate(eng, n):
            for k in left:
                eng.wait_ge(left[k], n)

        def walk(eng, key):
            for n, st in enumerate(stages):
                current[0] = n
                if n:
                    gate(eng, n)
                    if key == "dve":
                        first = banks_of_signals[(n - 1) % 2][0].num
                        eng.sem_clear(range(first, first + BANK))
                if key in st["progs"]:
                    st["progs"][key](eng)
                if key == "pe" and n + 1 < len(stages) and "lead" in stages[n + 1]["progs"]:
                    stages[n + 1]["progs"]["lead"](eng)
                eng.drain().then_inc(left[key], 1)

        @block.sync
        def _(sp):
            for n, st in enumerate(stages):
                current[0] = n
                if "sp_gated" in st["progs"]:
                    gate(sp, n)
                    st["progs"]["sp_gated"](sp)
                if "sp_free" in st["progs"]:
                    st["progs"]["sp_free"](sp, st["r0"])
                    continue
                r = st["r0"]
                for n_pairs, src in st["raw"]:
                    if n_pairs == 1:
                        for s in range(2):
                            load_unit(sp, r // 2, s, src(s, 0), RAW[s][:])
                    else:
                        def pair(i, r=r, src=src):
                            for s in range(2):
                                load_unit(sp, i + r // 2, s, src(s, i), RAW[s][:])
                        turns(sp, n_pairs, pair)
                    r += 2 * n_pairs

        @block.gpsimd
        def _(pool):
            for n, st in enumerate(stages):
                current[0] = n
                if st["dmas"]:
                    if n:
                        gate(pool, n)
                    for dst, src in st["dmas"]:
                        pool.dma_start(dst, src).then_inc(moved, 16)
                if "pool" in st["progs"]:
                    st["progs"]["pool"](pool)
                elif st["units"]:
                    split_pairs(pool, st["r0"], st["u0"], st["units"] // 2, st["per_unit"])

        @block.scalar
        def _(act):
            walk(act, "act")

        @block.vector
        def _(dve):
            walk(dve, "dve")

        @block.tensor
        def _(pe):
            walk(pe, "pe")


def kernel(**inputs):
    import concourse.bacc as _bacc
    from concourse.bass_utils import run_bass_kernel_spmd as _run

    def tiles(a):
        a = np.asarray(a)
        return np.ascontiguousarray(a.reshape(-1, P).T)

    g = {k: np.asarray(v) for k, v in inputs.items()}
    const = shape_constants()
    two = np.stack([tiles(g["c_2"]), tiles(g["c_ctx_2"])], 2).reshape(P, 16)
    taps = lambda w: np.ascontiguousarray(w[0].reshape(w.shape[1], 4, P).transpose(2, 1, 0).reshape(P, -1))
    parts = {
        "c": tiles(g["c"]), "c2": two, "ln_in_g": tiles(g["ln_in_g"]), "ln_in_b": tiles(g["ln_in_b"]),
        "ln1_g": tiles(g["ln1_g"]), "ln1_b": tiles(g["ln1_b"]), "ln2_g": tiles(g["ln2_g"]),
        "ln2_b": tiles(g["ln2_b"]), "e_norm": tiles(g["e_norm_2"]), "o_norm": tiles(g["o_norm_2"]),
        "b_ada": tiles(g["b_ada"]), "e_b": tiles(g["e_b_mod_2"]),
        "o_b": tiles(g["o_b_mod_2"]), "q_norm": tiles(g["mla_q_norm"]), "kv_norm": tiles(g["mla_kv_norm"]),
        "gn_g": tiles(g["ret_gn_g"]), "gn_b": tiles(g["ret_gn_b"]), "conv_w": taps(g["e_a_conv_w_2"]),
        "conv_b": tiles(g["e_a_conv_b_2"]), "a_ln_g": tiles(g["e_a_ln_g_2"]), "a_ln_b": tiles(g["e_a_ln_b_2"]),
        "pw_b": tiles(g["e_a_pw_b_2"]), "c_conv": taps(g["o_c_conv_w_2"]),
        "sink": np.broadcast_to(g["o_sink_2"], (P, 8)), "zeta": const["cols"][:, 0:4],
        "inv_ret": const["cols"][:, 4:5], "inv_mla": const["cols"][:, 5:6], "g_chunk": const["cols"][:, 6:8],
        "eps1": const["cols"][:, 8:9], "eps2": const["cols"][:, 9:10],
    }
    arrays = {
        "vecs": np.concatenate([parts[n] for n, _ in VEC_PARTS], 1),
        "masks": mask_constants(),
        "x": g["x"][0], "ctx": g["ctx_2"][0], "positions": g["positions"],
        "final_gain": g["final_norm_2"].reshape(1, D),
        "w_ada": g["w_ada"][0], "w_in": g["w_in"][0], "w_uq": g["w_uq"][0], "w_ukv": g["w_ukv"][0],
        "w_out": g["w_out"][0], "w_ff1": g["w_ff1"][0], "w_ff2": g["w_ff2"][0],
        "e_w_mod": g["e_w_mod_2"][0], "e_w_in": g["e_w_in_2"][0], "e_a_pw_w": g["e_a_pw_w_2"][0],
        "e_b_fw": g["e_b_fw_2"][0], "e_w_out": g["e_w_out_2"][0], "o_w_mod": g["o_w_mod_2"][0],
        "o_w_in": g["o_w_in_2"][0], "o_w_out": g["o_w_out_2"][0],
    }
    arrays.update({k: v for k, v in const.items() if k != "cols"})
    nc = _bacc.Bacc("TRN2", target_bir_lowering=False, num_devices=1)
    named, args = {}, {}
    for name, a in arrays.items():
        a = np.ascontiguousarray(a)
        named[f"in_{name}"] = a
        args[name] = nc.dram_tensor(f"in_{name}", a.shape, mybir.dt.from_np(a.dtype), kind="ExternalInput").ap()
    out = nc.dram_tensor("out_0", (SEQ, D), F32, kind="ExternalOutput").ap()
    build_program(nc, args, out)
    r = _run(nc, [named], core_ids=[0])
    return r.results[0]["out_0"].reshape(1, SEQ, D)
```
